# Optimizing a Trainium2 kernel written in Bass

```python
import math
import jax
import jax.numpy as jnp
from jax import lax
import numpy as np

D_MODEL = 2048
BATCH = 1
SEQ = 256
DEPTH = 2

GLA_H = 4
GLA_DK = 64
GLA_DV = 128
GLA_GATE_RANK = 16
GLA_GATE_TAU = 16.0
GLA_CHUNK = 16
SSD_DINNER = 512
SSD_HD = 64
SSD_H = SSD_DINNER // SSD_HD
SSD_G = 2
SSD_N = 128
SSD_CONV = 4
SSD_CONV_DIM = SSD_DINNER + 2 * SSD_G * SSD_N
SSD_CHUNK = 64
MLA_H = 4
MLA_NOPE = 128
MLA_ROPE = 64
MLA_QK = MLA_NOPE + MLA_ROPE
MLA_V = 128
MLA_Q_LORA = 384
MLA_KV_LORA = 128
DIL_H = 4
DIL_HD = 128
DIL_CONFIGS = ((128, 1), (512, 4), (2048, 16))
DIL_MAX_W = 2048

Q_BLOCK = 128
ROPE_THETA = 10000.0
EPS = 1e-6
D_MIX = GLA_H * GLA_DV + SSD_DINNER + MLA_H * MLA_V + DIL_H * DIL_HD
IN_WIDTHS = (GLA_H * GLA_DV, SSD_DINNER, MLA_H * MLA_V, DIL_H * DIL_HD,
             GLA_H * GLA_DK, GLA_H * GLA_DK, GLA_H * GLA_DV, GLA_GATE_RANK,
             SSD_CONV_DIM, SSD_H,
             MLA_Q_LORA, MLA_KV_LORA, MLA_ROPE,
             DIL_H * DIL_HD, DIL_H * DIL_HD, DIL_H * DIL_HD)
N_IN = sum(IN_WIDTHS)

kernel_name = 'hybrid_gla_ssd_mla_dilated_parallel_heads'

def _split(u, widths):
    out, start = [], 0
    for w in widths:
        out.append(u[..., start:start + w])
        start += w
    return out

def _rmsnorm(x, g):
    xf = x.astype(jnp.float32)
    y = xf * lax.rsqrt(jnp.mean(xf * xf, axis=-1, keepdims=True) + EPS)
    return (y * g.astype(jnp.float32)).astype(x.dtype)

def _rope(x, pos):
    d = x.shape[-1]
    half = d // 2
    inv_freq = jnp.exp(-math.log(ROPE_THETA) * jnp.arange(half, dtype=jnp.float32) * (2.0 / d))
    ang = pos.astype(jnp.float32)[:, :, None] * inv_freq
    cos = jnp.cos(ang)[:, :, None, :]
    sin = jnp.sin(ang)[:, :, None, :]
    xf = x.astype(jnp.float32)
    x1, x2 = xf[..., :half], xf[..., half:]
    return jnp.concatenate([x1 * cos - x2 * sin, x2 * cos + x1 * sin], axis=-1).astype(x.dtype)

def _gla(q, k, v, log_a, norm_g):
    Bsz, S, H, DK = q.shape
    DV = v.shape[-1]
    C = GLA_CHUNK
    N = S // C

    def chunks(t):
        return t.astype(jnp.float32).reshape(Bsz, N, C, H, t.shape[-1]).transpose(0, 3, 1, 2, 4)

    qc = chunks(q) * (DK ** -0.5)
    kc = chunks(k)
    vc = chunks(v)
    bc = jnp.cumsum(chunks(log_a), axis=3)
    causal = jnp.tril(jnp.ones((C, C), bool))[:, :, None]
    diff = bc[:, :, :, :, None, :] - bc[:, :, :, None, :, :]
    decay = jnp.exp(jnp.where(causal, diff, -jnp.inf))
    attn = jnp.einsum('bhnid,bhnjd,bhnijd->bhnij', qc, kc, decay)
    o_intra = jnp.einsum('bhnij,bhnjv->bhniv', attn, vc)
    b_last = bc[:, :, :, -1, :]
    upd = jnp.einsum('bhncd,bhncv->bhndv', kc * jnp.exp(b_last[:, :, :, None, :] - bc), vc)

    def step(state, inp):
        dec, u = inp
        return state * dec[..., None] + u, state

    init = jnp.zeros((Bsz, H, DK, DV), jnp.float32)
    _, s_before = lax.scan(step, init, (jnp.moveaxis(jnp.exp(b_last), 2, 0), jnp.moveaxis(upd, 2, 0)))
    s_before = jnp.moveaxis(s_before, 0, 2)
    o_inter = jnp.einsum('bhncd,bhndv->bhncv', qc * jnp.exp(bc), s_before)
    o = (o_intra + o_inter).transpose(0, 2, 3, 1, 4).reshape(Bsz, S, H, DV)
    return _rmsnorm(o, norm_g).reshape(Bsz, S, H * DV)

def _segsum(x):
    T = x.shape[-1]
    xe = jnp.broadcast_to(x[..., :, None], x.shape + (T,))
    xe = jnp.where(jnp.tril(jnp.ones((T, T), bool), -1), xe, 0.0)
    ss = jnp.cumsum(xe, axis=-2)
    return jnp.where(jnp.tril(jnp.ones((T, T), bool)), ss, -jnp.inf)

def _ssd_scan(X, A, Bm, Cm):
    b, s, h, p = X.shape
    n = Bm.shape[-1]
    L = SSD_CHUNK
    c = s // L
    Xc = X.reshape(b, c, L, h, p)
    Bc = Bm.reshape(b, c, L, h, n)
    Cc = Cm.reshape(b, c, L, h, n)
    Ac = A.reshape(b, c, L, h).transpose(0, 3, 1, 2)
    A_cs = jnp.cumsum(Ac, axis=-1)
    Lm = jnp.exp(_segsum(Ac))
    y_diag = jnp.einsum('bclhn,bcshn,bhcls,bcshp->bclhp', Cc, Bc, Lm, Xc)
    decay_states = jnp.exp(A_cs[..., -1:] - A_cs)
    states = jnp.einsum('bclhn,bhcl,bclhp->bchpn', Bc, decay_states, Xc)

    def step(st, inp):
        dec, s_new = inp
        return st * dec[:, :, None, None] + s_new, st

    init = jnp.zeros((b, h, p, n), jnp.float32)
    _, prev = lax.scan(step, init, (jnp.moveaxis(jnp.exp(A_cs[..., -1]), 2, 0), jnp.moveaxis(states, 1, 0)))
    prev = jnp.moveaxis(prev, 0, 1)
    y_off = jnp.einsum('bclhn,bchpn,bhcl->bclhp', Cc, prev, jnp.exp(A_cs))
    return (y_diag + y_off).reshape(b, s, h, p)

def _ssd_mixer(xbc, dt_raw, z, conv_w, conv_b, dt_bias, A_log, D, norm_g):
    Bsz, S, _ = xbc.shape
    xpad = jnp.pad(xbc.astype(jnp.float32), ((0, 0), (SSD_CONV - 1, 0), (0, 0)))
    conv = jnp.broadcast_to(conv_b.astype(jnp.float32), (Bsz, S, SSD_CONV_DIM))
    for j in range(SSD_CONV):
        conv = conv + xpad[:, j:j + S, :] * conv_w[j].astype(jnp.float32)
    xbc = jax.nn.silu(conv)
    xs, Bm, Cm = _split(xbc, (SSD_DINNER, SSD_G * SSD_N, SSD_G * SSD_N))
    xs = xs.reshape(Bsz, S, SSD_H, SSD_HD)
    Bm = jnp.repeat(Bm.reshape(Bsz, S, SSD_G, SSD_N), SSD_H // SSD_G, axis=2)
    Cm = jnp.repeat(Cm.reshape(Bsz, S, SSD_G, SSD_N), SSD_H // SSD_G, axis=2)
    dt = jax.nn.softplus(dt_raw.astype(jnp.float32) + dt_bias.astype(jnp.float32))
    A = -jnp.exp(A_log.astype(jnp.float32))
    y = _ssd_scan(xs * dt[..., None], dt * A, Bm, Cm) + xs * D.astype(jnp.float32)[:, None]
    y = y.reshape(Bsz, S, SSD_DINNER) * jax.nn.silu(z.astype(jnp.float32))
    y = _rmsnorm(y.reshape(Bsz, S, SSD_G, SSD_DINNER // SSD_G), norm_g.reshape(SSD_G, SSD_DINNER // SSD_G))
    return y.reshape(Bsz, S, SSD_DINNER)

def _causal_attention(q, k, v):
    Bsz, S, H, dq = q.shape
    nb = S // Q_BLOCK
    scale = dq ** -0.5
    qb = q.reshape(Bsz, nb, Q_BLOCK, H, dq).transpose(1, 0, 2, 3, 4)
    kpos = jnp.arange(S)

    def one(args):
        qi, i = args
        s = jnp.einsum('bqhd,bkhd->bhqk', qi, k, preferred_element_type=jnp.float32) * scale
        qpos = i * Q_BLOCK + jnp.arange(Q_BLOCK)
        s = jnp.where(kpos[None, :] <= qpos[:, None], s, -jnp.inf)
        p = jax.nn.softmax(s, axis=-1)
        return jnp.einsum('bhqk,bkhd->bqhd', p.astype(v.dtype), v)

    o = lax.map(one, (qb, jnp.arange(nb)))
    return o.transpose(1, 0, 2, 3, 4).reshape(Bsz, S, H, v.shape[-1])

def _mla(c_q, c_kv, k_rope, positions, q_norm_g, kv_norm_g, w_uq, w_ukv, q_head_g, k_head_g):
    Bsz, S, _ = c_q.shape
    q = (_rmsnorm(c_q, q_norm_g) @ w_uq).reshape(Bsz, S, MLA_H, MLA_QK)
    kv = (_rmsnorm(c_kv, kv_norm_g) @ w_ukv).reshape(Bsz, S, MLA_H, MLA_NOPE + MLA_V)
    k_nope, v = kv[..., :MLA_NOPE], kv[..., MLA_NOPE:]
    k_r = jnp.broadcast_to(k_rope[:, :, None, :], (Bsz, S, MLA_H, MLA_ROPE))
    k = _rmsnorm(jnp.concatenate([k_nope, k_r], axis=-1), k_head_g)
    q = _rmsnorm(q, q_head_g)
    q = jnp.concatenate([q[..., :MLA_NOPE], _rope(q[..., MLA_NOPE:], positions)], axis=-1)
    k = jnp.concatenate([k[..., :MLA_NOPE], _rope(k[..., MLA_NOPE:], positions)], axis=-1)
    return _causal_attention(q, k, v).reshape(Bsz, S, MLA_H * MLA_V)

def _dilated_attention(q, k, v):
    Bsz, S, H, Dh = q.shape
    nb = S // Q_BLOCK
    scale = Dh ** -0.5
    pad = ((0, 0), (DIL_MAX_W, 0), (0, 0), (0, 0))
    kp = jnp.pad(k, pad)
    vp = jnp.pad(v, pad)
    qb = q.reshape(Bsz, nb, Q_BLOCK, H, Dh).transpose(1, 0, 2, 3, 4)
    rows = np.arange(Q_BLOCK)

    def one(args):
        qi, i = args
        t0 = i * Q_BLOCK
        scores, vals, sizes = [], [], []
        for (w, d) in DIL_CONFIGS:
            taps = np.arange(w // d + 1)
            idx = rows[:, None] + w - taps[None, :] * d
            start = t0 + DIL_MAX_W - w
            ks = lax.dynamic_slice_in_dim(kp, start, Q_BLOCK + w, axis=1)
            vs = lax.dynamic_slice_in_dim(vp, start, Q_BLOCK + w, axis=1)
            kg = jnp.take(ks, idx, axis=1)
            s = jnp.einsum('bqhd,bqjhd->bhqj', qi, kg, preferred_element_type=jnp.float32) * scale
            valid = (t0 + rows[:, None] - taps[None, :] * d) >= 0
            scores.append(jnp.where(valid, s, -jnp.inf))
            vals.append(jnp.take(vs, idx, axis=1))
            sizes.append(taps.shape[0])
        p = jax.nn.softmax(jnp.concatenate(scores, axis=-1), axis=-1)
        out = None
        for p_c, v_c in zip(_split(p, sizes), vals):
            o_c = jnp.einsum('bhqj,bqjhd->bqhd', p_c.astype(v_c.dtype), v_c)
            out = o_c if out is None else out + o_c
        return out

    o = lax.map(one, (qb, jnp.arange(nb)))
    return o.transpose(1, 0, 2, 3, 4).reshape(Bsz, S, H * Dh)

def setup_inputs(seed: int = 0) -> dict:
    key = jax.random.key(seed)
    ks = jax.random.split(key, 24)

    def nrm(k, shape, scale):
        return jax.random.normal(k, shape, jnp.float32) * scale

    def gain(k, n):
        return 1.0 + nrm(k, (DEPTH, n), 0.02)

    x = nrm(ks[0], (BATCH, SEQ, D_MODEL), 1.0)
    offs = jax.random.randint(ks[1], (BATCH, 1), 0, SEQ, dtype=jnp.int32)
    positions = offs + jnp.arange(SEQ, dtype=jnp.int32)[None, :]
    dt0 = jnp.exp(jax.random.uniform(ks[2], (DEPTH, SSD_H), jnp.float32, math.log(1e-3), math.log(1e-1)))
    return {
        'x': x,
        'positions': positions,
        'ln_g': gain(ks[3], D_MODEL),
        'w_in': nrm(ks[4], (DEPTH, D_MODEL, N_IN), D_MODEL ** -0.5),
        'w_out': nrm(ks[5], (DEPTH, D_MIX, D_MODEL), D_MIX ** -0.5),
        'gla_gate_w2': nrm(ks[6], (DEPTH, GLA_GATE_RANK, GLA_H * GLA_DK), GLA_GATE_RANK ** -0.5),
        'gla_gate_b': nrm(ks[7], (DEPTH, GLA_H * GLA_DK), 0.1),
        'gla_norm_g': gain(ks[8], GLA_DV),
        'ssd_conv_w': nrm(ks[9], (DEPTH, SSD_CONV, SSD_CONV_DIM), SSD_CONV ** -0.5),
        'ssd_conv_b': nrm(ks[10], (DEPTH, SSD_CONV_DIM), 0.02),
        'ssd_dt_bias': dt0 + jnp.log(-jnp.expm1(-dt0)),
        'ssd_A_log': jnp.log(jax.random.uniform(ks[11], (DEPTH, SSD_H), jnp.float32, 1.0, 16.0)),
        'ssd_D': 1.0 + nrm(ks[12], (DEPTH, SSD_H), 0.1),
        'ssd_norm_g': gain(ks[13], SSD_DINNER),
        'mla_q_norm_g': gain(ks[14], MLA_Q_LORA),
        'mla_kv_norm_g': gain(ks[15], MLA_KV_LORA),
        'mla_w_uq': nrm(ks[16], (DEPTH, MLA_Q_LORA, MLA_H * MLA_QK), MLA_Q_LORA ** -0.5),
        'mla_w_ukv': nrm(ks[17], (DEPTH, MLA_KV_LORA, MLA_H * (MLA_NOPE + MLA_V)), MLA_KV_LORA ** -0.5),
        'mla_q_head_g': gain(ks[18], MLA_QK),
        'mla_k_head_g': gain(ks[19], MLA_QK),
        'dil_q_g': gain(ks[20], DIL_HD),
        'dil_k_g': gain(ks[21], DIL_HD),
    }

def reference(x, positions, ln_g, w_in, w_out, gla_gate_w2, gla_gate_b, gla_norm_g,
              ssd_conv_w, ssd_conv_b, ssd_dt_bias, ssd_A_log, ssd_D, ssd_norm_g,
              mla_q_norm_g, mla_kv_norm_g, mla_w_uq, mla_w_ukv, mla_q_head_g, mla_k_head_g,
              dil_q_g, dil_k_g):
    Bsz, S, _ = x.shape
    for l in range(DEPTH):
        h = _rmsnorm(x, ln_g[l])
        u = h @ w_in[l]
        (g_a, g_b, g_c, g_d, a_q, a_k, a_v, a_lr, b_xbc, b_dt,
         c_q, c_kv, c_kr, d_q, d_k, d_v) = _split(u, IN_WIDTHS)
        log_a = jax.nn.log_sigmoid((a_lr @ gla_gate_w2[l] + gla_gate_b[l]).astype(jnp.float32)) / GLA_GATE_TAU
        y_a = _gla(a_q.reshape(Bsz, S, GLA_H, GLA_DK), a_k.reshape(Bsz, S, GLA_H, GLA_DK),
                   a_v.reshape(Bsz, S, GLA_H, GLA_DV), log_a.reshape(Bsz, S, GLA_H, GLA_DK),
                   gla_norm_g[l]) * jax.nn.silu(g_a)
        y_b = _ssd_mixer(b_xbc, b_dt, g_b, ssd_conv_w[l], ssd_conv_b[l], ssd_dt_bias[l],
                         ssd_A_log[l], ssd_D[l], ssd_norm_g[l])
        y_c = _mla(c_q, c_kv, c_kr, positions, mla_q_norm_g[l], mla_kv_norm_g[l], mla_w_uq[l],
                   mla_w_ukv[l], mla_q_head_g[l], mla_k_head_g[l]) * jax.nn.silu(g_c)
        dq = _rope(_rmsnorm(d_q.reshape(Bsz, S, DIL_H, DIL_HD), dil_q_g[l]), positions)
        dk = _rope(_rmsnorm(d_k.reshape(Bsz, S, DIL_H, DIL_HD), dil_k_g[l]), positions)
        y_d = _dilated_attention(dq, dk, d_v.reshape(Bsz, S, DIL_H, DIL_HD)) * jax.nn.silu(g_d)
        y = jnp.concatenate([y_a, y_b, y_c, y_d], axis=-1).astype(x.dtype)
        x = x + y @ w_out[l]
    return x


_drawn_inputs = setup_inputs


def setup_inputs(seed=0):
    import zlib

    import numpy as np

    out = dict(_drawn_inputs(seed))
    spreads = {}
    factors = {'gla_gate_b': 3.525,
     'gla_norm_g': 7.82,
     'ssd_conv_b': 3.194,
     'ssd_norm_g': 4.186,
     'mla_q_norm_g': 8.0,
     'mla_kv_norm_g': 8.0,
     'mla_q_head_g': 8.0,
     'mla_k_head_g': 8.0,
     'dil_q_g': 8.0,
     'dil_k_g': 8.0}
    for name, (base, spread) in spreads.items():
        noise = np.random.default_rng([zlib.crc32(name.encode()), seed]).standard_normal(out[name].shape)
        drawn = base * np.exp(spread * noise) if base else spread * noise
        out[name] = jnp.asarray(drawn.astype(out[name].dtype))
    for name, factor in factors.items():
        out[name] = (out[name] * factor).astype(out[name].dtype)
    return out
```

```python
from contextlib import ExitStack

import numpy as np

import concourse.bass as bass
from concourse import mybir

ALU = mybir.AluOpType
ACT = mybir.ActivationFunctionType
AX = mybir.AxisListType
F32 = mybir.dt.float32
F32R = mybir.dt.float32r
U8 = mybir.dt.uint8
I32 = mybir.dt.int32

P = 128
S, D, DEPTH = 256, 2048, 2
T = S // P
KT = D // P
EPS = 1e-6
GLA_H, GLA_DK, GLA_DV, GLA_R, GLA_TAU = 4, 64, 128, 16, 16.0
SSD_DI, SSD_H, SSD_G, SSD_N, SSD_TAPS = 512, 8, 2, 128, 4
SSD_HD = SSD_DI // SSD_H
SSD_C = SSD_DI + 2 * SSD_G * SSD_N
MLA_H, MLA_NOPE, MLA_ROPE, MLA_V, MLA_QL, MLA_KVL = 4, 128, 64, 128, 384, 128
MLA_QK = MLA_NOPE + MLA_ROPE
DIL_H, DIL_HD = 4, 128
DIL_CONFIGS = ((128, 1), (512, 4), (2048, 16))
N_GATE = 2048
N_IN = 6232
GA, GB, GC, GD = range(4)

WIDTHS = (("aq", 256), ("ak", 256), ("av", 512), ("alr", GLA_R), ("xbc", SSD_C), ("dt", SSD_H), ("cq", MLA_QL),
          ("ckv", MLA_KVL), ("ckr", MLA_ROPE), ("dq", 512), ("dk", 512), ("dv", 512))
COL, _at = {}, 0
for _name, _w in WIDTHS:
    COL[_name] = _at
    _at += _w
N_U = _at
assert N_GATE + N_U == N_IN

WB = 512
BLOCKS = [("u", N_GATE + c, min(WB, N_U - c)) for c in range(0, N_U, WB)]
GATE_ORDER = (GB, GA, GC, GD)
GATE_BLOCK = {}
for _g in GATE_ORDER:
    GATE_BLOCK[len(BLOCKS)] = _g
    BLOCKS.append(("gate", _g * WB, WB))
N_INB = len(BLOCKS)
OUT_BLOCK = {}
for _c in range(D // WB):
    OUT_BLOCK[len(BLOCKS)] = _c
    BLOCKS.append(("out", _c * WB, WB))
UK = 2
UPB = KT // UK
UNITS = len(BLOCKS) * UPB
U_OUT = N_INB * UPB
RAW, SPLIT = 4, 4
assert UNITS % RAW == 0 and UNITS % SPLIT == 0

LEVELS = (64, 32, 16, 8, 4, 2, 1)
NEG = -1e30

C_ID, C_TRI, C_ONE, C_TRI2 = 0, 128, 256, 384
C_CZ, C_CM = 512, 640
C_DA = 768
C_DM = 1024
C_FR = 1280
NC = C_FR + DIL_HD // 2


def tables():
    c = np.zeros((P, NC), np.float32)
    i = np.arange(P)
    c[:, C_ID:C_ID + P] = i[:, None] == i[None, :]
    c[:, C_TRI:C_TRI + P] = i[:, None] <= i[None, :]
    c[:, C_ONE:C_ONE + P] = 1
    c[:, C_TRI2:C_TRI2 + P] = i[:, None] <= i[None, :]
    c[:, C_CM:C_CM + P] = np.where(i[None, :] <= i[:, None], 0, NEG)
    far = (P + i[:, None]) - np.arange(2 * P)[None, :]
    taps = sum(((far >= 0) & (far <= w) & (far % d == 0)).astype(np.float32) for w, d in DIL_CONFIGS)
    c[:, C_DA:C_DA + 2 * P] = np.where(taps > 0, 0, NEG)
    c[:, C_DM:C_DM + 2 * P] = taps
    half = DIL_HD // 2
    c[:, C_FR:] = np.exp(np.float32(-np.log(10000.0)) * np.arange(half, dtype=np.float32) * np.float32(2.0 / DIL_HD))
    m = np.zeros((P, 1 + len(LEVELS), P), np.int32)
    m[:, 0] = i[:, None] == i[None, :]
    for n, b in enumerate(LEVELS):
        key, query = i[:, None], i[None, :]
        m[:, 1 + n] = (key // (2 * b) == query // (2 * b)) & (key % (2 * b) < b) & (query % (2 * b) >= b)
    return c, m.reshape(P, -1)


PE_AT = {"gla qk": 10, "gla lr": 27, "gla z": 30, "gla G": 33}
XY_AT = {}
L0 = 37
for _n in range(8):
    PE_AT[f"gla level {_n}"] = L0 + 2 * _n
PE_AT["gla diag"] = L0 + 16
PE_AT["gla out"] = L0 + 20
B0 = 61
PE_AT |= {"ssd xT 0": B0, "ssd xT 1": B0 + 1, "ssd xs": B0 + 6, "ssd cum": B0 + 7, "ssd CB": B0 + 8,
          "ssd bcast 0": B0 + 9, "ssd Y 0": B0 + 12, "ssd bcast 1": B0 + 13, "ssd Y 1": B0 + 16}
M0 = 78
PE_AT |= {"mla cT": M0, "mla q 0": M0 + 1, "mla q 1": M0 + 2, "mla kv 0": M0 + 3, "mla kv 1": M0 + 4,
          "mla qT": M0 + 10, "mla kT": M0 + 11, "mla rT": M0 + 12}
for _n in range(2):
    PE_AT |= {f"mla S {_n}": M0 + 13 + 3 * _n, f"mla PT {_n}": M0 + 14 + 3 * _n, f"mla O {_n}": M0 + 15 + 3 * _n}
D0 = 97
PE_AT |= {"dil qT": D0, "dil kT": D0}
for _n in range(2):
    PE_AT |= {f"dil S {_n}": D0 + 2 + 2 * _n, f"dil PT {_n}": D0 + 3 + 2 * _n, f"dil O {_n}": D0 + 3 + 2 * _n}

EVAC_AT = {(b + 1) * UPB + (6 if b == N_INB - 4 else 2): b for b in range(N_INB)}

ORDER = {"pe": [], "act": [], "dve": [], "pool": []}
COUNTING = [True]


def build(nc, x_d, pos_d, ln_g, w_in, w_out, gla_w2, gla_b, gla_ng, conv_w, conv_b, dt_bias, A_log, D_d, ssd_ng,
          q_ng, kv_ng, w_uq, w_ukv, q_hg, k_hg, dq_g, dk_g, consts_d, masks_d, out_d):
    ctx = ExitStack()
    with ctx:
        def sb(name, shape, dt=F32):
            return ctx.enter_context(nc.sbuf_tensor(name, shape, dt))

        def sem(name):
            return ctx.enter_context(nc.semaphore(name))

        x = sb("x", [P, T, D])
        raw = sb("raw", [P, RAW, UK, WB])
        w_hi = sb("w_hi", [P, SPLIT, UK, WB], F32R)
        w_lo = sb("w_lo", [P, SPLIT, UK, WB], F32R)
        a_hi = sb("a_hi", [P, KT, S], F32R)
        a_lo = sb("a_lo", [P, KT, S], F32R)
        u = sb("u", [P, T, N_U])
        o = sb("o", [P, 4, T, WB])
        cst = sb("cst", [P, NC])
        lmask = sb("lmask", [P, 1 + len(LEVELS), P], U8)
        sc = sb("sincos", [P, 2, T, DIL_HD // 2])
        allp = sb("allp", [P, DEPTH * 56])
        prm = sb("prm", [P, 56])
        prow = sb("prow", [P, P])
        posi = sb("posi", [P, T], I32)
        posf = sb("posf", [P, T])
        NB = {"gla_ng": 128, "ssd_ng": 512, "q_ng": 384, "kv_ng": 128, "q_hg": 192, "k_hg": 192, "dq_g": 128, "dk_g": 128,
              "dtb": 8, "alog": 8, "D": 8}
        bc, at = {}, 0
        bcp = sb("bcp", [P, sum(NB.values())])
        for k, n in NB.items():
            bc[k] = bcp[:, at:at + n]
            at += n
        wuq = sb("wuq", [P, MLA_QL // P, MLA_H * MLA_QK])
        wukv = sb("wukv", [P, MLA_H * (MLA_NOPE + MLA_V)])
        w2 = sb("w2", [GLA_R + 1, 256])
        alrT = sb("alrT", [GLA_R + 1, S])
        eps = sb("eps", [P, 1])
        st = sb("st", [P, 160])
        ar = sb("arena", [P, 7704])

        ident = cst[:, C_ID:C_ID + P]
        tri = cst[:, C_TRI:C_TRI + P]
        ones = cst[:, C_ONE:C_ONE + P]
        tri_ones = cst[:, C_TRI:C_TRI + 2 * P]
        cmask = cst[:, C_CZ:C_CZ + 2 * P]
        dadd = cst[:, C_DA:C_DA + 2 * P]
        dmul = cst[:, C_DM:C_DM + 2 * P]

        def A(start, size, pat=None, **k):
            v = ar[:, start:start + size]
            return v.rearrange(pat, **k) if pat else v

        def two(v, n):
            return v.rearrange("p (a b) -> p a b", a=n)

        h_full = two(A(0, 1024), 4)
        qT = o[:, 2, 0, :].rearrange("p (a s) -> p a s", a=2)
        kT = o[:, 2, 1, :].rearrange("p (a s) -> p a s", a=2)
        acc = o[:, 3].rearrange("p r (t a q) -> p r t a q", t=T, a=2)
        GT = two(A(0, 512), 2)
        Dl = [A(512, 512), A(1024, 512)]
        Wl = [A(1536, 512), A(2048, 512)]
        cross = A(2560, 512, "p (r a q) -> p r a q", r=2, a=2)
        la = two(A(3072, 512), 2)
        lt = two(A(3584, 512), 2)
        xc = two(A(4096, 8 * (S + 3)), 8)
        xdt = two(A(4096, 1024), 2)
        CBm = two(A(256, 768), 2)
        M = two(A(6168, 1536), 4)
        Grow = A(0, 256)

        def conv(f):
            return u[:, f // 4, COL["xbc"] + (f % 4) * S:COL["xbc"] + (f % 4 + 1) * S]
        conv4 = [u[:, t, COL["xbc"]:COL["xbc"] + 4 * S] for t in range(2)]
        bsq = u[:, :, COL["cq"]:COL["cq"] + SSD_DI]
        mqk = u[:, :, 0:8 * MLA_QK].rearrange("p t (h d) -> p t h d", h=8)
        mv = u[:, :, 1536:2048]
        msq = A(0, 3072, "p (t h d) -> p t h d", t=T, h=8)
        mtmp = [A(i * 512, 512, "p (t h d) -> p t h d", t=T, h=8) for i in range(4)]
        mqT, mkT = two(A(0, 1024), 4), two(A(1024, 1024), 4)
        mrT = A(2048, 1024, "p (a b s) -> p a b s", a=2, b=2)
        mrr = A(2048, 1024, "p (t h d) -> p t h d", t=T, h=8)
        Pb, PT = two(A(4096, 768), 2), two(A(4864, 768), 2)
        cT = two(A(3072, 1024), 4)
        gate = two(A(3072, 1024), 2)
        dqk = u[:, :, COL["dq"]:COL["dq"] + 1024].rearrange("p t (h d) -> p t h d", h=8)
        dv = u[:, :, COL["dv"]:COL["dv"] + 512]
        dsq = A(5632, 2048, "p (t h d) -> p t h d", t=T, h=8)
        dtmp = [A(5632 + i * 512, 512, "p (t h d) -> p t h d", t=T, h=4) for i in range(4)]
        dqT, dkT = two(A(5632, 1024), 4), two(A(6656, 1024), 4)

        def stat(a, n):
            return st[:, a:a + n]
        xss, xrs = stat(0, 2), stat(2, 2)
        gss, grs = stat(4, 8), stat(12, 8)
        dtv, dta, las, gcol, eA, dts = stat(20, 16), stat(36, 16), stat(52, 16), stat(68, 16), stat(84, 8), stat(92, 16)
        bss, brs = stat(108, 4), stat(112, 4)
        css, crs = stat(116, 4), stat(120, 4)
        mx, nm, sm, ri = stat(124, 4), stat(128, 4), stat(132, 4), stat(136, 4)
        mss = stat(140, 16)
        mrs = mss

        acc_ps = ctx.enter_context(nc.psum_tensor("gemm", [P, 2, T, WB], F32))
        pair = ctx.enter_context(nc.psum_tensor("pairs", [P, 2, 2, 512], F32))

        consts_in, small_in, x_in, params_in, out_written = sem("consts_in"), sem("small_in"), sem("x_in"), sem("params_in"), sem("out_written")
        layer_ready, paced, setup_chain = sem("layer_ready"), sem("paced"), sem("setup_chain")
        weights_in = [sem(f"weights_in_{i}") for i in range(RAW)]
        hi_done, split_done, unit_used, block_done = sem("hi_done"), sem("split_done"), sem("unit_used"), sem("block_done")
        stage = {e: sem(f"{e}_stages") for e in ORDER}
        setup = {e: sem(f"{e}_setup") for e in ORDER}
        seen = {e: [] for e in ORDER}

        def signal(e, name):
            if COUNTING[0]:
                ORDER[e].append(name)
            else:
                assert ORDER[e][len(seen[e])] == name, (e, name, ORDER[e][len(seen[e])])
            seen[e].append(name)
            return stage[e], 1

        def reached(e, l):
            def f(name):
                n = ORDER[e].index(name) if name in ORDER[e] else 0
                if not COUNTING[0]:
                    assert name in ORDER[e], name
                return stage[e], l * len(ORDER[e]) + n + 1
            return f

        block = ctx.enter_context(nc.Block())

        def weights(l, b, k0):
            kind, c0, w = BLOCKS[b]
            m = w_out if kind == "out" else w_in
            return m[l].rearrange("(k p) n -> p k n", p=P)[:, k0:k0 + UK, c0:c0 + w]

        N_PARAMS = len(NB) + 4

        @block.sync
        def _(sp):
            sp.dma_start(cst[:, :], consts_d).then_inc(consts_in, 16)
            sp.dma_start(x[:, :, :], x_d.rearrange("o (t p) n -> p (o t) n", p=P)).then_inc(x_in, 16)
            with sp.Fori(0, DEPTH) as l:
                for n in range(UNITS):
                    b, k0 = n // UPB, n % UPB * UK
                    sp.wait_ge(split_done, l * UNITS + n + 1)
                    if k0 == 0 and BLOCKS[b][1] == 0:
                        sp.sem_inc(paced, 1)
                    sp.dma_start(raw[:, n % RAW, :, 0:BLOCKS[b][2]], weights(l, b, k0)).then_inc(weights_in[n % RAW], 16)
            for c in range(D // WB):
                sp.wait_ge(*reached("dve", DEPTH - 1)(f"x {c}"))
                sp.dma_start(out_d.rearrange("o (t p) n -> p (o t) n", p=P)[:, :, c * WB:(c + 1) * WB],
                             x[:, :, c * WB:(c + 1) * WB]).then_inc(out_written, 16)
            sp.wait_ge(out_written, 16 * (D // WB))

        @block.gpsimd
        def _(pool):
            rows = 0
            for l in range(DEPTH):
                for src, n in ((ln_g[l].rearrange("(k p) -> k p", p=P), KT),
                               (conv_w[l].rearrange("j (c p) -> (j c) p", p=P), SSD_TAPS * 8),
                               (conv_b[l].rearrange("(c p) -> c p", p=P), 8)):
                    pool.dma_start(prow[rows:rows + n, :], src).then_inc(small_in, 16)
                    rows += n
            pool.dma_start(posi[:, :], pos_d.rearrange("o (t p) -> p (o t)", p=P), allow_slow_non_contiguous=True).then_inc(small_in, 16)
            pool.dma_start(A(1024, 1024).bitcast(I32), masks_d).then_inc(small_in, 16)
            with pool.Fori(0, DEPTH) as l:
                pool.wait_ge(layer_ready, l + 1)
                for k, src in (("gla_ng", gla_ng), ("ssd_ng", ssd_ng), ("q_ng", q_ng), ("kv_ng", kv_ng), ("q_hg", q_hg),
                               ("k_hg", k_hg), ("dq_g", dq_g), ("dk_g", dk_g), ("dtb", dt_bias), ("alog", A_log), ("D", D_d)):
                    pool.dma_start(bc[k], src[l].partition_broadcast(P)).then_inc(params_in, 16)
                pool.dma_start(w2[0:GLA_R, :], gla_w2[l]).then_inc(params_in, 16)
                pool.dma_start(w2[GLA_R:GLA_R + 1, :], gla_b[l].unsqueeze(0)).then_inc(params_in, 16)
                pool.dma_start(wuq[:, :, :], w_uq[l].rearrange("(k p) n -> p k n", p=P)).then_inc(params_in, 16)
                pool.dma_start(wukv[:, :], w_ukv[l]).then_inc(params_in, 16)

        N_SMALL = 16 * (3 * DEPTH + 2)

        @block.tensor
        def _(pe):
            pe.sem_inc(unit_used, SPLIT)
            pe.wait_ge(consts_in, 16)
            pe.wait_ge(small_in, N_SMALL)
            pe.transpose(pair[:, 1, 1, 0:56 * DEPTH], prow[0:56 * DEPTH, :], ident[0:56 * DEPTH, 0:56 * DEPTH]).then_inc(setup["pe"], 1)
            with pe.Fori(0, DEPTH) as l:
                me, act, dve = reached("pe", l), reached("act", l), reached("dve", l)

                def unit(n):
                    b, k0 = n // UPB, n % UPB * UK
                    w = BLOCKS[b][2]
                    if k0 == 0 and b >= 2:
                        e = f"evac {b - 2}"
                        if b - 2 in OUT_BLOCK:
                            pe.wait_ge(*dve(f"x {OUT_BLOCK[b - 2]}"))
                        else:
                            pe.wait_ge(*act(e))
                    pe.wait_ge(split_done, l * UNITS + n + 1 + RAW)
                    if n < UPB and n % 2 == 0:
                        pe.wait_ge(*dve(f"xT {n // 2}"))
                    if U_OUT <= n < U_OUT + UPB and n % 2 == 0:
                        pe.wait_ge(*dve(f"yT {(n - U_OUT) // 2}"))
                    for j in range(UK):
                        k = k0 + j
                        for t in range(T):
                            acc_t = acc_ps[:, b % 2, t, 0:w]
                            tok = slice(t * P, (t + 1) * P)
                            hi, lo = w_hi[:, n % SPLIT, j, 0:w], w_lo[:, n % SPLIT, j, 0:w]
                            pe.matmul(acc_t, a_hi[:, k, tok], hi, start=k == 0, stop=False)
                            pe.matmul(acc_t, a_hi[:, k, tok], lo, start=False, stop=False)
                            last = pe.matmul(acc_t, a_lo[:, k, tok], hi, start=False, stop=k == KT - 1)
                    last.then_inc(unit_used, 1)

                jobs = [0]

                def bank():
                    jobs[0] += 1
                    return pair[:, jobs[0] % 2]

                def act_T(src, name, j):
                    ps = bank()
                    for kk in range(4):
                        for t in range(T):
                            f = (4 * j + kk) * P
                            last = pe.transpose(ps[:, kk // 2, (kk % 2) * S + t * P:(kk % 2) * S + (t + 1) * P], src(t, f), ident)
                    last.then_inc(*signal("pe", f"{name} {j}"))

                def xT(j):
                    if j == 0:
                        pe.wait_ge(layer_ready, l + 1)
                    if j >= 2:
                        pe.wait_ge(*dve(f"xT {j - 2}"))
                    act_T(lambda t, f: x[:, t, f:f + P], "xT", j)

                def yT(j):
                    pe.wait_ge(*dve(f"y {j}"))
                    pe.wait_ge(*dve("gateB") if j < 0 else dve("dil O 1") if j < 2 else dve(f"yT {j - 2}"))
                    act_T(lambda t, f: o[:, f // WB, t, f % WB:f % WB + P], "yT", j)

                def gla_qk():
                    pe.wait_ge(*act("evac 0"))
                    pe.wait_ge(*dve("xT 3"))
                    ps = bank()
                    for a in range(2):
                        for p in range(2):
                            for t in range(T):
                                c = a * 256 + p * P
                                last = pe.transpose(ps[:, a, p * S + t * P:p * S + (t + 1) * P], u[:, t, c:c + P], ident)
                    last.then_inc(*signal("pe", "gla qk"))

                def gla_lr():
                    pe.wait_ge(*act("evac 2"))
                    pe.wait_ge(*dve("xT 3"))
                    ps = bank()
                    for t in range(T):
                        last = pe.transpose(ps[0:GLA_R, 0, t * P:(t + 1) * P], u[:, t, COL["alr"]:COL["alr"] + GLA_R], ident)
                    last.then_inc(*signal("pe", "gla lr"))

                def gla_z():
                    pe.wait_ge(*act("gla lr"))
                    pe.wait_ge(*act("gla k"))
                    pe.wait_ge(params_in, (l + 1) * 16 * N_PARAMS)
                    ps = bank()
                    for t in range(T):
                        last = pe.matmul(ps[:, 0, t * 256:(t + 1) * 256], alrT[:, t * P:(t + 1) * P], w2[:, :], start=True, stop=True)
                    last.then_inc(*signal("pe", "gla z"))

                def gla_G():
                    pe.wait_ge(*dve("gla la"))
                    ps = bank()
                    for p in range(2):
                        pe.matmul(ps[:, 0, p * S:(p + 1) * S], la[:, 0, p * P:(p + 1) * P], tri_ones, start=True, stop=False)
                        last = pe.matmul(ps[:, 0, p * S + P:(p + 1) * S], la[:, 1, p * P:(p + 1) * P], tri, start=False, stop=True)
                    last.then_inc(*signal("pe", "gla G"))

                def gla_level(n):
                    pe.wait_ge(*dve(f"gla W {n}"))
                    if n == 1:
                        pe.wait_ge(*act("gla G"))
                    if n >= 2:
                        pe.wait_ge(*dve(f"gla merge {n - 2}"))
                    if n == 2:
                        pe.wait_ge(*dve("gla cross"))
                    ps = bank()
                    W = two(Wl[n % 2], 2)
                    for r in range(2):
                        for p in range(2):
                            rows = slice(64 * r, 64 * r + 64)
                            if n == 0:
                                last = pe.matmul(ps[:, r, p * P:(p + 1) * P], W[rows, p, 0:P], W[rows, p, P:S], start=True, stop=True)
                            else:
                                for t in range(T):
                                    tok = slice(t * P, (t + 1) * P)
                                    c = (t * 2 + p) * P
                                    last = pe.matmul(ps[:, r, c:c + P], W[rows, p, tok], W[rows, p, tok], start=True, stop=True)
                    last.then_inc(*signal("pe", f"gla level {n}"))

                def gla_diag():
                    pe.wait_ge(*dve("gla merge 6"))
                    ps = bank()
                    for r in range(2):
                        for p in range(2):
                            for t in range(T):
                                rows, tok = slice(64 * r, 64 * r + 64), slice(t * P, (t + 1) * P)
                                c = (t * 2 + p) * P
                                last = pe.matmul(ps[:, r, c:c + P], kT[rows, p, tok], qT[rows, p, tok], start=True, stop=True)
                    last.then_inc(*signal("pe", "gla diag"))

                def gla_out():
                    pe.wait_ge(*dve("gla diag"))
                    ps = bank()
                    for h in range(GLA_H):
                        r, p = h % 2, h // 2
                        c = slice(h * GLA_DV, (h + 1) * GLA_DV)
                        v = slice(COL["av"] + h * GLA_DV, COL["av"] + (h + 1) * GLA_DV)
                        pe.matmul(ps[:, 0, c], acc[:, r, 0, p], u[:, 0, v], start=True, stop=True)
                        pe.matmul(ps[:, 1, c], cross[:, r, p], u[:, 0, v], start=True, stop=False)
                        last = pe.matmul(ps[:, 1, c], acc[:, r, 1, p], u[:, 1, v], start=False, stop=True)
                    last.then_inc(*signal("pe", "gla out"))

                def ssd_xT(i):
                    pe.wait_ge(*act("evac 4"))
                    pe.wait_ge(*dve("gla diag") if i == 0 else dve("gla o"))
                    ps = bank()
                    for kk in range(4):
                        for t in range(T):
                            c = COL["xbc"] + (4 * i + kk) * P
                            last = pe.transpose(ps[:, kk // 2, (kk % 2) * S + t * P:(kk % 2) * S + (t + 1) * P], u[:, t, c:c + P], ident)
                    last.then_inc(*signal("pe", f"ssd xT {i}"))

                def ssd_xs():
                    pe.wait_ge(*act("ssd silu 1"))
                    ps = bank()
                    for f in range(4):
                        for t in range(T):
                            last = pe.transpose(ps[:, t, f * P:(f + 1) * P], conv(f)[:, t * P:(t + 1) * P], ident)
                    last.then_inc(*signal("pe", "ssd xs"))

                def ssd_cum():
                    pe.wait_ge(*dve("ssd la"))
                    ps = bank()
                    l8 = [las[:, t * SSD_H:(t + 1) * SSD_H] for t in range(T)]
                    pe.matmul(ps[0:SSD_H, 0, 0:S], l8[0], tri_ones, start=True, stop=False)
                    pe.matmul(ps[0:SSD_H, 0, P:S], l8[1], tri, start=False, stop=True)
                    pe.matmul(ps[:, 1, 0:8], tri, l8[0], start=True, stop=True)
                    pe.matmul(ps[:, 1, 8:16], ones, l8[0], start=True, stop=False)
                    pe.matmul(ps[:, 1, 8:16], tri, l8[1], start=False, stop=True).then_inc(*signal("pe", "ssd cum"))

                def ssd_CB():
                    pe.wait_ge(*dve("ssd xdt"))
                    ps = bank()
                    for g in range(SSD_G):
                        pe.matmul(ps[:, g, 0:S], conv(4 + g)[:, 0:P], conv(6 + g), start=True, stop=True)
                        last = pe.matmul(ps[:, g, S:S + P], conv(4 + g)[:, P:S], conv(6 + g)[:, P:S], start=True, stop=True)
                    last.then_inc(*signal("pe", "ssd CB"))

                def ssd_bcast(g):
                    pe.wait_ge(*act("ssd grow"))
                    pe.wait_ge(*act("ssd gcol") if g == 0 else dve("ssd E 0"))
                    ps = bank()
                    for h in range(4):
                        pick = ident[0:SSD_H, 4 * g + h:4 * g + h + 1].to_broadcast([SSD_H, P])
                        last = pe.matmul(ps[:, h // 2, (h % 2) * S:(h % 2 + 1) * S], pick, Grow[0:SSD_H, :], start=True, stop=True)
                    last.then_inc(*signal("pe", f"ssd bcast {g}"))

                def ssd_Y(g):
                    pe.wait_ge(*dve(f"ssd M {g}"))
                    pe.wait_ge(*dve("ssd CB") if g == 0 else dve("ssd y 0"))
                    ps = bank()
                    for h in range(4):
                        hh = slice((4 * g + h) * SSD_HD, (4 * g + h + 1) * SSD_HD)
                        c = slice(h * SSD_HD, (h + 1) * SSD_HD)
                        pe.matmul(ps[:, 0, c], M[:, h, 0:P], xdt[:, 0, hh], start=True, stop=True)
                        pe.matmul(ps[:, 1, c], M[:, h, P:S], xdt[:, 0, hh], start=True, stop=False)
                        last = pe.matmul(ps[:, 1, c], M[:, h, S:S + P], xdt[:, 1, hh], start=False, stop=True)
                    last.then_inc(*signal("pe", f"ssd Y {g}"))

                def mla_cT():
                    pe.wait_ge(*dve("mla cn"))
                    pe.wait_ge(*dve("ssd y 0"))
                    pe.wait_ge(*dve("ssd E 1"))
                    ps = bank()
                    for kk in range(4):
                        for t in range(T):
                            c = COL["cq"] + kk * P
                            last = pe.transpose(ps[:, kk // 2, (kk % 2) * S + t * P:(kk % 2) * S + (t + 1) * P], u[:, t, c:c + P], ident)
                    last.then_inc(*signal("pe", "mla cT"))

                def mla_q(t):
                    pe.wait_ge(*act("mla cT"))
                    pe.wait_ge(*dve("ssd y 1") if t == 0 else act("mla cT"))
                    ps = bank()
                    for half, (c, w) in enumerate(((0, 512), (512, 256))):
                        for k in range(3):
                            last = pe.matmul(ps[:, half, 0:w], cT[:, k, t * P:(t + 1) * P], wuq[:, k, c:c + w], start=k == 0, stop=k == 2)
                    last.then_inc(*signal("pe", f"mla q {t}"))

                def mla_kv(t):
                    pe.wait_ge(*act(f"mla q {t}"))
                    ps = bank()
                    for half in range(2):
                        last = pe.matmul(ps[:, half, :], cT[:, 3, t * P:(t + 1) * P], wukv[:, half * 512:half * 512 + 512], start=True, stop=True)
                    last.then_inc(*signal("pe", f"mla kv {t}"))

                def heads_T(name, src, free):
                    pe.wait_ge(*free)
                    ps = bank()
                    for h in range(4):
                        for t in range(T):
                            last = pe.transpose(ps[:, h // 2, (h % 2) * S + t * P:(h % 2) * S + (t + 1) * P], src(t, h), ident)
                    last.then_inc(*signal("pe", name))

                def scores(m, i, kq, rope, free):
                    pe.wait_ge(*free)
                    ps = bank()
                    for r in range(2):
                        h = 2 * i + r
                        for c0, c1, qs in ((0, P, slice(0, P)), (P, P + S, slice(P, S))):
                            ks = slice(0, c1 - c0)
                            q, k = kq
                            last = pe.matmul(ps[:, r, c0:c1], q[:, h, qs], k[:, h, ks], start=True, stop=not rope)
                            if rope:
                                rows = slice(64 * (h % 2), 64 * (h % 2) + 64)
                                last = pe.matmul(ps[:, r, c0:c1], mrT[rows, 0, h // 2, qs], mrT[rows, 1, h // 2, ks], start=False, stop=True)
                    last.then_inc(*signal("pe", f"{m} S {i}"))

                def probs_T(m, i, free):
                    pe.wait_ge(*(act if m == "mla" else dve)(f"{m} P {i}"))
                    pe.wait_ge(*free)
                    ps = bank()
                    for r in range(2):
                        for c in range(3):
                            last = pe.transpose(ps[:, r, c * P:(c + 1) * P], Pb[:, r, c * P:(c + 1) * P], ident)
                    last.then_inc(*signal("pe", f"{m} PT {i}"))

                def values(m, i, v):
                    pe.wait_ge(*act(f"{m} PT {i}"))
                    pe.wait_ge(*dve(f"{m} max {i}"))
                    ps = bank()
                    for r in range(2):
                        h, c = 2 * i + r, slice(r * P, (r + 1) * P)
                        hv = slice(h * P, (h + 1) * P)
                        pe.matmul(ps[:, 0, c], PT[:, r, 0:P], v[:, 0, hv], start=True, stop=True)
                        pe.matmul(ps[:, 1, c], PT[:, r, P:2 * P], v[:, 0, hv], start=True, stop=False)
                        last = pe.matmul(ps[:, 1, c], PT[:, r, 2 * P:3 * P], v[:, 1, hv], start=False, stop=True)
                    last.then_inc(*signal("pe", f"{m} O {i}"))

                def mla_qT():
                    pe.wait_ge(*dve("mla rope"))
                    heads_T("mla qT", lambda t, h: mqk[:, t, h, 0:P], act("mla kv 0"))

                def mla_kT():
                    heads_T("mla kT", lambda t, h: mqk[:, t, 4 + h, 0:P], act("mla kv 1"))

                def mla_rT():
                    rr = mrr.rearrange("p t (a b) d -> p t a (b d)", b=2)
                    heads_T("mla rT", lambda t, h: rr[:, t, h], act("mla qT"))

                run = {"gla qk": gla_qk, "gla lr": gla_lr, "gla z": gla_z, "gla G": gla_G, "gla diag": gla_diag,
                       "gla out": gla_out, "ssd xs": ssd_xs, "ssd cum": ssd_cum, "ssd CB": ssd_CB, "mla cT": mla_cT,
                       "mla qT": mla_qT, "mla kT": mla_kT, "mla rT": mla_rT}

                def stages(n):
                    for name in PE_AT:
                        if PE_AT[name] != n:
                            continue
                        i = int(name[-1]) if name[-1].isdigit() else None
                        if name in run:
                            run[name]()
                        elif name.startswith("gla level"):
                            gla_level(i)
                        elif name.startswith("ssd xT"):
                            ssd_xT(i)
                        elif name.startswith("ssd bcast"):
                            ssd_bcast(i)
                        elif name.startswith("ssd Y"):
                            ssd_Y(i)
                        elif name.startswith("mla q "):
                            mla_q(i)
                        elif name.startswith("mla kv"):
                            mla_kv(i)
                        elif name == "dil qT":
                            pe.wait_ge(*dve("dil rope 1"))
                            heads_T(name, lambda t, h: dqk[:, t, h], act("mla PT 1"))
                        elif name == "dil kT":
                            heads_T(name, lambda t, h: dqk[:, t, 4 + h], dve("mla O 1"))
                        elif name.startswith("mla S"):
                            scores("mla", i, (mqT, mkT), True, act("mla rT") if i == 0 else act("mla PT 0"))
                        elif name.startswith("dil S"):
                            scores("dil", i, (dqT, dkT), False, act("dil kT") if i == 0 else act("dil PT 0"))
                        elif name.startswith("mla PT"):
                            probs_T("mla", i, act("mla rT") if i == 0 else dve("mla O 0"))
                        elif name.startswith("dil PT"):
                            probs_T("dil", i, act("dil kT") if i == 0 else dve("dil O 0"))
                        elif name.startswith("mla O"):
                            values("mla", i, mv)
                        elif name.startswith("dil O"):
                            values("dil", i, dv)

                xT(0)
                xT(1)
                for n in range(UNITS):
                    if n == U_OUT:
                        yT(0)
                        yT(1)
                    unit(n)
                    if n in (1, 3):
                        xT(2 + n // 2)
                    if n in (U_OUT + 1, U_OUT + 3):
                        yT(2 + (n - U_OUT) // 2)
                    stages(n)

        SC = {"mla": MLA_QK ** -0.5, "dil": DIL_HD ** -0.5}

        def pair_of(name):
            n = ORDER["pe"].index(name) if name in ORDER["pe"] else 0
            return pair[:, (n + 1) % 2]

        def slot(name, lag=3):
            return PE_AT[name] + lag

        @block.scalar
        def _(act_):
            act_.preload_act_table_set("natural_log_exp_and_others")
            act_.wait_ge(consts_in, 16)
            act_.wait_ge(small_in, N_SMALL)
            act_.wait_ge(setup["dve"], 5)
            act_.preload_act_table_set("silu_and_others")
            act_.activation(sc[:, :, :, :].rearrange("p a t d -> p (a t d)"), sc[:, :, :, :].rearrange("p a t d -> p (a t d)"), ACT.Sin).then_inc(setup["act"], 1)
            act_.preload_act_table_set("natural_log_exp_and_others")
            with act_.Fori(0, DEPTH) as l:
                pe, me, dve = reached("pe", l), reached("act", l), reached("dve", l)
                A_ = act_.activation

                def hi(n):
                    w = BLOCKS[n // UPB][2]
                    act_.wait_ge(weights_in[n % RAW], (l * (UNITS // RAW) + n // RAW + 1) * 16)
                    act_.wait_ge(unit_used, l * UNITS + n + 1)
                    A_(w_hi[:, n % SPLIT, :, 0:w], raw[:, n % RAW, :, 0:w], ACT.Copy).then_inc(hi_done, 1)

                def rsqrt(dst, src, name, scale=1.0):
                    A_(dst, src, ACT.Ln, bias=eps[:, 0:1], scale=scale).then_inc(*signal("act", name + " ln"))
                    act_.wait_ge(*me(name + " ln"))
                    A_(dst, dst, ACT.Exp, scale=-0.5).then_inc(*signal("act", name))

                def x_stats():
                    act_.wait_ge(layer_ready, l + 1)
                    for t in range(T):
                        last = A_(u[:, t, 0:D], x[:, t, :], ACT.Square, accum_out=xss[:, t:t + 1])
                    last.then_inc(*signal("act", "xss"))
                    act_.wait_ge(*me("xss"))
                    rsqrt(xrs, xss, "xrs", 1.0 / D)

                def xT(j):
                    act_.wait_ge(*dve(f"xg {j}"))
                    A_(a_hi[:, 4 * j:4 * j + 4, :], h_full, ACT.Copy).then_inc(*signal("act", f"xT {j}"))

                def yT(j):
                    act_.wait_ge(*pe(f"yT {j}"))
                    if j == 0:
                        act_.wait_ge(unit_used, l * UNITS + U_OUT + SPLIT)
                    A_(a_hi[:, 4 * j:4 * j + 4, :], pair_of(f"yT {j}").rearrange("p b (k s) -> p (b k) s", k=2), ACT.Copy).then_inc(*signal("act", f"yT {j}"))

                def evac(b):
                    kind, c0, w = BLOCKS[b]
                    act_.wait_ge(unit_used, l * UNITS + (b + 1) * UPB + SPLIT)
                    if kind == "u":
                        for t in range(T):
                            last = A_(u[:, t, c0 - N_GATE:c0 - N_GATE + w], acc_ps[:, b % 2, t, 0:w], ACT.Copy, scale=xrs[:, t:t + 1])
                    else:
                        g = GATE_ORDER.index(GATE_BLOCK[b])
                        act_.wait_ge(*(pe("mla kv 1") if g == 0 else dve(f"gated {GB}" if g == 1 else f"y {GATE_ORDER[g - 1]}")))
                        for t in range(T):
                            last = A_(gate[:, t, :], acc_ps[:, b % 2, t, :], ACT.Silu, scale=xrs[:, t:t + 1])
                    last.then_inc(*signal("act", f"evac {b}"))

                def gla_qk():
                    act_.wait_ge(*pe("gla qk"))
                    ps = pair_of("gla qk")
                    A_(qT, two(ps[:, 0, :], 2), ACT.Copy, scale=GLA_DK ** -0.5).then_inc(*signal("act", "gla q"))
                    A_(kT, two(ps[:, 1, :], 2), ACT.Copy).then_inc(*signal("act", "gla k"))

                def gla_lr():
                    act_.wait_ge(*pe("gla lr"))
                    A_(alrT[0:GLA_R, :], pair_of("gla lr")[0:GLA_R, 0, 0:S], ACT.Copy).then_inc(*signal("act", "gla lr"))

                def gla_z():
                    act_.wait_ge(*pe("gla z"))
                    A_(lt, two(pair_of("gla z")[:, 0, :], 2), ACT.Abs).then_inc(*signal("act", "gla abs"))
                    act_.wait_ge(*me("gla abs"))
                    A_(lt, lt, ACT.Exp, scale=-1.0).then_inc(*signal("act", "gla exp"))
                    act_.wait_ge(*me("gla exp"))
                    A_(lt, lt, ACT.Ln, bias=1.0).then_inc(*signal("act", "gla ln"))

                def gla_G():
                    act_.wait_ge(*pe("gla G"))
                    A_(GT, two(pair_of("gla G")[:, 0, :], 2), ACT.Copy, scale=1.0 / GLA_TAU).then_inc(*signal("act", "gla G"))

                def gla_E(n):
                    B = P >> n
                    v = Dl[n % 2].rearrange("p (a s) -> p a s", s=2 * B)
                    act_.wait_ge(*dve(f"gla D {n}"))
                    A_(v[:, :, 0:B], v[:, :, 0:B], ACT.Exp, scale=-1.0)
                    A_(v[:, :, B:2 * B], v[:, :, B:2 * B], ACT.Exp).then_inc(*signal("act", f"gla E {n}"))

                def gla_norm():
                    act_.wait_ge(*pe("gla out"))
                    act_.wait_ge(*pe("gla diag"))
                    ps = pair_of("gla out")
                    A_(A(512, 1024), ps.rearrange("p t c -> p (t c)"), ACT.Square).then_inc(*signal("act", "gla sq"))
                    act_.wait_ge(*dve("gla ss"))
                    rsqrt(grs, gss, "gla rs", 1.0 / GLA_DV)

                def ssd_xT(i):
                    act_.wait_ge(*pe(f"ssd xT {i}"))
                    A_(xc[:, 4 * i:4 * i + 4, 3:3 + S], pair_of(f"ssd xT {i}").rearrange("p b (k s) -> p (b k) s", k=2), ACT.Copy).then_inc(*signal("act", f"ssd xT {i}"))

                def ssd_silu(i):
                    act_.wait_ge(*dve("ssd conv"))
                    A_(conv4[1 - i], conv4[1 - i], ACT.Silu).then_inc(*signal("act", f"ssd silu {i}"))

                def ssd_dt():
                    act_.wait_ge(*dve("ssd dt0"))
                    A_(dta, dtv, ACT.Abs).then_inc(*signal("act", "ssd abs"))
                    act_.wait_ge(*me("ssd abs"))
                    A_(dta, dta, ACT.Exp, scale=-1.0).then_inc(*signal("act", "ssd exp"))
                    A_(eA, bc["alog"], ACT.Exp).then_inc(*signal("act", "ssd eA"))
                    act_.wait_ge(*me("ssd eA"))
                    A_(dta, dta, ACT.Ln, bias=1.0).then_inc(*signal("act", "ssd ln"))

                def ssd_cum():
                    act_.wait_ge(*pe("ssd cum"))
                    ps = pair_of("ssd cum")
                    A_(Grow[0:SSD_H, :], ps[0:SSD_H, 0, 0:S], ACT.Copy).then_inc(*signal("act", "ssd grow"))
                    A_(gcol, ps[:, 1, 0:16], ACT.Copy).then_inc(*signal("act", "ssd gcol"))

                def ssd_exp(g):
                    act_.wait_ge(*dve(f"ssd E {g}"))
                    A_(M[:, :, :], M[:, :, :], ACT.Exp).then_inc(*signal("act", f"ssd exp {g}"))

                def ssd_sq():
                    act_.wait_ge(*dve(f"gated {GB}"))
                    A_(bsq, o[:, GB], ACT.Square).then_inc(*signal("act", "ssd sq"))
                    act_.wait_ge(*dve("ssd ss"))
                    rsqrt(brs, bss, "ssd rs", 1.0 / 256)

                def mla_c():
                    act_.wait_ge(*me("evac 5"))
                    for t in range(T):
                        A_(A(1536 + t * 512, MLA_QL), u[:, t, COL["cq"]:COL["cq"] + MLA_QL], ACT.Square, scale=MLA_QL ** -0.5, accum_out=css[:, t:t + 1])
                        last = A_(A(1536 + t * 512 + MLA_QL, MLA_KVL), u[:, t, COL["ckv"]:COL["ckv"] + MLA_KVL], ACT.Square, scale=MLA_KVL ** -0.5, accum_out=css[:, 2 + t:3 + t])
                    last.then_inc(*signal("act", "mla css"))
                    act_.wait_ge(*me("mla css"))
                    rsqrt(crs, css, "mla crs")

                def mla_cT():
                    act_.wait_ge(*pe("mla cT"))
                    A_(cT, pair_of("mla cT").rearrange("p b (k s) -> p (b k) s", k=2), ACT.Copy).then_inc(*signal("act", "mla cT"))

                def mla_q(t):
                    act_.wait_ge(*pe(f"mla q {t}"))
                    A_(u[:, t, 0:768], pair_of(f"mla q {t}").rearrange("p b c -> p (b c)")[:, 0:768], ACT.Copy).then_inc(*signal("act", f"mla q {t}"))

                def mla_kv(t):
                    act_.wait_ge(*pe(f"mla kv {t}"))
                    ps = pair_of(f"mla kv {t}").rearrange("p b (h c) -> p (b h) c", h=2)
                    A_(mqk[:, t, 4:8, 0:P], ps[:, :, 0:P], ACT.Copy)
                    A_(mqk[:, t, 4:8, P:MLA_QK], u[:, t, COL["ckr"]:COL["ckr"] + 64].unsqueeze(1).to_broadcast([P, 4, 64]), ACT.Copy)
                    A_(mv[:, t, :].rearrange("p (h c) -> p h c", h=4), ps[:, :, P:2 * P], ACT.Copy).then_inc(*signal("act", f"mla kv {t}"))

                def mla_sq():
                    act_.wait_ge(*me("mla kv 1"))
                    for t in range(T):
                        last = A_(msq[:, t], mqk[:, t], ACT.Square)
                    last.then_inc(*signal("act", "mla sq"))
                    act_.wait_ge(*dve("mla ss"))
                    rsqrt(mrs, mss, "mla rs", 1.0 / MLA_QK)

                def dil_sq():
                    act_.wait_ge(*me("evac 7"))
                    for t in range(T):
                        last = A_(dsq[:, t], dqk[:, t], ACT.Square)
                    last.then_inc(*signal("act", "dil sq"))
                    act_.wait_ge(*dve("dil ss"))
                    rsqrt(mrs, mss, "dil rs", 1.0 / DIL_HD)

                def heads_T(name, dst):
                    act_.wait_ge(*pe(name))
                    A_(dst, pair_of(name).rearrange("p b (k s) -> p (b k) s", k=2), ACT.Copy).then_inc(*signal("act", name))

                def probs(m, i):
                    act_.wait_ge(*dve(f"{m} nmax {i}"))
                    for r in range(2):
                        for t, (c0, c1) in enumerate(((0, P), (P, P + S))):
                            j = 2 * r + t
                            last = A_(Pb[:, r, c0:c1], Pb[:, r, c0:c1], ACT.Exp, bias=nm[:, j:j + 1], scale=SC[m],
                                      accum_out=sm[:, j:j + 1] if m == "mla" else None)
                    last.then_inc(*signal("act", f"{m} P {i}"))

                def probs_T(m, i):
                    act_.wait_ge(*pe(f"{m} PT {i}"))
                    A_(PT[:, :, :], pair_of(f"{m} PT {i}")[:, :, 0:384], ACT.Copy).then_inc(*signal("act", f"{m} PT {i}"))

                for n in range(UNITS):
                    hi(n)
                    if n == 1:
                        xT(0)
                        xT(1)
                        x_stats()
                    if n == 3:
                        xT(2)
                    if n == 5:
                        xT(3)
                    if n == U_OUT + 3:
                        yT(0)
                        yT(1)
                        yT(2)
                    if n == U_OUT + 5:
                        yT(3)
                    if n in EVAC_AT:
                        evac(EVAC_AT[n])
                    if n == slot("gla qk"):
                        gla_qk()
                    if n == slot("gla lr"):
                        gla_lr()
                    if n == slot("gla z"):
                        gla_z()
                    if n == slot("gla G"):
                        gla_G()
                        gla_E(0)
                        gla_E(1)
                    for i in range(6):
                        if n == PE_AT[f"gla level {i}"] + 2:
                            gla_E(i + 2)
                    if n == slot("gla out"):
                        gla_norm()
                    for i in range(2):
                        if n == slot(f"ssd xT {i}"):
                            ssd_xT(i)
                    if n == slot("ssd xT 1", 2):
                        ssd_dt()
                    if n == slot("ssd xs", 0):
                        ssd_silu(0)
                        ssd_silu(1)
                    if n == slot("ssd cum"):
                        ssd_cum()
                    for i in range(2):
                        if n == slot(f"ssd bcast {i}"):
                            ssd_exp(i)
                    if n == slot("mla cT", -1):
                        mla_c()
                    if n == slot("mla cT"):
                        mla_cT()
                    for i in range(2):
                        if n == slot(f"mla q {i}"):
                            mla_q(i)
                        if n == slot(f"mla kv {i}"):
                            mla_kv(i)
                    if n == slot("mla kv 1"):
                        mla_sq()
                    if n == slot("mla qT"):
                        heads_T("mla qT", mqT)
                    if n == slot("mla kT"):
                        heads_T("mla kT", mkT)
                    if n == slot("mla rT"):
                        heads_T("mla rT", mrT.rearrange("p a b s -> p (a b) s"))
                    if n == slot("mla S 0", 1):
                        dil_sq()
                    if n == slot("dil qT"):
                        heads_T("dil qT", dqT)
                    if n == slot("dil kT"):
                        heads_T("dil kT", dkT)
                    for m in ("mla", "dil"):
                        for i in range(2):
                            if n == slot(f"{m} S {i}"):
                                probs(m, i)
                            if n == slot(f"{m} PT {i}"):
                                probs_T(m, i)
                    if n == 8 * 10 + 14:
                        ssd_sq()

        @block.vector
        def _(v):
            v.memset(eps[:, :], EPS)
            v.memset(alrT[:, :], 1.0).then_inc(setup["dve"], 1)
            v.wait_ge(consts_in, 16)
            v.wait_ge(small_in, N_SMALL)
            v.tensor_copy(lmask[:, :, :].rearrange("p a b -> p (a b)"), A(1024, 1024).bitcast(I32))
            v.tensor_copy(posf[:, :], posi[:, :]).then_inc(setup["dve"], 1)
            v.wait_ge(setup["dve"], 2)
            ang, kk = A(0, 256, "p (a t d) -> p a t d", a=2, t=2, d=64), A(256, 256, "p (a t d) -> p a t d", a=2, t=2, d=64)
            for a in range(2):
                for t in range(T):
                    last = v.tensor_scalar(ang[:, a, t], cst[:, C_FR:C_FR + 64], posf[:, t:t + 1], None, ALU.mult)
            last.then_inc(setup["dve"], 1)
            v.wait_ge(setup["dve"], 3)
            af, kf = A(0, 256), A(256, 256)
            ch = [3]

            def link(ins):
                ch[0] += 1
                ins.then_inc(setup_chain, 1)
                v.wait_ge(setup_chain, ch[0] - 3)
            two_pi = 2 * np.pi
            c1 = 6.28125
            c2 = float(np.float32(np.round((two_pi - c1) * 2 ** 20) / 2 ** 20))
            c3 = float(two_pi - c1 - c2)
            magic = 1.5 * 2.0 ** 23
            link(v.tensor_scalar(kf[:, 0:128], af[:, 0:128], 1 / two_pi, None, ALU.mult))
            link(v.tensor_scalar(kf[:, 128:256], af[:, 128:256], 1 / two_pi, 0.25, ALU.mult, ALU.add))
            link(v.tensor_scalar(kf, kf, magic, None, ALU.add))
            link(v.tensor_scalar(kf, kf, magic, None, ALU.subtract))
            for c in (c1, c2, c3):
                link(v.scalar_tensor_tensor(af, kf, -c, af, ALU.mult, ALU.add))
            link(v.tensor_scalar(af[:, 128:256], af[:, 128:256], float(np.pi / 2), None, ALU.add))
            v.tensor_scalar(sc[:, :, :, :].rearrange("p a t d -> p (a t d)"), af, float(np.float32(3.1415925)), -float(np.float32(3.1415925)), ALU.min, ALU.max).then_inc(setup["dve"], 1)
            v.wait_ge(setup["pe"], 1)
            v.tensor_copy(allp[:, :], pair[:, 1, 1, 0:56 * DEPTH]).then_inc(setup["dve"], 1)
            v.sem_inc(split_done, RAW)
            v.wait_ge(setup["act"], 1)
            v.wait_ge(setup["dve"], 5)
            v.wait_ge(x_in, 16)
            v.sem_inc(layer_ready, 1)
            with v.Fori(0, DEPTH) as l:
                pe, act, me = reached("pe", l), reached("act", l), reached("dve", l)
                TT, TS, STT = v.tensor_tensor, v.tensor_scalar, v.scalar_tensor_tensor
                sig = lambda name: signal("dve", name)
                v.memset(xc[:, :, 0:3], 0.0).then_inc(*sig("pad"))
                v.tensor_copy(prm[:, :], allp[:, bass.ds(l * 56, 56)]).then_inc(*sig("prm"))

                def lo(n):
                    w = BLOCKS[n // UPB][2]
                    v.wait_ge(hi_done, l * UNITS + n + 1)
                    TT(w_lo[:, n % SPLIT, :, 0:w], raw[:, n % RAW, :, 0:w], w_hi[:, n % SPLIT, :, 0:w].bitcast(F32), ALU.subtract).then_inc(split_done, 1)

                def xT(j):
                    v.wait_ge(*pe(f"xT {j}"))
                    if j == 0:
                        v.wait_ge(*me("prm"))
                    else:
                        v.wait_ge(*act(f"xT {j - 1}"))
                        v.wait_ge(*me(f"xT {j - 1}"))
                    g = prm[:, 4 * j:4 * j + 4].unsqueeze(2).to_broadcast([P, 4, S])
                    TT(h_full, pair_of(f"xT {j}").rearrange("p b (k s) -> p (b k) s", k=2), g, ALU.mult).then_inc(*sig(f"xg {j}"))
                    v.wait_ge(*act(f"xT {j}"))
                    TT(a_lo[:, 4 * j:4 * j + 4, :], h_full, a_hi[:, 4 * j:4 * j + 4, :].bitcast(F32), ALU.subtract).then_inc(*sig(f"xT {j}"))

                def yT(j):
                    v.wait_ge(*act(f"yT {j}"))
                    TT(a_lo[:, 4 * j:4 * j + 4, :], pair_of(f"yT {j}").rearrange("p b (k s) -> p (b k) s", k=2), a_hi[:, 4 * j:4 * j + 4, :].bitcast(F32), ALU.subtract).then_inc(*sig(f"yT {j}"))

                def x_update(b):
                    c = OUT_BLOCK[b]
                    v.wait_ge(unit_used, l * UNITS + (b + 1) * UPB + SPLIT)
                    last = TT(x[:, :, c * WB:(c + 1) * WB], x[:, :, c * WB:(c + 1) * WB], acc_ps[:, b % 2, :, :], ALU.add)
                    last.then_inc(*sig(f"x {c}"))
                    if c == D // WB - 1:
                        v.wait_ge(*me(f"x {c}"))
                        v.sem_inc(layer_ready, 1)

                def gated(g):
                    b = [k for k in GATE_BLOCK if GATE_BLOCK[k] == g][0]
                    v.wait_ge(*act(f"evac {b}"))
                    v.wait_ge(*me({GA: "gla o", GB: "ssd y 1", GC: "mla O 1", GD: "dil O 1"}[g]))
                    TT(o[:, g], o[:, g], gate, ALU.mult).then_inc(*sig(f"gated {g}" if g == GB else f"y {g}"))

                def gla_la():
                    v.wait_ge(*act("gla ln"))
                    STT(la, two(pair_of("gla z")[:, 0, :], 2), 0.0, lt, ALU.min, ALU.subtract).then_inc(*sig("gla la"))

                def gla_D(n):
                    B = P >> n
                    g = GT.rearrange("p a s -> p (a s)").rearrange("p (n s) -> p n s", s=2 * B)
                    ref = g[:, :, B - 1:B].to_broadcast([P, S // B, 2 * B])
                    if n == 0:
                        v.wait_ge(*act("gla G"))
                    if n >= 2:
                        v.wait_ge(*me(f"gla W {n - 2}"))
                    TT(Dl[n % 2].rearrange("p (n s) -> p n s", s=2 * B), g, ref, ALU.subtract).then_inc(*sig(f"gla D {n}"))

                def gla_W(n):
                    B = P >> n
                    h = lambda t: t.rearrange("p (n s) -> p n s", s=2 * B)
                    W, E = h(Wl[n % 2]), h(Dl[n % 2])
                    k, q = h(kT.rearrange("p a s -> p (a s)")), h(qT.rearrange("p a s -> p (a s)"))
                    v.wait_ge(*act(f"gla E {n}"))
                    if n >= 2:
                        v.wait_ge(*pe(f"gla level {n - 2}"))
                    TT(W[:, :, 0:B], k[:, :, 0:B], E[:, :, 0:B], ALU.mult)
                    TT(W[:, :, B:], q[:, :, B:], E[:, :, B:], ALU.mult).then_inc(*sig(f"gla W {n}"))

                acc8 = acc.rearrange("p r t a q -> p (r t a) q")

                def gla_merge(n):
                    if n == 0:
                        v.wait_ge(*pe("gla level 0"))
                        v.memset(acc8, 0.0).then_inc(*sig("gla zero"))
                        v.tensor_copy(cross.rearrange("p r a q -> p r (a q)"), pair_of("gla level 0")[:, :, 0:256]).then_inc(*sig("gla cross"))
                        v.wait_ge(*me("gla cross"))
                        v.nop().then_inc(*sig("gla merge 0"))
                        return
                    name = f"gla level {n}" if n < 8 else "gla diag"
                    i = n if n < 8 else 0
                    v.wait_ge(*pe(name))
                    v.wait_ge(*me(f"gla merge {n - 1}"))
                    v.memset(st[:, 159:160], 0.0)
                    ps = pair_of(name).rearrange("p r (c q) -> p (r c) q", c=4)
                    v.copy_predicated(acc8, lmask[:, i].unsqueeze(1).to_broadcast([P, 8, P]), ps).then_inc(*sig(f"gla merge {n}" if n < 8 else "gla diag"))

                def gla_norm():
                    v.wait_ge(*act("gla sq"))
                    v.tensor_reduce(gss, A(512, 1024, "p (g c) -> p g c", g=8), AX.X, ALU.add).then_inc(*sig("gla ss"))
                    v.wait_ge(*act("gla rs"))
                    ps = pair_of("gla out").rearrange("p t (h c) -> p (t h) c", h=4)
                    oa = o[:, GA].rearrange("p t (h c) -> p (t h) c", h=4)
                    TT(oa, ps, grs.unsqueeze(2).to_broadcast([P, 8, P]), ALU.mult).then_inc(*sig("gla o0"))
                    v.wait_ge(*me("gla o0"))
                    TT(oa, oa, bc["gla_ng"].unsqueeze(1).to_broadcast([P, 8, P]), ALU.mult).then_inc(*sig("gla o"))

                def ssd_dt0():
                    v.wait_ge(*act("evac 4"))
                    v.wait_ge(params_in, (l + 1) * 16 * N_PARAMS)
                    TT(two(dtv, 2), u[:, :, COL["dt"]:COL["dt"] + 8], bc["dtb"].unsqueeze(1).to_broadcast([P, 2, 8]), ALU.add).then_inc(*sig("ssd dt0"))
                    v.wait_ge(*act("ssd ln"))
                    STT(dts, dtv, 0.0, dta, ALU.max, ALU.add).then_inc(*sig("ssd dt"))
                    v.wait_ge(*me("ssd dt"))
                    STT(two(las, 2), two(dts, 2), -1.0, eA.unsqueeze(1).to_broadcast([P, 2, 8]), ALU.mult, ALU.mult).then_inc(*sig("ssd la"))

                def ssd_conv():
                    v.wait_ge(*act("ssd xT 1"))
                    v.wait_ge(*me("pad"))
                    for f in range(8):
                        TS(conv(f), xc[:, f, 3:3 + S], prm[:, 16 + 24 + f:16 + 25 + f], prm[:, 48 + f:49 + f], ALU.mult, ALU.add).then_inc(*sig(f"conv 3 {f}"))
                    for j in (2, 1, 0):
                        for f in range(8):
                            if f == 0:
                                v.wait_ge(*me("conv 3 7" if j == 2 else f"conv {j + 1}"))
                            last = STT(conv(f), xc[:, f, j:j + S], prm[:, 16 + 8 * j + f:17 + 8 * j + f], conv(f), ALU.mult, ALU.add)
                        last.then_inc(*sig(f"conv {j}"))
                    v.wait_ge(*me("conv 0"))
                    v.nop().then_inc(*sig("ssd conv"))

                def ssd_xs():
                    v.wait_ge(*pe("ssd xs"))
                    ps = pair_of("ssd xs").rearrange("p t (h c) -> p t h c", h=8)
                    ob = o[:, GB].rearrange("p t (h c) -> p t h c", h=8)
                    TT(ob, ps, bc["D"].unsqueeze(1).unsqueeze(3).to_broadcast([P, T, 8, 64]), ALU.mult).then_inc(*sig("ssd xD"))
                    TT(xdt.rearrange("p t (h c) -> p (t h) c", h=8), ps.rearrange("p t h c -> p (t h) c"), dts.unsqueeze(2).to_broadcast([P, 16, 64]), ALU.mult).then_inc(*sig("ssd xdt"))

                def ssd_CB():
                    v.wait_ge(*pe("ssd CB"))
                    mk = cst[:, C_TRI:C_TRI + 384].unsqueeze(1).to_broadcast([P, 2, 384])
                    TT(CBm, pair_of("ssd CB")[:, :, 0:384], mk, ALU.mult).then_inc(*sig("ssd CB"))

                def ssd_E(g):
                    v.wait_ge(*pe(f"ssd bcast {g}"))
                    v.wait_ge(*act("ssd gcol"))
                    if g == 1:
                        v.wait_ge(*pe("ssd Y 0"))
                    ps = pair_of(f"ssd bcast {g}").rearrange("p b (h s) -> p (b h) s", h=2)
                    for h in range(4):
                        hh = 4 * g + h
                        TS(M[:, h, 0:S], ps[:, h, :], gcol[:, hh:hh + 1], 0.0, ALU.subtract, ALU.min)
                        last = TS(M[:, h, S:S + P], ps[:, h, P:S], gcol[:, 8 + hh:9 + hh], 0.0, ALU.subtract, ALU.min)
                    last.then_inc(*sig(f"ssd E {g}"))
                    v.wait_ge(*act(f"ssd exp {g}"))
                    v.wait_ge(*me("ssd CB"))
                    TT(M[:, :, :], M[:, :, :], CBm[:, g, :].unsqueeze(1).to_broadcast([P, 4, 384]), ALU.mult).then_inc(*sig(f"ssd M {g}"))

                def ssd_y(g):
                    v.wait_ge(*pe(f"ssd Y {g}"))
                    ob = o[:, GB, :, g * 256:(g + 1) * 256]
                    TT(ob, ob, pair_of(f"ssd Y {g}")[:, :, 0:256], ALU.add).then_inc(*sig(f"ssd y {g}"))

                def ssd_norm():
                    v.wait_ge(*act("ssd sq"))
                    v.tensor_reduce(two(bss, 2), bsq.rearrange("p t (g c) -> p t g c", g=2), AX.X, ALU.add).then_inc(*sig("ssd ss"))
                    v.wait_ge(*act("ssd rs"))
                    ob = o[:, GB].rearrange("p t (g c) -> p (t g) c", g=2)
                    TT(ob, ob, brs.unsqueeze(2).to_broadcast([P, 4, 256]), ALU.mult).then_inc(*sig("ssd n"))
                    v.wait_ge(*me("ssd n"))
                    TT(o[:, GB], o[:, GB], bc["ssd_ng"].unsqueeze(1).to_broadcast([P, 2, 512]), ALU.mult).then_inc(*sig(f"y {GB}"))

                def mla_cn():
                    v.wait_ge(*act("mla crs"))
                    for t in range(T):
                        a, b = (u[:, t, COL[k]:COL[k] + n] for k, n in (("cq", MLA_QL), ("ckv", MLA_KVL)))
                        STT(a, a, crs[:, t:t + 1], bc["q_ng"], ALU.mult, ALU.mult)
                        last = STT(b, b, crs[:, 2 + t:3 + t], bc["kv_ng"], ALU.mult, ALU.mult)
                    last.then_inc(*sig("mla cn"))

                def norm_heads(m, buf, sq, hd, g0, g1):
                    v.wait_ge(*act(f"{m} sq"))
                    for t in range(T):
                        last = v.tensor_reduce(mss[:, 8 * t:8 * t + 8], sq[:, t], AX.X, ALU.add)
                    last.then_inc(*sig(f"{m} ss"))
                    v.wait_ge(*act(f"{m} rs"))
                    TT(buf, buf, two(mrs, 2).unsqueeze(3).to_broadcast([P, T, 8, hd]), ALU.mult).then_inc(*sig(f"{m} n"))
                    v.wait_ge(*me(f"{m} n"))
                    for t in range(T):
                        TT(buf[:, t, 0:4], buf[:, t, 0:4], g0.unsqueeze(1).to_broadcast([P, 4, hd]), ALU.mult)
                        last = TT(buf[:, t, 4:8], buf[:, t, 4:8], g1.unsqueeze(1).to_broadcast([P, 4, hd]), ALU.mult)
                    last.then_inc(*sig(f"{m} g"))
                    v.wait_ge(*me(f"{m} g"))

                def rope(name, x1, x2, y1, y2, tmp, nh, hd, step):
                    s, c = (sc[:, a, :, 0:64:step].unsqueeze(2).to_broadcast([P, T, nh, hd]) for a in range(2))
                    TT(tmp[0], x1, c, ALU.mult)
                    TT(tmp[1], x2, s, ALU.mult)
                    TT(tmp[2], x2, c, ALU.mult)
                    TT(tmp[3], x1, s, ALU.mult).then_inc(*sig(name + " tmp"))
                    v.wait_ge(*me(name + " tmp"))
                    TT(y1, tmp[0], tmp[1], ALU.subtract)
                    TT(y2, tmp[2], tmp[3], ALU.add).then_inc(*sig(name))

                def mla_norm():
                    norm_heads("mla", mqk, msq, MLA_QK, bc["q_hg"], bc["k_hg"])
                    rope("mla rope", mqk[:, :, :, P:P + 32], mqk[:, :, :, P + 32:P + 64], mrr[:, :, :, 0:32], mrr[:, :, :, 32:64], mtmp, 8, 32, 2)

                def dil_norm():
                    norm_heads("dil", dqk, dsq, DIL_HD, bc["dq_g"], bc["dk_g"])
                    for i in range(2):
                        b = dqk[:, :, 4 * i:4 * i + 4]
                        if i:
                            v.wait_ge(*me("dil rope 0"))
                        rope(f"dil rope {i}", b[:, :, :, 0:64], b[:, :, :, 64:128], b[:, :, :, 0:64], b[:, :, :, 64:128], dtmp, 4, 64, 1)

                def smax(m, i):
                    v.wait_ge(*pe(f"{m} S {i}"))
                    if i:
                        v.wait_ge(*pe(f"{m} PT {i - 1}"))
                    ps = pair_of(f"{m} S {i}")
                    mk = cmask if m == "mla" else dadd
                    v.memset(st[:, 159:160], 0.0)
                    for r in range(2):
                        for t, (c0, c1) in enumerate(((0, P), (P, P + S))):
                            j = 2 * r + t
                            last = v.tensor_tensor_reduce(out=Pb[:, r, c0:c1], in0=ps[:, r, c0:c1], in1=mk[:, 2 * P - (c1 - c0):], scale=1.0,
                                                          scalar=-3e38, op0=ALU.add, op1=ALU.max, accum_out=mx[:, j:j + 1])
                    last.then_inc(*sig(f"{m} max {i}"))
                    v.wait_ge(*me(f"{m} max {i}"))
                    TS(nm, mx, -SC[m], None, ALU.mult).then_inc(*sig(f"{m} nmax {i}"))

                def taps(i):
                    v.wait_ge(*act(f"dil P {i}"))
                    for r in range(2):
                        for t, (c0, c1) in enumerate(((0, P), (P, P + S))):
                            j = 2 * r + t
                            last = v.tensor_tensor_reduce(out=Pb[:, r, c0:c1], in0=Pb[:, r, c0:c1], in1=dmul[:, 2 * P - (c1 - c0):], scale=1.0,
                                                          scalar=0.0, op0=ALU.mult, op1=ALU.add, accum_out=sm[:, j:j + 1])
                    last.then_inc(*sig(f"dil P {i}"))

                def out_heads(m, i):
                    if m == "dil":
                        v.wait_ge(*me(f"dil P {i}"))
                    else:
                        v.wait_ge(*act(f"mla P {i}"))
                    if (m, i) != ("mla", 0):
                        v.wait_ge(*me(f"{m} O 0" if i else "mla O 1"))
                    v.reciprocal(ri, sm).then_inc(*sig(f"{m} ri {i}"))
                    v.wait_ge(*me(f"{m} ri {i}"))
                    v.wait_ge(*pe(f"{m} O {i}"))
                    ps = pair_of(f"{m} O {i}")
                    g = GC if m == "mla" else GD
                    for t in range(T):
                        for r in range(2):
                            h, j = 2 * i + r, 2 * r + t
                            last = TS(o[:, g, t, h * P:(h + 1) * P], ps[:, t, r * P:(r + 1) * P], ri[:, j:j + 1], None, ALU.mult)
                    last.then_inc(*sig(f"{m} O {i}"))

                for n in range(UNITS):
                    lo(n)
                    if n == 1:
                        xT(0)
                        xT(1)
                    if n == 3:
                        xT(2)
                    if n == 5:
                        xT(3)
                    if n == U_OUT + 3:
                        gated(GD)
                        yT(0)
                        yT(1)
                        yT(2)
                    if n == U_OUT + 5:
                        yT(3)
                    if n % UPB == 2 and n // UPB - 1 >= N_INB:
                        x_update(n // UPB - 1)
                    if n == slot("gla z"):
                        gla_la()
                    if n == slot("gla G"):
                        gla_D(0)
                        gla_D(1)
                        gla_W(0)
                    for i in range(1, 8):
                        if n == PE_AT[f"gla level {i - 1}"] + 1:
                            if i < 7:
                                gla_D(i + 1)
                            gla_W(i)
                    for i in range(8):
                        if n == PE_AT[f"gla level {i}"] + 3:
                            gla_merge(i)
                    if n == slot("gla diag"):
                        gla_merge(8)
                    if n == slot("gla out"):
                        gla_norm()
                    if n == slot("ssd xT 1", 1):
                        ssd_dt0()
                    if n == slot("ssd xT 1", 3):
                        ssd_conv()
                    if n == slot("ssd xs"):
                        ssd_xs()
                    if n == slot("ssd CB"):
                        ssd_CB()
                    for i in range(2):
                        if n == slot(f"ssd bcast {i}"):
                            ssd_E(i)
                        if n == slot(f"ssd Y {i}"):
                            ssd_y(i)
                    if n == slot("mla cT", -1):
                        mla_cn()
                    if n == slot("mla kv 1"):
                        mla_norm()
                    if n == slot("mla S 0", 1):
                        dil_norm()
                    for m in ("mla", "dil"):
                        for i in range(2):
                            if n == slot(f"{m} S {i}"):
                                smax(m, i)
                                if m == "dil":
                                    taps(i)
                            if n == slot(f"{m} O {i}"):
                                out_heads(m, i)
                    if n == 8 * 10 + 7:
                        gated(GB)
                    if n == 8 * 10 + 14:
                        ssd_norm()
                    if n == 8 * 11 + 7:
                        gated(GA)
                    if n == U_OUT - 1:
                        gated(GC)
                x_update(len(BLOCKS) - 1)


_INS = ["x", "positions", "ln_g", "w_in", "w_out", "gla_gate_w2", "gla_gate_b", "gla_norm_g", "ssd_conv_w", "ssd_conv_b",
        "ssd_dt_bias", "ssd_A_log", "ssd_D", "ssd_norm_g", "mla_q_norm_g", "mla_kv_norm_g", "mla_w_uq", "mla_w_ukv",
        "mla_q_head_g", "mla_k_head_g", "dil_q_g", "dil_k_g"]
_OUTS = [((1, S, D), "float32")]


def kernel(**inputs):
    import concourse.bacc as _bacc
    from concourse.bass_utils import run_bass_kernel_spmd as _run

    consts, masks = tables()
    given = {n: np.ascontiguousarray(inputs[n]) for n in _INS} | {"consts": consts, "masks": masks}
    for counting in (True, False):
        COUNTING[0] = counting
        if counting:
            for e in ORDER:
                ORDER[e].clear()
        nc = _bacc.Bacc("TRN2", target_bir_lowering=False, num_devices=1)
        arrays, args = {}, []
        for name, a in given.items():
            arrays[f"in_{name}_dram"] = a
            args.append(nc.dram_tensor(f"in_{name}_dram", a.shape, mybir.dt.from_np(a.dtype), kind="ExternalInput").ap())
        for i, (shape, dtype) in enumerate(_OUTS):
            args.append(nc.dram_tensor(f"out_{i}_dram", shape, mybir.dt.from_np(np.dtype(dtype)), kind="ExternalOutput").ap())
        build(nc, *args)
    r = _run(nc, [arrays], core_ids=[0])
    return r.results[0]["out_0_dram"]
```

```python
from contextlib import ExitStack

import numpy as np

import concourse.bass as bass
from concourse import mybir

ALU = mybir.AluOpType
ACT = mybir.ActivationFunctionType
AX = mybir.AxisListType
F32 = mybir.dt.float32
F32R = mybir.dt.float32r
U8 = mybir.dt.uint8
I32 = mybir.dt.int32

P = 128
S, D, DEPTH = 256, 2048, 2
T = S // P
KT = D // P
EPS = 1e-6
GLA_H, GLA_DK, GLA_DV, GLA_R, GLA_TAU = 4, 64, 128, 16, 16.0
SSD_DI, SSD_H, SSD_G, SSD_N, SSD_TAPS = 512, 8, 2, 128, 4
SSD_HD = SSD_DI // SSD_H
SSD_C = SSD_DI + 2 * SSD_G * SSD_N
MLA_H, MLA_NOPE, MLA_ROPE, MLA_V, MLA_QL, MLA_KVL = 4, 128, 64, 128, 384, 128
MLA_QK = MLA_NOPE + MLA_ROPE
DIL_H, DIL_HD = 4, 128
DIL_CONFIGS = ((128, 1), (512, 4), (2048, 16))
N_GATE = 2048
N_IN = 6232
GA, GB, GC, GD = range(4)

WIDTHS = (("aq", 256), ("ak", 256), ("av", 512), ("alr", GLA_R), ("xbc", SSD_C), ("dt", SSD_H), ("cq", MLA_QL),
          ("ckv", MLA_KVL), ("ckr", MLA_ROPE), ("dq", 512), ("dk", 512), ("dv", 512))
COL, _at = {}, 0
for _name, _w in WIDTHS:
    COL[_name] = _at
    _at += _w
N_U = _at
assert N_GATE + N_U == N_IN

WB = 512
NARROW = 278
BLOCKS = [("u", N_GATE + c, WB) for c in (0, 1024, 512, 1536, 2048, 2560)]
BLOCKS += [("u", N_GATE + 3072 + i * NARROW, NARROW) for i in range(4)]
assert 3072 + 4 * NARROW == N_U
GATE_ORDER = (GB, GA, GC, GD)
GATE_BLOCK = {}
for _g in GATE_ORDER:
    GATE_BLOCK[len(BLOCKS)] = _g
    BLOCKS.append(("gate", _g * WB, WB))
N_INB = len(BLOCKS)
OUT_BLOCK = {}
for _c in range(D // WB):
    OUT_BLOCK[len(BLOCKS)] = _c
    BLOCKS.append(("out", _c * WB, WB))
UK = 2
UPB = KT // UK
UNITS = len(BLOCKS) * UPB
U_OUT = N_INB * UPB
RAW, SPLIT = 4, 4
assert UNITS % RAW == 0 and UNITS % SPLIT == 0

LEVELS = (64, 32, 16, 8, 4, 2, 1)
NEG = -1e30

C_ID, C_TRI, C_ONE, C_TRI2 = 0, 128, 256, 384
C_CZ, C_CM = 512, 640
C_DA = 768
C_DM = 1024
C_FR = 1280
NC = C_FR + DIL_HD // 2


def tables():
    c = np.zeros((P, NC), np.float32)
    i = np.arange(P)
    c[:, C_ID:C_ID + P] = i[:, None] == i[None, :]
    c[:, C_TRI:C_TRI + P] = i[:, None] <= i[None, :]
    c[:, C_ONE:C_ONE + P] = 1
    c[:, C_TRI2:C_TRI2 + P] = i[:, None] <= i[None, :]
    c[:, C_CM:C_CM + P] = np.where(i[None, :] <= i[:, None], 0, NEG)
    far = (P + i[:, None]) - np.arange(2 * P)[None, :]
    taps = sum(((far >= 0) & (far <= w) & (far % d == 0)).astype(np.float32) for w, d in DIL_CONFIGS)
    c[:, C_DA:C_DA + 2 * P] = np.where(taps > 0, 0, NEG)
    c[:, C_DM:C_DM + 2 * P] = taps
    half = DIL_HD // 2
    c[:, C_FR:] = np.exp(np.float32(-np.log(10000.0)) * np.arange(half, dtype=np.float32) * np.float32(2.0 / DIL_HD))
    m = np.zeros((P, 1 + len(LEVELS), P), np.int32)
    m[:, 0] = i[:, None] == i[None, :]
    for n, b in enumerate(LEVELS):
        key, query = i[:, None], i[None, :]
        m[:, 1 + n] = (key // (2 * b) == query // (2 * b)) & (key % (2 * b) < b) & (query % (2 * b) >= b)
    return c, m.reshape(P, -1)


PE_AT = {"gla qk": 10, "gla lr": 19, "gla z": 21, "gla G": 23}
for _n in range(8):
    PE_AT[f"gla level {_n}"] = 26 + 2 * _n
PE_AT |= {"gla diag": 42, "ssd xT 0": 43, "ssd xT 1": 44, "gla out": 45, "ssd cum": 50, "ssd CB": 56, "ssd bcast 0": 58,
          "ssd xs": 62, "mla cT": 64, "ssd bcast 1": 66, "mla q 0": 67, "mla q 1": 68, "ssd Y 0": 70, "mla kv 0": 71,
          "mla kv 1": 73, "ssd Y 1": 76, "mla qT": 85, "mla kT": 86, "mla rT": 87, "mla S 0": 89, "mla PT 0": 92,
          "mla S 1": 93, "mla O 0": 94, "dil qT": 95, "mla PT 1": 96, "dil kT": 97, "mla O 1": 98, "dil S 0": 99,
          "dil PT 0": 102, "dil S 1": 103, "dil O 0": 104, "dil PT 1": 106, "yT 0": 107, "dil O 1": 108, "yT 1": 109,
          "yT 2": 110, "yT 3": 114}
LAST_READER = {"gla qk": ("act", "gla k"), "gla lr": ("act", "gla lr"), "gla z": ("dve", "gla la"), "gla G": ("act", "gla G"),
               "gla level 0": ("act", "gla cross"), "gla diag": ("dve", "gla diag"), "gla out": ("dve", "gla o"),
               "ssd xT 0": ("act", "ssd xT 0"), "ssd xT 1": ("act", "ssd xT 1"), "ssd xs": ("dve", "ssd xdt"),
               "ssd cum": ("act", "ssd gcol"), "ssd CB": ("dve", "ssd CB"), "ssd bcast 0": ("dve", "ssd E 0"),
               "ssd bcast 1": ("dve", "ssd E 1"), "ssd Y 0": ("dve", "ssd y 0"), "ssd Y 1": ("dve", "ssd y 1"),
               "mla cT": ("act", "mla cT"), "mla qT": ("act", "mla qT"), "mla kT": ("act", "mla kT"), "mla rT": ("act", "mla rT"),
               "dil qT": ("act", "dil qT"), "dil kT": ("act", "dil kT")}
LAST_READER |= {f"gla level {n}": ("dve", f"gla merge {n}") for n in range(1, 8)}
LAST_READER |= {f"mla {w} {t}": ("act", f"mla {w} {t}") for w in ("q", "kv") for t in range(2)}
for _m in ("mla", "dil"):
    for _i in range(2):
        LAST_READER |= {f"{_m} S {_i}": ("dve", f"{_m} max {_i}"), f"{_m} PT {_i}": ("act", f"{_m} PT {_i}"),
                        f"{_m} O {_i}": ("dve", f"{_m} O {_i}")}
LAST_READER |= {f"yT {_j}": ("dve", f"yT {_j}") for _j in range(4)}
JOBS = list(PE_AT)
X_NEXT = {UNITS - 6: 0, UNITS - 4: 1}
EVAC_AT = {(b + 1) * UPB + 2: b for b in range(N_INB)}

ORDER = {"pe": [], "act": [], "dve": [], "pool": []}
COUNTING = [True]


def build(nc, x_d, pos_d, ln_g, w_in, w_out, gla_w2, gla_b, gla_ng, conv_w, conv_b, dt_bias, A_log, D_d, ssd_ng,
          q_ng, kv_ng, w_uq, w_ukv, q_hg, k_hg, dq_g, dk_g, consts_d, masks_d, out_d):
    ctx = ExitStack()
    with ctx:
        def sb(name, shape, dt=F32):
            return ctx.enter_context(nc.sbuf_tensor(name, shape, dt))

        def sem(name):
            return ctx.enter_context(nc.semaphore(name))

        x = sb("x", [P, T, D])
        raw = sb("raw", [P, RAW, UK, WB])
        w_hi = sb("w_hi", [P, SPLIT, UK, WB], F32R)
        w_lo = sb("w_lo", [P, SPLIT, UK, WB], F32R)
        a_hi = sb("a_hi", [P, KT, S], F32R)
        a_lo = sb("a_lo", [P, KT, S], F32R)
        u = sb("u", [P, T, N_U])
        o = sb("o", [P, 4, T, WB])
        cst = sb("cst", [P, NC])
        lmask = sb("lmask", [P, 1 + len(LEVELS), P], U8)
        angle = sb("angle", [P, 2 * T * DIL_HD // 2])
        sc = sb("sincos", [P, 2, T, DIL_HD // 2])
        allp = sb("allp", [P, (DEPTH + 1) * 56])
        lng = sb("lng", [P, KT])
        prm = sb("prm", [P, 56])
        prow = sb("prow", [P, P])
        posi = sb("posi", [P, T], I32)
        posf = sb("posf", [P, T])
        NB = {"gla_ng": 128, "ssd_ng": 512, "q_ng": 384, "kv_ng": 128, "q_hg": 192, "k_hg": 192, "dq_g": 128, "dk_g": 128,
              "dtb": 8, "alog": 8, "D": 8}
        bc, at = {}, 0
        bcp = sb("bcp", [P, sum(NB.values())])
        for k, n in NB.items():
            bc[k] = bcp[:, at:at + n]
            at += n
        wuq = sb("wuq", [P, MLA_QL // P, MLA_H * MLA_QK])
        wukv = sb("wukv", [P, MLA_H * (MLA_NOPE + MLA_V)])
        w2 = sb("w2", [GLA_R + 1, 256])
        alrT = sb("alrT", [GLA_R + 1, S])
        powers = sb("powers", [P, 32])
        eps, minus_half = powers[:, 0:16], powers[:, 16:32]
        st = sb("st", [P, 161])
        sth = sb("sth", [P, 64])
        ar = sb("arena", [P, 7704])

        ident = cst[:, C_ID:C_ID + P]
        tri = cst[:, C_TRI:C_TRI + P]
        ones = cst[:, C_ONE:C_ONE + P]
        tri_ones = cst[:, C_TRI:C_TRI + 2 * P]
        cmask = cst[:, C_CZ:C_CZ + 2 * P]
        dadd = cst[:, C_DA:C_DA + 2 * P]
        dmul = cst[:, C_DM:C_DM + 2 * P]

        def A(start, size, pat=None, **k):
            v = ar[:, start:start + size]
            return v.rearrange(pat, **k) if pat else v

        def two(v, n):
            return v.rearrange("p (a b) -> p a b", a=n)

        h_full = two(A(0, 1024), 4)
        qT = o[:, 2, 0, :].rearrange("p (a s) -> p a s", a=2)
        kT = o[:, 2, 1, :].rearrange("p (a s) -> p a s", a=2)
        acc = o[:, 3].rearrange("p r (t a q) -> p r t a q", t=T, a=2)
        GT = two(A(0, 512), 2)
        Dl = [A(512, 512), A(1024, 512)]
        Wl = [A(1536, 512), A(2048, 512)]
        Ql = [A(6168 + 512 * i, 512, "p (r t a s) -> p r t a s", r=2, t=T, a=2) for i in range(2)]
        cross = A(2560, 512, "p (r a q) -> p r a q", r=2, a=2)
        la = two(A(3072, 512), 2)
        lt = two(A(3584, 512), 2)
        xc = two(A(4096, 8 * (S + 3)), 8)
        xdt = two(A(4096, 1024), 2)
        CBm = two(A(256, 768), 2)
        M = [two(A(a, 1536), 4) for a in (6168, 1536)]
        Grow = A(0, 256)

        def conv(f):
            return u[:, f // 4, COL["xbc"] + (f % 4) * S:COL["xbc"] + (f % 4 + 1) * S]
        conv4 = [u[:, t, COL["xbc"]:COL["xbc"] + 4 * S] for t in range(2)]
        bsq = u[:, :, COL["cq"]:COL["cq"] + SSD_DI]
        mqk = u[:, :, 0:8 * MLA_QK].rearrange("p t (h d) -> p t h d", h=8)
        mv = u[:, :, 1536:2048]
        msq = A(6168, 1536, "p (t h d) -> p t h d", t=T, h=4)
        mtmp = [A(i * 512, 512, "p (t h d) -> p t h d", t=T, h=8) for i in range(4)]
        mqT, mkT = two(A(0, 1024), 4), two(A(1024, 1024), 4)
        mrT = A(2048, 1024, "p (a b s) -> p a b s", a=2, b=2)
        mrr = A(2048, 1024, "p (t h d) -> p t h d", t=T, h=8)
        Pb, PT = two(A(4096, 768), 2), two(A(4864, 768), 2)
        cT = two(A(3072, 1024), 4)
        gate = two(A(3072, 1024), 2)
        dqk = u[:, :, COL["dq"]:COL["dq"] + 1024].rearrange("p t (h d) -> p t h d", h=8)
        dv = u[:, :, COL["dv"]:COL["dv"] + 512]
        dsq = A(5632, 1024, "p (t h d) -> p t h d", t=T, h=4)
        dtmp = [A(5632 + i * 512, 512, "p (t h d) -> p t h d", t=T, h=4) for i in range(4)]
        dqT, dkT = two(A(5632, 1024), 4), two(A(6656, 1024), 4)

        def stat(a, n):
            return st[:, a:a + n]
        xss, xrs = stat(0, 2), stat(2, 2)
        gss, grs = stat(4, 8), stat(12, 8)
        dtv, dta, las, gcol, eA, dts = stat(20, 16), stat(36, 16), stat(52, 16), stat(68, 16), stat(84, 8), stat(92, 16)
        bss, brs = stat(108, 4), stat(112, 4)
        css, crs = stat(116, 4), stat(120, 4)
        mx, nm, sm, ri = stat(124, 4), stat(128, 4), (stat(132, 4), stat(140, 4)), stat(136, 4)
        nv = stat(144, 16)
        mss, mrs, dss, drs = (sth[:, 16 * i:16 * i + 16] for i in range(4))

        acc_ps = ctx.enter_context(nc.psum_tensor("gemm", [P, 2, T, WB], F32))
        pair = ctx.enter_context(nc.psum_tensor("pairs", [P, 2, 2, 512], F32))

        ident_in, rows_in, small_in, params_in, out_written = (sem(k) for k in ("ident_in", "rows_in", "small_in", "params_in", "out_written"))
        x_in = [sem(f"x_in_{c}") for c in range(D // WB)]
        paced, setup_chain = sem("paced"), sem("setup_chain")
        x_updated = sem("x_updated")
        x_turned, x_gained, x_hi, x_lo = sem("x_turned"), sem("x_gained"), sem("x_hi"), sem("x_lo")
        weights_in = [sem(f"weights_in_{i}") for i in range(RAW)]
        hi_done, split_done, unit_used, block_done = sem("hi_done"), sem("split_done"), sem("unit_used"), sem("block_done")
        stage = {e: sem(f"{e}_stages") for e in ORDER}
        setup = {e: sem(f"{e}_setup") for e in ORDER}
        seen = {e: [] for e in ORDER}

        def signal(e, name):
            if COUNTING[0]:
                ORDER[e].append(name)
            else:
                assert ORDER[e][len(seen[e])] == name, (e, name, ORDER[e][len(seen[e])])
            seen[e].append(name)
            return stage[e], 1

        def reached(e, l):
            def f(name):
                n = ORDER[e].index(name) if name in ORDER[e] else 0
                if not COUNTING[0]:
                    assert name in ORDER[e], name
                return stage[e], l * len(ORDER[e]) + n + 1
            return f

        block = ctx.enter_context(nc.Block())

        def weights(l, b, k0):
            kind, c0, w = BLOCKS[b]
            m = w_out if kind == "out" else w_in
            return m[l].rearrange("(k p) n -> p k n", p=P)[:, k0:k0 + UK, c0:c0 + w]

        def x_load(engine, c):
            engine.dma_start(x[:, :, c * WB:(c + 1) * WB],
                             x_d.rearrange("o (t p) n -> p (o t) n", p=P)[:, :, c * WB:(c + 1) * WB]).then_inc(x_in[c], 16)

        N_PARAMS = len(NB) + 4

        @block.sync
        def _(sp):
            sp.dma_start(cst[:, 0:P], consts_d[:, 0:P]).then_inc(ident_in, 16)
            for c in (0, 1):
                x_load(sp, c)
            with sp.Fori(0, DEPTH) as l:
                for n in range(UNITS):
                    b, k0 = n // UPB, n % UPB * UK
                    sp.wait_ge(split_done, l * UNITS + n + 1)
                    if k0 == 0 and BLOCKS[b][1] == 0:
                        sp.sem_inc(paced, 1)
                    sp.dma_start(raw[:, n % RAW, :, 0:BLOCKS[b][2]], weights(l, b, k0)).then_inc(weights_in[n % RAW], 16)
            for c in range(D // WB):
                sp.wait_ge(x_updated, 4 * DEPTH + c + 1)
                sp.dma_start(out_d.rearrange("o (t p) n -> p (o t) n", p=P)[:, :, c * WB:(c + 1) * WB],
                             x[:, :, c * WB:(c + 1) * WB]).then_inc(out_written, 16)
            sp.wait_ge(out_written, 16 * (D // WB))

        @block.gpsimd
        def _(pool):
            pool.dma_start(posi[:, :], pos_d.rearrange("o (t p) -> p (o t)", p=P), allow_slow_non_contiguous=True).then_inc(small_in, 16)
            pool.wait_ge(x_in[1], 16)
            pool.dma_start(cst[:, P:], consts_d[:, P:]).then_inc(small_in, 16)
            pool.dma_start(A(1024, 1024).bitcast(I32), masks_d).then_inc(small_in, 16)
            for c in (2, 3):
                pool.wait_ge(x_in[c], 16)
                pool.sem_inc(x_updated, 3 if c == 2 else 1)
            pool.memset(eps, EPS)
            pool.memset(minus_half, -0.5)
            pool.wait_ge(small_in, 16 * 3)
            pool.tensor_copy(lmask[:, :, :].rearrange("p a b -> p (a b)"), A(1024, 1024).bitcast(I32))
            steps = [0]

            def link(ins):
                steps[0] += 1
                ins.then_inc(setup_chain, 1)
                pool.wait_ge(setup_chain, steps[0])
            two_pi = 2 * np.pi
            c1 = 6.28125
            c2 = float(np.float32(np.round((two_pi - c1) * 2 ** 20) / 2 ** 20))
            c3 = float(two_pi - c1 - c2)
            magic = 1.5 * 2.0 ** 23
            af, kf = angle[:, :], A(2048, 256)
            tf = A(2304, 256)
            link(pool.tensor_copy(posf[:, :], posi[:, :]))
            for a in range(2):
                for t in range(T):
                    link(pool.tensor_scalar(af[:, (2 * a + t) * 64:(2 * a + t + 1) * 64], cst[:, C_FR:C_FR + 64], posf[:, t:t + 1], None, ALU.mult))
            link(pool.tensor_scalar(kf[:, 0:128], af[:, 0:128], 1 / two_pi, 0.0, ALU.mult, ALU.add))
            link(pool.tensor_scalar(kf[:, 128:256], af[:, 128:256], 1 / two_pi, 0.25, ALU.mult, ALU.add))
            link(pool.tensor_scalar(kf, kf, magic, None, ALU.add))
            link(pool.tensor_scalar(kf, kf, magic, None, ALU.subtract))
            for c in (c1, c2, c3):
                link(pool.tensor_scalar(tf, kf, c, None, ALU.mult))
                link(pool.tensor_tensor(af, af, tf, ALU.subtract))
            link(pool.tensor_scalar(af[:, 128:256], af[:, 128:256], float(np.pi / 2), None, ALU.add))
            top = float(np.float32(3.1415925))
            pool.tensor_scalar(af, af, top, -top, ALU.min, ALU.max).then_inc(setup["pool"], 1)
            with pool.Fori(0, DEPTH) as l:
                me, act = reached("pool", l), reached("act", l)
                for k, src in (("gla_ng", gla_ng), ("ssd_ng", ssd_ng), ("q_ng", q_ng), ("kv_ng", kv_ng), ("q_hg", q_hg),
                               ("k_hg", k_hg), ("dq_g", dq_g), ("dk_g", dk_g), ("dtb", dt_bias), ("alog", A_log), ("D", D_d)):
                    pool.dma_start(bc[k], src[l].partition_broadcast(P)).then_inc(params_in, 16)
                pool.dma_start(w2[0:GLA_R, :], gla_w2[l]).then_inc(params_in, 16)
                pool.dma_start(w2[GLA_R:GLA_R + 1, :], gla_b[l].unsqueeze(0)).then_inc(params_in, 16)
                pool.dma_start(wuq[:, :, :], w_uq[l].rearrange("(k p) n -> p k n", p=P)).then_inc(params_in, 16)
                pool.dma_start(wukv[:, :], w_ukv[l]).then_inc(params_in, 16)

                def rsqrt(name, dst, mean):
                    n = mean.shape[-1]
                    pool.wait_ge(*act(name + " sum"))
                    pool.tensor_tensor(nv[:, 0:n], mean, eps[:, 0:n], ALU.add).then_inc(*signal("pool", name + " mean"))
                    pool.wait_ge(*me(name + " mean"))
                    pool.tensor_tensor(dst, nv[:, 0:n], minus_half[:, 0:n], ALU.pow).then_inc(*signal("pool", name))
                    pool.wait_ge(*me(name))

                rsqrt("x rs", xrs, xss)
                rsqrt("gla rs", grs, gss)
                rsqrt("mla crs", crs, css)
                rsqrt("mla rs 0", mrs[:, 0:8], mss[:, 0:8])
                rsqrt("mla rs 1", mrs[:, 8:16], mss[:, 8:16])
                rsqrt("dil rs 0", drs[:, 0:8], dss[:, 0:8])
                rsqrt("dil rs 1", drs[:, 8:16], dss[:, 8:16])
                rsqrt("ssd rs", brs, bss)
                pool.wait_ge(*reached("dve", l)("yT 3"))

        @block.tensor
        def _(pe):
            pe.sem_inc(unit_used, SPLIT)
            pe.wait_ge(ident_in, 16)
            pe.wait_ge(rows_in, 16 * 3 * DEPTH)
            pe.transpose(acc_ps[:, 1, 1, 0:56 * DEPTH], prow[0:56 * DEPTH, :], ident[0:56 * DEPTH, 0:56 * DEPTH]).then_inc(setup["pe"], 1)

            def xT(j, l):
                if l is None:
                    l = 0
                    pe.wait_ge(x_in[j], 16)
                else:
                    pe.wait_ge(x_updated, 4 * l + j + 1)
                if j >= 2:
                    pe.wait_ge(x_lo, 4 * l + j - 1)
                ps = pair[:, j % 2]
                for kk in range(4):
                    for t in range(T):
                        f = (4 * j + kk) * P
                        last = pe.transpose(ps[:, kk // 2, (kk % 2) * S + t * P:(kk % 2) * S + (t + 1) * P], x[:, t, f:f + P], ident)
                last.then_inc(x_turned, 1)

            for j in range(2):
                xT(j, None)
            with pe.Fori(0, DEPTH) as l:
                me, act, dve = reached("pe", l), reached("act", l), reached("dve", l)

                def unit(n):
                    b, k0 = n // UPB, n % UPB * UK
                    w = BLOCKS[b][2]
                    if k0 == 0 and b >= 2:
                        if b - 2 in OUT_BLOCK:
                            pe.wait_ge(x_updated, 4 * (l + 1) + OUT_BLOCK[b - 2] + 1)
                        else:
                            pe.wait_ge(*act(f"evac {b - 2}"))
                    if n == UPB:
                        pe.wait_ge(x_updated, 4 * (l + 1))
                    pe.wait_ge(split_done, l * UNITS + n + 1 + RAW)
                    if n < UPB and n % 2 == 0:
                        pe.wait_ge(x_lo, 4 * l + n // 2 + 1)
                    if U_OUT <= n < U_OUT + UPB and n % 2 == 0:
                        pe.wait_ge(*dve(f"yT {(n - U_OUT) // 2}"))
                    for j in range(UK):
                        k = k0 + j
                        for t in range(T):
                            acc_t = acc_ps[:, b % 2, t, 0:w]
                            tok = slice(t * P, (t + 1) * P)
                            hi, lo = w_hi[:, n % SPLIT, j, 0:w], w_lo[:, n % SPLIT, j, 0:w]
                            pe.matmul(acc_t, a_hi[:, k, tok], hi, start=k == 0, stop=False)
                            pe.matmul(acc_t, a_hi[:, k, tok], lo, start=False, stop=False)
                            last = pe.matmul(acc_t, a_lo[:, k, tok], hi, start=False, stop=k == KT - 1)
                    last.then_inc(unit_used, 1)

                jobs, now = [0], [0]

                def bank():
                    jobs[0] += 1
                    n = jobs[0]
                    assert PE_AT[JOBS[n - 1]] == now[0]
                    if n >= 3:
                        e, done = LAST_READER[JOBS[n - 3]]
                        pe.wait_ge(*{"act": act, "dve": dve}[e](done))
                    else:
                        pe.wait_ge(x_lo, 4 * l + 2 + n)
                    return pair[:, n % 2]

                def yT(j):
                    pe.wait_ge(*dve(f"y {j}"))
                    ps = bank()
                    for kk in range(4):
                        for t in range(T):
                            f = kk * P
                            last = pe.transpose(ps[:, kk // 2, (kk % 2) * S + t * P:(kk % 2) * S + (t + 1) * P], o[:, j, t, f:f + P], ident)
                    last.then_inc(*signal("pe", f"yT {j}"))

                def gla_qk():
                    pe.wait_ge(*act("evac 0"))
                    ps = bank()
                    for a in range(2):
                        for p in range(2):
                            for t in range(T):
                                c = a * 256 + p * P
                                last = pe.transpose(ps[:, a, p * S + t * P:p * S + (t + 1) * P], u[:, t, c:c + P], ident)
                    last.then_inc(*signal("pe", "gla qk"))

                def gla_lr():
                    pe.wait_ge(*act("evac 1"))
                    ps = bank()
                    for t in range(T):
                        last = pe.transpose(ps[0:GLA_R, 0, t * P:(t + 1) * P], u[:, t, COL["alr"]:COL["alr"] + GLA_R], ident)
                    last.then_inc(*signal("pe", "gla lr"))

                def gla_z():
                    pe.wait_ge(*act("gla lr"))
                    pe.wait_ge(params_in, (l + 1) * 16 * N_PARAMS)
                    ps = bank()
                    for t in range(T):
                        last = pe.matmul(ps[:, 0, t * 256:(t + 1) * 256], alrT[:, t * P:(t + 1) * P], w2[:, :], start=True, stop=True)
                    last.then_inc(*signal("pe", "gla z"))

                def gla_G():
                    pe.wait_ge(*dve("gla la"))
                    ps = bank()
                    for p in range(2):
                        pe.matmul(ps[:, 0, p * S:(p + 1) * S], la[:, 0, p * P:(p + 1) * P], tri_ones, start=True, stop=False)
                        last = pe.matmul(ps[:, 0, p * S + P:(p + 1) * S], la[:, 1, p * P:(p + 1) * P], tri, start=False, stop=True)
                    last.then_inc(*signal("pe", "gla G"))

                def gla_level(n):
                    pe.wait_ge(*dve(f"gla W {n}"))
                    ps = bank()
                    W = two(Wl[n % 2], 2)
                    for p in range(2):
                        if n == 0:
                            for r in range(2):
                                rows = slice(64 * r, 64 * r + 64)
                                last = pe.matmul(ps[:, r, p * P:(p + 1) * P], W[rows, p, 0:P], W[rows, p, P:S], start=True, stop=True)
                        else:
                            for t in range(T):
                                to = ps[:, 0, :].rearrange("p (r t a s) -> p r t a s", r=2, t=T, a=2)[:, :, t, p, :]
                                last = pe.matmul(to, W[:, p, t * P:(t + 1) * P], Ql[n % 2][:, :, t, p, :], start=True, stop=True)
                    last.then_inc(*signal("pe", f"gla level {n}"))

                def gla_diag():
                    ps = bank()
                    for r in range(2):
                        for p in range(2):
                            for t in range(T):
                                rows, tok = slice(64 * r, 64 * r + 64), slice(t * P, (t + 1) * P)
                                c = (t * 2 + p) * P
                                last = pe.matmul(ps[:, r, c:c + P], kT[rows, p, tok], qT[rows, p, tok], start=True, stop=True)
                    last.then_inc(*signal("pe", "gla diag"))

                def gla_out():
                    pe.wait_ge(*dve("gla diag"))
                    pe.wait_ge(*act("gla cross"))
                    ps = bank()
                    for h in range(GLA_H):
                        r, p = h % 2, h // 2
                        c = slice(h * GLA_DV, (h + 1) * GLA_DV)
                        v = slice(COL["av"] + h * GLA_DV, COL["av"] + (h + 1) * GLA_DV)
                        pe.matmul(ps[:, 0, c], acc[:, r, 0, p], u[:, 0, v], start=True, stop=True)
                        pe.matmul(ps[:, 1, c], cross[:, r, p], u[:, 0, v], start=True, stop=False)
                        last = pe.matmul(ps[:, 1, c], acc[:, r, 1, p], u[:, 1, v], start=False, stop=True)
                    last.then_inc(*signal("pe", "gla out"))

                def ssd_xT(i):
                    pe.wait_ge(*act("evac 4"))
                    ps = bank()
                    for kk in range(4):
                        for t in range(T):
                            c = COL["xbc"] + (4 * i + kk) * P
                            last = pe.transpose(ps[:, kk // 2, (kk % 2) * S + t * P:(kk % 2) * S + (t + 1) * P], u[:, t, c:c + P], ident)
                    last.then_inc(*signal("pe", f"ssd xT {i}"))

                def ssd_xs():
                    pe.wait_ge(*act("ssd silu 0"))
                    ps = bank()
                    for f in range(4):
                        for t in range(T):
                            last = pe.transpose(ps[:, t, f * P:(f + 1) * P], conv(f)[:, t * P:(t + 1) * P], ident)
                    last.then_inc(*signal("pe", "ssd xs"))

                def ssd_cum():
                    pe.wait_ge(*dve("ssd la"))
                    ps = bank()
                    l8 = [las[:, t * SSD_H:(t + 1) * SSD_H] for t in range(T)]
                    pe.matmul(ps[0:SSD_H, 0, 0:S], l8[0], tri_ones, start=True, stop=False)
                    pe.matmul(ps[0:SSD_H, 0, P:S], l8[1], tri, start=False, stop=True)
                    pe.matmul(ps[:, 1, 0:8], tri, l8[0], start=True, stop=True)
                    pe.matmul(ps[:, 1, 8:16], ones, l8[0], start=True, stop=False)
                    pe.matmul(ps[:, 1, 8:16], tri, l8[1], start=False, stop=True).then_inc(*signal("pe", "ssd cum"))

                def ssd_CB():
                    pe.wait_ge(*act("ssd silu 1"))
                    ps = bank()
                    for g in range(SSD_G):
                        pe.matmul(ps[:, g, 0:S], conv(4 + g)[:, 0:P], conv(6 + g), start=True, stop=True)
                        last = pe.matmul(ps[:, g, S:S + P], conv(4 + g)[:, P:S], conv(6 + g)[:, P:S], start=True, stop=True)
                    last.then_inc(*signal("pe", "ssd CB"))

                def ssd_bcast(g):
                    pe.wait_ge(*act("ssd grow"))
                    ps = bank()
                    for h in range(4):
                        pick = ident[0:SSD_H, 4 * g + h:4 * g + h + 1].to_broadcast([SSD_H, P])
                        last = pe.matmul(ps[:, h // 2, (h % 2) * S:(h % 2 + 1) * S], pick, Grow[0:SSD_H, :], start=True, stop=True)
                    last.then_inc(*signal("pe", f"ssd bcast {g}"))

                def ssd_Y(g):
                    pe.wait_ge(*dve(f"ssd M {g}"))
                    pe.wait_ge(*dve("ssd xdt"))
                    ps = bank()
                    for h in range(4):
                        hh = slice((4 * g + h) * SSD_HD, (4 * g + h + 1) * SSD_HD)
                        c = slice(h * SSD_HD, (h + 1) * SSD_HD)
                        pe.matmul(ps[:, 0, c], M[g][:, h, 0:P], xdt[:, 0, hh], start=True, stop=True)
                        pe.matmul(ps[:, 1, c], M[g][:, h, P:S], xdt[:, 0, hh], start=True, stop=False)
                        last = pe.matmul(ps[:, 1, c], M[g][:, h, S:S + P], xdt[:, 1, hh], start=False, stop=True)
                    last.then_inc(*signal("pe", f"ssd Y {g}"))

                def mla_cT():
                    pe.wait_ge(*dve("mla cn"))
                    ps = bank()
                    for kk in range(4):
                        for t in range(T):
                            c = COL["cq"] + kk * P
                            last = pe.transpose(ps[:, kk // 2, (kk % 2) * S + t * P:(kk % 2) * S + (t + 1) * P], u[:, t, c:c + P], ident)
                    last.then_inc(*signal("pe", "mla cT"))

                def mla_q(t):
                    pe.wait_ge(*act("mla cT"))
                    ps = bank()
                    for half, (c, w) in enumerate(((0, 512), (512, 256))):
                        for k in range(3):
                            last = pe.matmul(ps[:, half, 0:w], cT[:, k, t * P:(t + 1) * P], wuq[:, k, c:c + w], start=k == 0, stop=k == 2)
                    last.then_inc(*signal("pe", f"mla q {t}"))

                def mla_kv(t):
                    ps = bank()
                    for half in range(2):
                        last = pe.matmul(ps[:, half, :], cT[:, 3, t * P:(t + 1) * P], wukv[:, half * 512:half * 512 + 512], start=True, stop=True)
                    last.then_inc(*signal("pe", f"mla kv {t}"))

                def heads_T(name, src):
                    ps = bank()
                    for h in range(4):
                        for t in range(T):
                            last = pe.transpose(ps[:, h // 2, (h % 2) * S + t * P:(h % 2) * S + (t + 1) * P], src(t, h), ident)
                    last.then_inc(*signal("pe", name))

                def scores(m, i, kq, rope):
                    pe.wait_ge(*act("mla rT" if rope else "dil kT"))
                    ps = bank()
                    for r in range(2):
                        h = 2 * i + r
                        for c0, c1, qs in ((0, P, slice(0, P)), (P, P + S, slice(P, S))):
                            ks = slice(0, c1 - c0)
                            q, k = kq
                            last = pe.matmul(ps[:, r, c0:c1], q[:, h, qs], k[:, h, ks], start=True, stop=not rope)
                            if rope:
                                rows = slice(64 * (h % 2), 64 * (h % 2) + 64)
                                last = pe.matmul(ps[:, r, c0:c1], mrT[rows, 0, h // 2, qs], mrT[rows, 1, h // 2, ks], start=False, stop=True)
                    last.then_inc(*signal("pe", f"{m} S {i}"))

                def probs_T(m, i):
                    pe.wait_ge(*(act if m == "mla" else dve)(f"{m} P {i}"))
                    ps = bank()
                    for r in range(2):
                        for c in range(3):
                            last = pe.transpose(ps[:, r, c * P:(c + 1) * P], Pb[:, r, c * P:(c + 1) * P], ident)
                    last.then_inc(*signal("pe", f"{m} PT {i}"))

                def values(m, i, v):
                    pe.wait_ge(*act(f"{m} PT {i}"))
                    ps = bank()
                    for r in range(2):
                        h, c = 2 * i + r, slice(r * P, (r + 1) * P)
                        hv = slice(h * P, (h + 1) * P)
                        pe.matmul(ps[:, 0, c], PT[:, r, 0:P], v[:, 0, hv], start=True, stop=True)
                        pe.matmul(ps[:, 1, c], PT[:, r, P:2 * P], v[:, 0, hv], start=True, stop=False)
                        last = pe.matmul(ps[:, 1, c], PT[:, r, 2 * P:3 * P], v[:, 1, hv], start=False, stop=True)
                    last.then_inc(*signal("pe", f"{m} O {i}"))

                def mla_qT():
                    pe.wait_ge(*dve("mla rope"))
                    heads_T("mla qT", lambda t, h: mqk[:, t, h, 0:P])

                def mla_kT():
                    heads_T("mla kT", lambda t, h: mqk[:, t, 4 + h, 0:P])

                def mla_rT():
                    rr = mrr.rearrange("p t (a b) d -> p t a (b d)", b=2)
                    heads_T("mla rT", lambda t, h: rr[:, t, h])

                run = {"gla qk": gla_qk, "gla lr": gla_lr, "gla z": gla_z, "gla G": gla_G, "gla diag": gla_diag,
                       "gla out": gla_out, "ssd xs": ssd_xs, "ssd cum": ssd_cum, "ssd CB": ssd_CB, "mla cT": mla_cT,
                       "mla qT": mla_qT, "mla kT": mla_kT, "mla rT": mla_rT}

                def stages(n):
                    for name in PE_AT:
                        if PE_AT[name] != n:
                            continue
                        i = int(name[-1]) if name[-1].isdigit() else None
                        if name.startswith("yT"):
                            yT(i)
                        elif name in run:
                            run[name]()
                        elif name.startswith("gla level"):
                            gla_level(i)
                        elif name.startswith("ssd xT"):
                            ssd_xT(i)
                        elif name.startswith("ssd bcast"):
                            ssd_bcast(i)
                        elif name.startswith("ssd Y"):
                            ssd_Y(i)
                        elif name.startswith("mla q "):
                            mla_q(i)
                        elif name.startswith("mla kv"):
                            mla_kv(i)
                        elif name == "dil qT":
                            pe.wait_ge(*dve("dil rope 1"))
                            heads_T(name, lambda t, h: dqk[:, t, h])
                        elif name == "dil kT":
                            heads_T(name, lambda t, h: dqk[:, t, 4 + h])
                        elif name.startswith("mla S"):
                            scores("mla", i, (mqT, mkT), True)
                        elif name.startswith("dil S"):
                            scores("dil", i, (dqT, dkT), False)
                        elif name.startswith("mla PT"):
                            probs_T("mla", i)
                        elif name.startswith("dil PT"):
                            probs_T("dil", i)
                        elif name.startswith("mla O"):
                            values("mla", i, mv)
                        elif name.startswith("dil O"):
                            values("dil", i, dv)

                for n in range(UNITS):
                    unit(n)
                    if n in (0, 2):
                        xT(2 + n // 2, l)
                    now[0] = n
                    stages(n)
                    if n in X_NEXT:
                        xT(X_NEXT[n], l + 1)

        SC = {"mla": MLA_QK ** -0.5, "dil": DIL_HD ** -0.5}

        def pair_of(name):
            return pair[:, (JOBS.index(name) + 1) % 2]

        def slot(name, lag=3):
            return PE_AT[name] + lag

        @block.scalar
        def _(act_):
            A_ = act_.activation
            rows = 0
            for l in range(DEPTH):
                for src, n in ((ln_g[l].rearrange("(k p) -> k p", p=P), KT),
                               (conv_w[l].rearrange("j (c p) -> (j c) p", p=P), SSD_TAPS * 8),
                               (conv_b[l].rearrange("(c p) -> c p", p=P), 8)):
                    act_.dma_start(prow[rows:rows + n, :], src).then_inc(rows_in, 16)
                    rows += n
            act_.wait_ge(x_in[0], 16)
            for c in (2, 3):
                x_load(act_, c)

            def xT_hi(j, l, units):
                act_.wait_ge(x_gained, 4 * l + j + 1)
                act_.wait_ge(unit_used, units + SPLIT)
                A_(a_hi[:, 4 * j:4 * j + 4, :], h_full, ACT.Copy).then_inc(x_hi, 1)

            for j in range(2):
                xT_hi(j, 0, 0)
            act_.preload_act_table_set("natural_log_exp_and_others")
            with act_.Fori(0, DEPTH) as l:
                pe, me, dve, pool = reached("pe", l), reached("act", l), reached("dve", l), reached("pool", l)

                def hi(n):
                    w = BLOCKS[n // UPB][2]
                    act_.wait_ge(weights_in[n % RAW], (l * (UNITS // RAW) + n // RAW + 1) * 16)
                    act_.wait_ge(unit_used, l * UNITS + n + 1)
                    A_(w_hi[:, n % SPLIT, :, 0:w], raw[:, n % RAW, :, 0:w], ACT.Copy).then_inc(hi_done, 1)

                def x_stats():
                    act_.wait_ge(x_updated, 4 * (l + 1))
                    for t in range(T):
                        last = A_(u[:, t, 0:D], x[:, t, :], ACT.Square, scale=D ** -0.5, accum_out=xss[:, t:t + 1])
                    last.then_inc(*signal("act", "x rs sum"))

                def yT(j):
                    act_.wait_ge(*pe(f"yT {j}"))
                    act_.wait_ge(unit_used, l * UNITS + (N_INB - 1) * UPB + 2 * (j + 1) + SPLIT)
                    A_(a_hi[:, 4 * j:4 * j + 4, :], pair_of(f"yT {j}").rearrange("p b (k s) -> p (b k) s", k=2), ACT.Copy).then_inc(*signal("act", f"yT {j}"))

                def evac(b):
                    kind, c0, w = BLOCKS[b]
                    act_.wait_ge(unit_used, l * UNITS + (b + 1) * UPB + SPLIT)
                    if b == 0:
                        act_.wait_ge(*pool("x rs"))
                        act_.wait_ge(*me("x rs sum"))
                    if kind == "u":
                        for t in range(T):
                            last = A_(u[:, t, c0 - N_GATE:c0 - N_GATE + w], acc_ps[:, b % 2, t, 0:w], ACT.Copy, scale=xrs[:, t:t + 1])
                    else:
                        g = GATE_ORDER.index(GATE_BLOCK[b])
                        act_.wait_ge(*(pe("mla kv 1") if g == 0 else dve(f"gated {GB}" if g == 1 else f"y {GATE_ORDER[g - 1]}")))
                        for t in range(T):
                            last = A_(gate[:, t, :], acc_ps[:, b % 2, t, :], ACT.Silu, scale=xrs[:, t:t + 1])
                    last.then_inc(*signal("act", f"evac {b}"))
                    if kind != "u":
                        act_.preload_act_table_set("natural_log_exp_and_others")

                def gla_qk():
                    act_.wait_ge(*pe("gla qk"))
                    ps = pair_of("gla qk")
                    A_(qT, two(ps[:, 0, :], 2), ACT.Copy, scale=GLA_DK ** -0.5).then_inc(*signal("act", "gla q"))
                    A_(kT, two(ps[:, 1, :], 2), ACT.Copy).then_inc(*signal("act", "gla k"))

                def gla_lr():
                    act_.wait_ge(*pe("gla lr"))
                    A_(alrT[0:GLA_R, :], pair_of("gla lr")[0:GLA_R, 0, 0:S], ACT.Copy).then_inc(*signal("act", "gla lr"))

                def gla_z():
                    act_.wait_ge(*pe("gla z"))
                    A_(lt, two(pair_of("gla z")[:, 0, :], 2), ACT.Abs).then_inc(*signal("act", "gla abs"))
                    act_.wait_ge(*me("gla abs"))
                    A_(lt, lt, ACT.Exp, scale=-1.0).then_inc(*signal("act", "gla exp"))
                    act_.wait_ge(*me("gla exp"))
                    A_(lt, lt, ACT.Ln, bias=1.0).then_inc(*signal("act", "gla ln"))

                def gla_G():
                    act_.wait_ge(*pe("gla G"))
                    A_(GT, two(pair_of("gla G")[:, 0, :], 2), ACT.Copy, scale=1.0 / GLA_TAU).then_inc(*signal("act", "gla G"))

                def gla_E(n):
                    B = P >> n
                    v = Dl[n % 2].rearrange("p (a s) -> p a s", s=2 * B)
                    act_.wait_ge(*dve(f"gla D {n}"))
                    A_(v[:, :, 0:B], v[:, :, 0:B], ACT.Exp, scale=-1.0)
                    A_(v[:, :, B:2 * B], v[:, :, B:2 * B], ACT.Exp).then_inc(*signal("act", f"gla E {n}"))

                def gla_cross():
                    act_.wait_ge(*pe("gla level 0"))
                    A_(cross.rearrange("p r a q -> p r (a q)"), pair_of("gla level 0")[:, :, 0:256], ACT.Copy).then_inc(*signal("act", "gla cross"))

                def gla_norm():
                    act_.wait_ge(*pe("gla out"))
                    act_.wait_ge(*dve("gla W 7"))
                    ps = pair_of("gla out")
                    for t in range(T):
                        for h in range(GLA_H):
                            j = t * GLA_H + h
                            last = A_(A(512 + j * P, P), ps[:, t, h * P:(h + 1) * P], ACT.Square, scale=GLA_DV ** -0.5, accum_out=gss[:, j:j + 1])
                    last.then_inc(*signal("act", "gla rs sum"))

                def ssd_xT(i):
                    act_.wait_ge(*pe("ssd xT 1"))
                    act_.wait_ge(*dve("pad"))
                    A_(xc[:, 4 * i:4 * i + 4, 3:3 + S], pair_of(f"ssd xT {i}").rearrange("p b (k s) -> p (b k) s", k=2), ACT.Copy).then_inc(*signal("act", f"ssd xT {i}"))

                def conv_tap3(i):
                    act_.wait_ge(*me(f"ssd xT {i}"))
                    act_.wait_ge(*dve("prm"))
                    for f in range(4 * i, 4 * i + 4):
                        last = A_(conv(f), xc[:, f, 3:3 + S], ACT.Identity, bias=prm[:, 48 + f:49 + f], scale=prm[:, 16 + 24 + f:16 + 25 + f])
                    last.then_inc(*signal("act", f"conv 3 {i}"))

                def sincos():
                    act_.wait_ge(setup["pool"], 1)
                    A_(sc[:, :, :, :].rearrange("p a t d -> p (a t d)"), angle[:, :], ACT.Sin).then_inc(*signal("act", "sincos"))

                def ssd_silu(i):
                    act_.wait_ge(*dve(f"conv {i} 5"))
                    A_(conv4[i], conv4[i], ACT.Silu).then_inc(*signal("act", f"ssd silu {i}"))

                def ssd_dt():
                    act_.wait_ge(*dve("ssd dt0"))
                    A_(dta, dtv, ACT.Abs).then_inc(*signal("act", "ssd abs"))
                    act_.wait_ge(*me("ssd abs"))
                    A_(dta, dta, ACT.Exp, scale=-1.0).then_inc(*signal("act", "ssd exp"))
                    A_(eA, bc["alog"], ACT.Exp).then_inc(*signal("act", "ssd eA"))
                    act_.wait_ge(*me("ssd eA"))
                    A_(dta, dta, ACT.Ln, bias=1.0).then_inc(*signal("act", "ssd ln"))

                def ssd_cum():
                    act_.wait_ge(*pe("ssd cum"))
                    ps = pair_of("ssd cum")
                    A_(Grow[0:SSD_H, :], ps[0:SSD_H, 0, 0:S], ACT.Copy).then_inc(*signal("act", "ssd grow"))
                    A_(gcol, ps[:, 1, 0:16], ACT.Copy).then_inc(*signal("act", "ssd gcol"))

                def ssd_exp(g):
                    act_.wait_ge(*dve(f"ssd E {g}"))
                    A_(M[g][:, :, :], M[g][:, :, :], ACT.Exp).then_inc(*signal("act", f"ssd exp {g}"))

                def ssd_sq():
                    act_.wait_ge(*dve(f"gated {GB}"))
                    for t in range(T):
                        for g in range(SSD_G):
                            c = slice(g * 256, (g + 1) * 256)
                            last = A_(bsq[:, t, c], o[:, GB, t, c], ACT.Square, scale=256 ** -0.5, accum_out=bss[:, 2 * t + g:2 * t + g + 1])
                    last.then_inc(*signal("act", "ssd rs sum"))

                def mla_c():
                    act_.wait_ge(*me("evac 5"))
                    for t in range(T):
                        A_(A(3072 + t * 512, MLA_QL), u[:, t, COL["cq"]:COL["cq"] + MLA_QL], ACT.Square, scale=MLA_QL ** -0.5, accum_out=css[:, t:t + 1])
                        last = A_(A(3072 + t * 512 + MLA_QL, MLA_KVL), u[:, t, COL["ckv"]:COL["ckv"] + MLA_KVL], ACT.Square, scale=MLA_KVL ** -0.5, accum_out=css[:, 2 + t:3 + t])
                    last.then_inc(*signal("act", "mla crs sum"))

                def mla_cT():
                    act_.wait_ge(*pe("mla cT"))
                    act_.wait_ge(*me("mla crs sum"))
                    A_(cT, pair_of("mla cT").rearrange("p b (k s) -> p (b k) s", k=2), ACT.Copy).then_inc(*signal("act", "mla cT"))

                def mla_q(t):
                    act_.wait_ge(*pe(f"mla q {t}"))
                    A_(u[:, t, 0:768], pair_of(f"mla q {t}").rearrange("p b c -> p (b c)")[:, 0:768], ACT.Copy).then_inc(*signal("act", f"mla q {t}"))

                def mla_kv(t):
                    act_.wait_ge(*pe(f"mla kv {t}"))
                    ps = pair_of(f"mla kv {t}").rearrange("p b (h c) -> p (b h) c", h=2)
                    A_(mqk[:, t, 4:8, 0:P], ps[:, :, 0:P], ACT.Copy)
                    A_(mqk[:, t, 4:8, P:MLA_QK], u[:, t, COL["ckr"]:COL["ckr"] + 64].unsqueeze(1).to_broadcast([P, 4, 64]), ACT.Copy)
                    A_(mv[:, t, :].rearrange("p (h c) -> p h c", h=4), ps[:, :, P:2 * P], ACT.Copy).then_inc(*signal("act", f"mla kv {t}"))

                def head_sums(m, i):
                    if m == "mla":
                        act_.wait_ge(*me("mla kv 1" if i else "mla q 1"))
                        act_.wait_ge(*pe("ssd Y 0"))
                        buf, sq, total = mqk, msq, mss
                    else:
                        act_.wait_ge(*me("dil rs 0 sum" if i else "mla rs 1 sum"))
                        buf, sq, total = dqk, dsq, dss
                    for t in range(T):
                        for h in range(4):
                            j = 8 * i + 4 * t + h
                            last = A_(sq[:, t, h, :], buf[:, t, 4 * i + h, :], ACT.Square, scale=buf.shape[-1] ** -0.5, accum_out=total[:, j:j + 1])
                    last.then_inc(*signal("act", f"{m} rs {i} sum"))

                def heads_T(name, dst):
                    act_.wait_ge(*pe(name))
                    A_(dst, pair_of(name).rearrange("p b (k s) -> p (b k) s", k=2), ACT.Copy).then_inc(*signal("act", name))

                def probs(m, i):
                    act_.wait_ge(*dve(f"{m} nmax {i}"))
                    for r in range(2):
                        for t, (c0, c1) in enumerate(((0, P), (P, P + S))):
                            j = 2 * r + t
                            last = A_(Pb[:, r, c0:c1], Pb[:, r, c0:c1], ACT.Exp, bias=nm[:, j:j + 1], scale=SC[m],
                                      accum_out=sm[i][:, j:j + 1] if m == "mla" else None)
                    last.then_inc(*signal("act", f"{m} P {i}"))

                def probs_T(m, i):
                    act_.wait_ge(*pe(f"{m} PT {i}"))
                    A_(PT[:, :, :], pair_of(f"{m} PT {i}")[:, :, 0:384], ACT.Copy).then_inc(*signal("act", f"{m} PT {i}"))

                for n in range(UNITS):
                    hi(n)
                    if n in (3, 5):
                        xT_hi((n + 1) // 2, l, l * UNITS)
                    if n == 6:
                        x_stats()
                    for j in range(4):
                        if n == slot(f"yT {j}"):
                            yT(j)
                    if n in EVAC_AT:
                        evac(EVAC_AT[n])
                    if n == slot("gla qk"):
                        gla_qk()
                    if n == slot("gla lr"):
                        gla_lr()
                    if n == slot("gla z"):
                        gla_z()
                    if n == slot("gla G"):
                        gla_G()
                        gla_E(0)
                        gla_E(1)
                    for i in range(6):
                        if n == PE_AT[f"gla level {i}"] + 2:
                            gla_E(i + 2)
                    if n == slot("gla level 0"):
                        gla_cross()
                    if n == 46:
                        ssd_xT(0)
                        ssd_dt()
                    if n == 47:
                        ssd_xT(1)
                        conv_tap3(1)
                    if n == slot("gla out"):
                        gla_norm()
                    if n == 49:
                        conv_tap3(0)
                    if n == slot("ssd cum"):
                        ssd_cum()
                    if n == 54:
                        ssd_silu(1)
                    if n == 55:
                        sincos()
                    if n == 56:
                        mla_c()
                    if n == 60:
                        ssd_silu(0)
                        act_.preload_act_table_set("natural_log_exp_and_others")
                    if n == 65:
                        ssd_exp(0)
                    if n == 71:
                        ssd_exp(1)
                    if n == slot("mla cT"):
                        mla_cT()
                    for i in range(2):
                        if n == slot(f"mla q {i}"):
                            mla_q(i)
                        if n == slot(f"mla kv {i}"):
                            mla_kv(i)
                    if n == 73:
                        head_sums("mla", 0)
                    if n == 77:
                        head_sums("mla", 1)
                    if n == 80:
                        head_sums("dil", 0)
                    if n == 82:
                        head_sums("dil", 1)
                    if n == slot("mla qT"):
                        heads_T("mla qT", mqT)
                    if n == slot("mla kT"):
                        heads_T("mla kT", mkT)
                    if n == slot("mla rT"):
                        heads_T("mla rT", mrT.rearrange("p a b s -> p (a b) s"))
                    if n == slot("dil qT"):
                        heads_T("dil qT", dqT)
                    if n == slot("dil kT"):
                        heads_T("dil kT", dkT)
                    for m in ("mla", "dil"):
                        for i in range(2):
                            if n == slot(f"{m} S {i}"):
                                probs(m, i)
                            if n == slot(f"{m} PT {i}"):
                                probs_T(m, i)
                    if n == 94:
                        ssd_sq()
                    if n in (UNITS - 3, UNITS - 1):
                        j = (n - UNITS + 3) // 2
                        xT_hi(j, l + 1, l * UNITS + UNITS - UPB + 2 * (j + 1))

        @block.vector
        def _(v):
            v.sem_inc(split_done, RAW)
            v.memset(alrT[:, :], 1.0)
            v.memset(allp[:, 56 * DEPTH:], 0.0)
            v.wait_ge(setup["pe"], 1)
            v.tensor_copy(allp[:, 0:56 * DEPTH], acc_ps[:, 1, 1, 0:56 * DEPTH]).then_inc(setup["dve"], 1)
            v.wait_ge(setup["dve"], 1)
            v.tensor_copy(lng[:, :], allp[:, 0:KT]).then_inc(setup["dve"], 1)
            v.wait_ge(setup["dve"], 2)

            def x_gain(j, l):
                v.wait_ge(x_turned, 4 * l + j + 1)
                if j:
                    v.wait_ge(x_lo, 4 * l + j)
                g = lng[:, 4 * j:4 * j + 4].unsqueeze(2).to_broadcast([P, 4, S])
                v.tensor_tensor(h_full, pair[:, j % 2].rearrange("p b (k s) -> p (b k) s", k=2), g, ALU.mult).then_inc(x_gained, 1)

            def xT_lo(j, l):
                v.wait_ge(x_gained, 4 * l + j + 1)
                v.wait_ge(x_hi, 4 * l + j + 1)
                v.tensor_tensor(a_lo[:, 4 * j:4 * j + 4, :], h_full, a_hi[:, 4 * j:4 * j + 4, :].bitcast(F32), ALU.subtract).then_inc(x_lo, 1)

            for j in range(2):
                x_gain(j, 0)
                xT_lo(j, 0)
            with v.Fori(0, DEPTH) as l:
                pe, act, me, pool = reached("pe", l), reached("act", l), reached("dve", l), reached("pool", l)
                TT, TS, STT = v.tensor_tensor, v.tensor_scalar, v.scalar_tensor_tensor
                sig = lambda name: signal("dve", name)
                v.memset(xc[:, :, 0:3], 0.0).then_inc(*sig("pad"))
                v.tensor_copy(prm[:, :], allp[:, bass.ds(l * 56, 56)]).then_inc(*sig("prm"))

                def lo(n):
                    w = BLOCKS[n // UPB][2]
                    v.wait_ge(hi_done, l * UNITS + n + 1)
                    TT(w_lo[:, n % SPLIT, :, 0:w], raw[:, n % RAW, :, 0:w], w_hi[:, n % SPLIT, :, 0:w].bitcast(F32), ALU.subtract).then_inc(split_done, 1)

                def yT(j):
                    v.wait_ge(*act(f"yT {j}"))
                    TT(a_lo[:, 4 * j:4 * j + 4, :], pair_of(f"yT {j}").rearrange("p b (k s) -> p (b k) s", k=2), a_hi[:, 4 * j:4 * j + 4, :].bitcast(F32), ALU.subtract).then_inc(*sig(f"yT {j}"))

                def x_update(b):
                    c = OUT_BLOCK[b]
                    v.wait_ge(unit_used, l * UNITS + (b + 1) * UPB + SPLIT)
                    TT(x[:, :, c * WB:(c + 1) * WB], x[:, :, c * WB:(c + 1) * WB], acc_ps[:, b % 2, :, :], ALU.add).then_inc(x_updated, 1)

                def gated(g):
                    b = [k for k in GATE_BLOCK if GATE_BLOCK[k] == g][0]
                    v.wait_ge(*act(f"evac {b}"))
                    v.wait_ge(*me({GA: "gla o", GB: "ssd y 1", GC: "mla O 1", GD: "dil O 1"}[g]))
                    TT(o[:, g], o[:, g], gate, ALU.mult).then_inc(*sig(f"gated {g}" if g == GB else f"y {g}"))

                def gla_la():
                    v.wait_ge(setup["pool"], 1)
                    v.wait_ge(*act("gla ln"))
                    STT(la, two(pair_of("gla z")[:, 0, :], 2), 0.0, lt, ALU.min, ALU.subtract).then_inc(*sig("gla la"))

                def gla_D(n):
                    B = P >> n
                    g = GT.rearrange("p a s -> p (a s)").rearrange("p (n s) -> p n s", s=2 * B)
                    ref = g[:, :, B - 1:B].to_broadcast([P, S // B, 2 * B])
                    if n == 0:
                        v.wait_ge(*act("gla G"))
                    if n >= 2:
                        v.wait_ge(*me(f"gla W {n - 2}"))
                    TT(Dl[n % 2].rearrange("p (n s) -> p n s", s=2 * B), g, ref, ALU.subtract).then_inc(*sig(f"gla D {n}"))

                def gla_W(n):
                    B = P >> n
                    h = lambda t: t.rearrange("p (n s) -> p n s", s=2 * B)
                    W, E = h(Wl[n % 2]), h(Dl[n % 2])
                    k, q = h(kT.rearrange("p a s -> p (a s)")), h(qT.rearrange("p a s -> p (a s)"))
                    v.wait_ge(*act(f"gla E {n}"))
                    if n < 2:
                        v.wait_ge(*me("gla zero 1"))
                    if n >= 2:
                        v.wait_ge(*pe(f"gla level {n - 2}"))
                    last = TT(W[:, :, 0:B], k[:, :, 0:B], E[:, :, 0:B], ALU.mult)
                    if n == 0:
                        last = TT(W[:, :, B:], q[:, :, B:], E[:, :, B:], ALU.mult)
                    else:
                        for r in range(2):
                            rows = slice(64 * r, 64 * r + 64)
                            for p in range(2):
                                blocks = slice(p * (S // (2 * B)), (p + 1) * (S // (2 * B)))
                                to = Ql[n % 2][rows, r, :, p, :]
                                if B < 64:
                                    to = to.rearrange("p t (n s) -> p t n s", s=B)
                                    qq, ee = (m[rows, blocks, B:].rearrange("p (t n) s -> p t n s", t=T) for m in (q, E))
                                else:
                                    qq, ee = (m[rows, blocks, B:] for m in (q, E))
                                last = TT(to, qq, ee, ALU.mult)
                    last.then_inc(*sig(f"gla W {n}"))

                acc8 = acc.rearrange("p r t a q -> p (r t a) q")

                def gla_merge(n):
                    name = f"gla level {n}" if n < 8 else "gla diag"
                    i = n if n < 8 else 0
                    v.wait_ge(*pe(name))
                    v.wait_ge(*me(f"gla merge {n - 1}" if n > 1 else "gla zero 1"))
                    v.memset(st[:, 160:161], 0.0)
                    ps = pair_of(name).rearrange("p r (c q) -> p (r c) q", c=4)
                    mask = lmask[:, i].unsqueeze(1).to_broadcast([P, 8, P])
                    if n < 8:
                        B = P >> n
                        to, mask = (k.rearrange("p c (n s) -> p c n s", s=2 * B)[:, :, :, B:] for k in (acc8, mask))
                        ps = pair_of(name)[:, 0, :].rearrange("p (c n s) -> p c n s", c=8, s=B)
                    else:
                        to = acc8
                    v.copy_predicated(to, mask, ps).then_inc(*sig(f"gla merge {n}" if n < 8 else "gla diag"))

                def gla_norm():
                    v.wait_ge(*pool("gla rs"))
                    ps = pair_of("gla out")
                    for t in range(T):
                        for h in range(GLA_H):
                            c, j = slice(h * P, (h + 1) * P), t * GLA_H + h
                            last = STT(o[:, GA, t, c], ps[:, t, c], grs[:, j:j + 1], bc["gla_ng"], ALU.mult, ALU.mult)
                    last.then_inc(*sig("gla o"))

                def ssd_dt0():
                    v.wait_ge(*act("evac 4"))
                    v.wait_ge(params_in, (l + 1) * 16 * N_PARAMS)
                    TT(two(dtv, 2), u[:, :, COL["dt"]:COL["dt"] + 8], bc["dtb"].unsqueeze(1).to_broadcast([P, 2, 8]), ALU.add).then_inc(*sig("ssd dt0"))

                def ssd_la():
                    v.wait_ge(*act("ssd ln"))
                    STT(dts, dtv, 0.0, dta, ALU.max, ALU.add).then_inc(*sig("ssd dt"))
                    v.wait_ge(*me("ssd dt"))
                    STT(two(las, 2), two(dts, 2), -1.0, eA.unsqueeze(1).to_broadcast([P, 2, 8]), ALU.mult, ALU.mult).then_inc(*sig("ssd la"))

                def conv_step(i, s):
                    if s == 0:
                        v.wait_ge(*act(f"conv 3 {i}"))
                    if s >= 2:
                        v.wait_ge(*me(f"conv {i} {s - 2}"))
                    j = 2 - s // 2
                    for f in range(4 * i + s % 2 * 2, 4 * i + s % 2 * 2 + 2):
                        last = STT(conv(f), xc[:, f, j:j + S], prm[:, 16 + 8 * j + f:17 + 8 * j + f], conv(f), ALU.mult, ALU.add)
                    last.then_inc(*sig(f"conv {i} {s}"))

                def ssd_xD():
                    v.wait_ge(*pe("ssd xs"))
                    ps = pair_of("ssd xs").rearrange("p t (h c) -> p t h c", h=8)
                    ob = o[:, GB].rearrange("p t (h c) -> p t h c", h=8)
                    TT(ob, ps, bc["D"].unsqueeze(1).unsqueeze(3).to_broadcast([P, T, 8, 64]), ALU.mult).then_inc(*sig("ssd xD"))

                def ssd_xdt():
                    v.wait_ge(*me("ssd xD"))
                    ps = pair_of("ssd xs").rearrange("p t (h c) -> p t h c", h=8)
                    TT(xdt.rearrange("p t (h c) -> p (t h) c", h=8), ps.rearrange("p t h c -> p (t h) c"), dts.unsqueeze(2).to_broadcast([P, 16, 64]), ALU.mult).then_inc(*sig("ssd xdt"))

                def ssd_CB():
                    v.wait_ge(*pe("ssd CB"))
                    mk = cst[:, C_TRI:C_TRI + 384].unsqueeze(1).to_broadcast([P, 2, 384])
                    TT(CBm, pair_of("ssd CB")[:, :, 0:384], mk, ALU.mult).then_inc(*sig("ssd CB"))

                def ssd_E(g, h):
                    if h == 0:
                        v.wait_ge(*pe(f"ssd bcast {g}"))
                        v.wait_ge(*act("ssd gcol"))
                    ps = pair_of(f"ssd bcast {g}").rearrange("p b (h s) -> p (b h) s", h=2)
                    hh = 4 * g + h
                    TS(M[g][:, h, 0:S], ps[:, h, :], gcol[:, hh:hh + 1], 0.0, ALU.subtract, ALU.min)
                    last = TS(M[g][:, h, S:S + P], ps[:, h, P:S], gcol[:, 8 + hh:9 + hh], 0.0, ALU.subtract, ALU.min)
                    if h == 3:
                        last.then_inc(*sig(f"ssd E {g}"))

                def ssd_M(g):
                    v.wait_ge(*act(f"ssd exp {g}"))
                    v.wait_ge(*me("ssd CB"))
                    TT(M[g][:, :, :], M[g][:, :, :], CBm[:, g, :].unsqueeze(1).to_broadcast([P, 4, 384]), ALU.mult).then_inc(*sig(f"ssd M {g}"))

                def ssd_y(g):
                    v.wait_ge(*pe(f"ssd Y {g}"))
                    v.wait_ge(*me("ssd xD"))
                    ob = o[:, GB, :, g * 256:(g + 1) * 256]
                    TT(ob, ob, pair_of(f"ssd Y {g}")[:, :, 0:256], ALU.add).then_inc(*sig(f"ssd y {g}"))

                def ssd_norm():
                    v.wait_ge(*pool("ssd rs"))
                    for t in range(T):
                        for g in range(SSD_G):
                            c = slice(g * 256, (g + 1) * 256)
                            last = STT(o[:, GB, t, c], o[:, GB, t, c], brs[:, 2 * t + g:2 * t + g + 1], bc["ssd_ng"][:, c], ALU.mult, ALU.mult)
                    last.then_inc(*sig(f"y {GB}"))

                def mla_cn(t):
                    v.wait_ge(*pool("mla crs"))
                    a, b = (u[:, t, COL[k]:COL[k] + n] for k, n in (("cq", MLA_QL), ("ckv", MLA_KVL)))
                    STT(a, a, crs[:, t:t + 1], bc["q_ng"], ALU.mult, ALU.mult)
                    last = STT(b, b, crs[:, 2 + t:3 + t], bc["kv_ng"], ALU.mult, ALU.mult)
                    if t:
                        last.then_inc(*sig("mla cn"))

                def head_norm(m, i, t):
                    v.wait_ge(*pool(f"{m} rs {i}"))
                    buf, rs = (mqk, mrs) if m == "mla" else (dqk, drs)
                    g = bc[("q_hg", "k_hg")[i] if m == "mla" else ("dq_g", "dk_g")[i]]
                    for h in range(4):
                        j = 8 * i + 4 * t + h
                        last = STT(buf[:, t, 4 * i + h, :], buf[:, t, 4 * i + h, :], rs[:, j:j + 1], g, ALU.mult, ALU.mult)
                    last.then_inc(*sig(f"{m} n {i} {t}"))

                def rope_products(name, after, x1, x2, tmp, nh, hd, step):
                    v.wait_ge(*act("sincos"))
                    v.wait_ge(*me(after))
                    s, c = (sc[:, a, :, 0:64:step].unsqueeze(2).to_broadcast([P, T, nh, hd]) for a in range(2))
                    TT(tmp[0], x1, c, ALU.mult)
                    TT(tmp[1], x2, s, ALU.mult)
                    TT(tmp[2], x2, c, ALU.mult)
                    TT(tmp[3], x1, s, ALU.mult).then_inc(*sig(name + " products"))

                def rope_sums(name, y1, y2, tmp):
                    v.wait_ge(*me(name + " products"))
                    TT(y1, tmp[0], tmp[1], ALU.subtract)
                    TT(y2, tmp[2], tmp[3], ALU.add).then_inc(*sig(name))

                def smax(m, i):
                    v.wait_ge(*pe(f"{m} S {i}"))
                    if i:
                        v.wait_ge(*pe(f"{m} PT {i - 1}"))
                    ps = pair_of(f"{m} S {i}")
                    mk = cmask if m == "mla" else dadd
                    v.memset(st[:, 160:161], 0.0)
                    for r in range(2):
                        for t, (c0, c1) in enumerate(((0, P), (P, P + S))):
                            j = 2 * r + t
                            last = v.tensor_tensor_reduce(out=Pb[:, r, c0:c1], in0=ps[:, r, c0:c1], in1=mk[:, 2 * P - (c1 - c0):], scale=1.0,
                                                          scalar=-3e38, op0=ALU.add, op1=ALU.max, accum_out=mx[:, j:j + 1])
                    last.then_inc(*sig(f"{m} max {i}"))
                    v.wait_ge(*me(f"{m} max {i}"))
                    TS(nm, mx, -SC[m], None, ALU.mult).then_inc(*sig(f"{m} nmax {i}"))

                def taps(i):
                    v.wait_ge(*act(f"dil P {i}"))
                    for r in range(2):
                        for t, (c0, c1) in enumerate(((0, P), (P, P + S))):
                            j = 2 * r + t
                            last = v.tensor_tensor_reduce(out=Pb[:, r, c0:c1], in0=Pb[:, r, c0:c1], in1=dmul[:, 2 * P - (c1 - c0):], scale=1.0,
                                                          scalar=0.0, op0=ALU.mult, op1=ALU.add, accum_out=sm[i][:, j:j + 1])
                    last.then_inc(*sig(f"dil P {i}"))

                def out_heads(m, i):
                    if m == "dil":
                        v.wait_ge(*me(f"dil P {i}"))
                    else:
                        v.wait_ge(*act(f"mla P {i}"))
                    if (m, i) != ("mla", 0):
                        v.wait_ge(*me(f"{m} O 0" if i else "mla O 1"))
                    v.reciprocal(ri, sm[i]).then_inc(*sig(f"{m} ri {i}"))
                    v.wait_ge(*me(f"{m} ri {i}"))
                    v.wait_ge(*pe(f"{m} O {i}"))
                    ps = pair_of(f"{m} O {i}")
                    g = GC if m == "mla" else GD
                    for t in range(T):
                        for r in range(2):
                            h, j = 2 * i + r, 2 * r + t
                            last = TS(o[:, g, t, h * P:(h + 1) * P], ps[:, t, r * P:(r + 1) * P], ri[:, j:j + 1], None, ALU.mult)
                    last.then_inc(*sig(f"{m} O {i}"))

                for n in range(UNITS):
                    lo(n)
                    if n in (3, 5):
                        x_gain((n + 1) // 2, l)
                        xT_lo((n + 1) // 2, l)
                    for j in range(4):
                        if n == slot(f"yT {j}"):
                            yT(j)
                    if n % UPB == 2 and n // UPB - 1 >= N_INB:
                        x_update(n // UPB - 1)
                    if n == slot("gla z"):
                        gla_la()
                        v.memset(acc8, 0.0)
                        for i in range(2):
                            v.memset(Wl[i], 0.0)
                            v.memset(Ql[i].rearrange("p r t a s -> p (r t a s)"), 0.0).then_inc(*sig(f"gla zero {i}"))
                    if n == slot("gla G"):
                        gla_D(0)
                        gla_D(1)
                        gla_W(0)
                    for i in range(1, 8):
                        if n == PE_AT[f"gla level {i - 1}"] + 1:
                            if i < 7:
                                gla_D(i + 1)
                            gla_W(i)
                        if n == PE_AT[f"gla level {i}"] + 3:
                            gla_merge(i)
                    if n == slot("gla diag"):
                        gla_merge(8)
                    if n == 45:
                        ssd_dt0()
                    if n == 47:
                        ssd_la()
                    for i in range(2):
                        for s in range(6):
                            if n == (54, 48)[i] + s:
                                conv_step(i, s)
                    if n == slot("gla out", 4):
                        gla_norm()
                    if n == slot("ssd CB"):
                        ssd_CB()
                    for t in range(T):
                        if n == 60 + t:
                            mla_cn(t)
                    for g in range(2):
                        for h in range(4):
                            if n == (62 + h, 69 + h // 2)[g]:
                                ssd_E(g, h)
                        if n == (68, 73)[g]:
                            ssd_M(g)
                    if n == 66:
                        ssd_xD()
                    if n == 67:
                        ssd_xdt()
                    if n == 73:
                        ssd_y(0)
                    if n == 79:
                        ssd_y(1)
                    for t in range(T):
                        if n == 77 + t:
                            head_norm("mla", 0, t)
                        if n == 81 + t:
                            head_norm("mla", 1, t)
                    if n == 83:
                        rope_products("mla rope", "mla n 1 1", mqk[:, :, :, P:P + 32], mqk[:, :, :, P + 32:P + 64], mtmp, 8, 32, 2)
                    if n == 84:
                        rope_sums("mla rope", mrr[:, :, :, 0:32], mrr[:, :, :, 32:64], mtmp)
                    for i in range(2):
                        b = dqk[:, :, 4 * i:4 * i + 4]
                        if n == 86 + i:
                            for t in range(T):
                                head_norm("dil", i, t)
                        if n == 88 + 2 * i:
                            rope_products(f"dil rope {i}", "dil rope 0" if i else "dil n 1 1", b[:, :, :, 0:64], b[:, :, :, 64:128], dtmp, 4, 64, 1)
                        if n == 89 + 2 * i:
                            rope_sums(f"dil rope {i}", b[:, :, :, 0:64], b[:, :, :, 64:128], dtmp)
                    for m in ("mla", "dil"):
                        for i in range(2):
                            if n == slot(f"{m} S {i}"):
                                smax(m, i)
                                if m == "dil":
                                    taps(i)
                            if n == slot(f"{m} O {i}"):
                                out_heads(m, i)
                    if n == 93:
                        gated(GB)
                    if n == 96:
                        ssd_norm()
                    if n == 99:
                        gated(GA)
                    if n == 107:
                        gated(GC)
                    if n == 115:
                        gated(GD)
                    if n == 128:
                        v.wait_ge(x_lo, 4 * (l + 1))
                        v.tensor_copy(lng[:, :], allp[:, bass.ds(l * 56 + 56, KT)]).then_inc(*sig("ln gain"))
                        v.wait_ge(*me("ln gain"))
                    if n in (UNITS - 3, UNITS - 1):
                        j = (n - UNITS + 3) // 2
                        x_gain(j, l + 1)
                        xT_lo(j, l + 1)
                x_update(len(BLOCKS) - 1)


_INS = ["x", "positions", "ln_g", "w_in", "w_out", "gla_gate_w2", "gla_gate_b", "gla_norm_g", "ssd_conv_w", "ssd_conv_b",
        "ssd_dt_bias", "ssd_A_log", "ssd_D", "ssd_norm_g", "mla_q_norm_g", "mla_kv_norm_g", "mla_w_uq", "mla_w_ukv",
        "mla_q_head_g", "mla_k_head_g", "dil_q_g", "dil_k_g"]
_OUTS = [((1, S, D), "float32")]


def kernel(**inputs):
    import concourse.bacc as _bacc
    from concourse.bass_utils import run_bass_kernel_spmd as _run

    consts, masks = tables()
    given = {n: np.ascontiguousarray(inputs[n]) for n in _INS} | {"consts": consts, "masks": masks}
    for counting in (True, False):
        COUNTING[0] = counting
        if counting:
            for e in ORDER:
                ORDER[e].clear()
        nc = _bacc.Bacc("TRN2", target_bir_lowering=False, num_devices=1)
        arrays, args = {}, []
        for name, a in given.items():
            arrays[f"in_{name}_dram"] = a
            args.append(nc.dram_tensor(f"in_{name}_dram", a.shape, mybir.dt.from_np(a.dtype), kind="ExternalInput").ap())
        for i, (shape, dtype) in enumerate(_OUTS):
            args.append(nc.dram_tensor(f"out_{i}_dram", shape, mybir.dt.from_np(np.dtype(dtype)), kind="ExternalOutput").ap())
        build(nc, *args)
    r = _run(nc, [arrays], core_ids=[0])
    return r.results[0]["out_0_dram"]
```

```python
from contextlib import ExitStack

import numpy as np

import concourse.bass as bass
from concourse import mybir

ALU = mybir.AluOpType
ACT = mybir.ActivationFunctionType
AX = mybir.AxisListType
F32 = mybir.dt.float32
F32R = mybir.dt.float32r
U8 = mybir.dt.uint8
I32 = mybir.dt.int32

P = 128
S, D, DEPTH = 256, 2048, 2
T = S // P
KT = D // P
EPS = 1e-6
GLA_H, GLA_DK, GLA_DV, GLA_R, GLA_TAU = 4, 64, 128, 16, 16.0
SSD_DI, SSD_H, SSD_G, SSD_N, SSD_TAPS = 512, 8, 2, 128, 4
SSD_HD = SSD_DI // SSD_H
SSD_C = SSD_DI + 2 * SSD_G * SSD_N
SSD_CT = SSD_C // P
MLA_H, MLA_NOPE, MLA_ROPE, MLA_V, MLA_QL, MLA_KVL = 4, 128, 64, 128, 384, 128
MLA_QK = MLA_NOPE + MLA_ROPE
DIL_H, DIL_HD = 4, 128
DIL_CONFIGS = ((128, 1), (512, 4), (2048, 16))
N_GATE = 2048
CONV_W = DEPTH * KT
CONV_B = CONV_W + DEPTH * SSD_TAPS * SSD_CT
ROWS = CONV_B + DEPTH * SSD_CT
N_IN = 6232
GA, GB, GC, GD = range(4)

WIDTHS = (("aq", 256), ("ak", 256), ("av", 512), ("alr", GLA_R), ("xbc", SSD_C), ("dt", SSD_H), ("cq", MLA_QL),
          ("ckv", MLA_KVL), ("ckr", MLA_ROPE), ("dq", 512), ("dk", 512), ("dv", 512))
COL, _at = {}, 0
for _name, _w in WIDTHS:
    COL[_name] = _at
    _at += _w
N_U = _at
assert N_GATE + N_U == N_IN

WB = 512
NARROW = 278
BLOCKS = [("u", N_GATE + c, WB) for c in (0, 1024, 512, 1536, 2048, 2560)]
BLOCKS += [("u", N_GATE + 3072 + i * NARROW, NARROW) for i in range(4)]
assert 3072 + 4 * NARROW == N_U
GATE_ORDER = (GB, GA, GC, GD)
GATE_BLOCK = {}
for _g in GATE_ORDER:
    GATE_BLOCK[len(BLOCKS)] = _g
    BLOCKS.append(("gate", _g * WB, WB))
N_INB = len(BLOCKS)
OUT_BLOCK = {}
for _c in range(D // WB):
    OUT_BLOCK[len(BLOCKS)] = _c
    BLOCKS.append(("out", _c * WB, WB))
UK = 2
UPB = KT // UK
UNITS = len(BLOCKS) * UPB
U_OUT = N_INB * UPB
RAW, SPLIT = 4, 4
assert UNITS % RAW == 0 and UNITS % SPLIT == 0

LEVELS = (64, 32, 16, 8, 4, 2, 1)
NEG = -1e30

C_ID, C_TRI, C_ONE, C_TRI2 = 0, 128, 256, 384
C_CZ, C_CM = 512, 640
C_DA = 768
C_DM = 1024
C_FR = 1280
NC = C_FR + DIL_HD // 2


def tables():
    c = np.zeros((P, NC), np.float32)
    i = np.arange(P)
    c[:, C_ID:C_ID + P] = i[:, None] == i[None, :]
    c[:, C_TRI:C_TRI + P] = i[:, None] <= i[None, :]
    c[:, C_ONE:C_ONE + P] = 1
    c[:, C_TRI2:C_TRI2 + P] = i[:, None] <= i[None, :]
    c[:, C_CM:C_CM + P] = np.where(i[None, :] <= i[:, None], 0, NEG)
    far = (P + i[:, None]) - np.arange(2 * P)[None, :]
    taps = sum(((far >= 0) & (far <= w) & (far % d == 0)).astype(np.float32) for w, d in DIL_CONFIGS)
    c[:, C_DA:C_DA + 2 * P] = np.where(taps > 0, 0, NEG)
    c[:, C_DM:C_DM + 2 * P] = taps
    half = DIL_HD // 2
    powers = np.float32(-np.log(10000.0)) * np.arange(half, dtype=np.float32) * np.float32(2.0 / DIL_HD)
    c[:, C_FR:] = np.exp(powers.astype(np.float64))
    m = np.zeros((P, 1 + len(LEVELS), P), np.int32)
    m[:, 0] = i[:, None] == i[None, :]
    for n, b in enumerate(LEVELS):
        key, query = i[:, None], i[None, :]
        m[:, 1 + n] = (key // (2 * b) == query // (2 * b)) & (key % (2 * b) < b) & (query % (2 * b) >= b)
    return c, m.reshape(P, -1)


PE_AT = {"gla qk": 10, "gla lr": 19, "gla z": 21, "gla G": 23}
for _n in range(8):
    PE_AT[f"gla level {_n}"] = 26 + 2 * _n
PE_AT |= {"gla diag": 42, "ssd xT 0": 43, "ssd xT 1": 44, "gla out": 45, "ssd cum": 50, "ssd CB": 56, "ssd bcast 0": 58,
          "ssd xs": 62, "mla cT": 64, "ssd bcast 1": 66, "mla q 0": 67, "mla q 1": 68, "ssd Y 0": 70, "mla kv 0": 71,
          "mla kv 1": 73, "ssd Y 1": 76, "mla qT": 85, "mla kT": 86, "mla rT": 87, "mla S 0": 89, "mla PT 0": 92,
          "mla S 1": 93, "mla O 0": 94, "dil qT": 95, "mla PT 1": 96, "dil kT": 97, "mla O 1": 98, "dil S 0": 99,
          "dil PT 0": 102, "dil S 1": 103, "dil O 0": 104, "dil PT 1": 106, "yT 0": 107, "dil O 1": 108, "yT 1": 109,
          "yT 2": 110, "yT 3": 114}
LAST_READER = {"gla qk": ("act", "gla k"), "gla lr": ("act", "gla lr"), "gla z": ("dve", "gla la"), "gla G": ("act", "gla G"),
               "gla level 0": ("act", "gla cross"), "gla diag": ("dve", "gla diag"), "gla out": ("dve", "gla o"),
               "ssd xT 0": ("act", "ssd xT 0"), "ssd xT 1": ("act", "ssd xT 1"), "ssd xs": ("dve", "ssd xdt"),
               "ssd cum": ("dve", "ssd row lo"), "ssd CB": ("dve", "ssd CB"), "ssd bcast 0": ("dve", "ssd E 0"),
               "ssd bcast 1": ("dve", "ssd E 1"), "ssd Y 0": ("dve", "ssd y 0"), "ssd Y 1": ("dve", "ssd y 1"),
               "mla cT": ("act", "mla cT"), "mla qT": ("act", "mla qT"), "mla kT": ("act", "mla kT"), "mla rT": ("act", "mla rT"),
               "dil qT": ("act", "dil qT"), "dil kT": ("act", "dil kT")}
LAST_READER |= {f"gla level {n}": ("dve", f"gla merge {n}") for n in range(1, 8)}
LAST_READER |= {f"mla {w} {t}": ("act", f"mla {w} {t}") for w in ("q", "kv") for t in range(2)}
for _m in ("mla", "dil"):
    for _i in range(2):
        LAST_READER |= {f"{_m} S {_i}": ("dve", f"{_m} max {_i}"), f"{_m} PT {_i}": ("act", f"{_m} PT {_i}"),
                        f"{_m} O {_i}": ("dve", f"{_m} O {_i}")}
LAST_READER |= {f"yT {_j}": ("dve", f"yT {_j}") for _j in range(4)}
JOBS = list(PE_AT)
X_NEXT = {UNITS - 6: 0, UNITS - 4: 1}
EVAC_AT = {(b + 1) * UPB + 2: b for b in range(N_INB)}

ORDER = {
    "pe":
        "gla qk, gla lr, gla z, gla G, gla level 0, gla level 1, gla level 2, gla level 3, gla level 4, gla level 5, "
        "gla level 6, gla level 7, gla diag, ssd xT 0, ssd xT 1, gla out, ssd cum, ssd CB, ssd bcast 0, ssd xs, "
        "mla cT, ssd bcast 1, mla q 0, mla q 1, ssd Y 0, mla kv 0, mla kv 1, ssd Y 1, mla qT, mla kT, mla rT, "
        "mla S 0, mla PT 0, mla S 1, mla O 0, dil qT, mla PT 1, dil kT, mla O 1, dil S 0, dil PT 0, dil S 1, dil O 0, "
        "dil PT 1, yT 0, dil O 1, yT 1, yT 2, yT 3",
    "act":
        "x rs sum, evac 0, gla q, gla k, evac 1, gla lr, gla abs, gla exp, gla ln, evac 2, gla G, gla E 0, gla E 1, "
        "gla E 2, gla cross, gla E 3, gla E 4, evac 3, gla E 5, gla E 6, gla E 7, evac 4, ssd xT 0, ssd abs, ssd exp, "
        "ssd eA, ssd ln, ssd xT 1, conv 3 1, gla rs sum, conv 3 0, evac 5, ssd row hi, ssd gcol, ssd silu 1, sincos, "
        "mla crs sum, evac 6, ssd silu 0, ssd exp 0, evac 7, mla cT, mla q 0, ssd exp 1, mla q 1, mla rs 0 sum, "
        "evac 8, mla kv 0, mla kv 1, mla rs 1 sum, dil rs 0 sum, evac 9, dil rs 1 sum, mla qT, mla kT, evac 10, "
        "mla rT, mla P 0, ssd rs sum, mla PT 0, mla P 1, evac 11, dil qT, mla PT 1, dil kT, dil P 0, dil PT 0, "
        "evac 12, dil P 1, dil PT 1, yT 0, yT 1, yT 2, evac 13, yT 3",
    "dve":
        "pad, conv par, gla la, gla zero 0, gla zero 1, gla D 0, gla D 1, gla W 0, gla D 2, gla W 1, gla D 3, "
        "gla W 2, gla merge 1, gla D 4, gla W 3, gla merge 2, gla D 5, gla W 4, gla merge 3, gla D 6, gla W 5, "
        "gla merge 4, gla D 7, gla W 6, gla merge 5, gla W 7, gla merge 6, gla merge 7, gla diag, ssd dt0, ssd dt, "
        "ssd la, conv 1 0, conv 1 1, gla o, conv 1 2, conv 1 3, conv 1 4, conv 1 5, ssd row lo, conv 0 0, conv 0 1, conv 0 2, "
        "conv 0 3, conv 0 4, conv 0 5, ssd CB, mla cn, ssd E 0, ssd xD, ssd xdt, ssd M 0, ssd E 1, ssd M 1, ssd y 0, "
        "mla n 0 0, mla n 0 1, ssd y 1, mla n 1 0, mla n 1 1, mla rope products, mla rope, dil n 0 0, dil n 0 1, "
        "dil n 1 0, dil n 1 1, dil rope 0 products, dil rope 0, dil rope 1 products, dil rope 1, mla max 0, "
        "mla nmax 0, gated 1, mla max 1, mla nmax 1, y 1, mla ri 0, mla O 0, y 0, mla ri 1, mla O 1, dil max 0, "
        "dil nmax 0, dil P 0, dil max 1, dil nmax 1, dil P 1, dil ri 0, dil O 0, y 2, yT 0, dil ri 1, dil O 1, yT 1, "
        "yT 2, y 3, yT 3, ln gain",
    "pool":
        "x rs mean, x rs, gla rs mean, gla rs, mla crs mean, mla crs, mla rs 0 mean, mla rs 0, mla rs 1 mean, "
        "mla rs 1, dil rs 0 mean, dil rs 0, dil rs 1 mean, dil rs 1, ssd rs mean, ssd rs",
}
ORDER = {e: names.split(", ") for e, names in ORDER.items()}


def build(nc, x_d, pos_d, ln_g, w_in, w_out, gla_w2, gla_b, gla_ng, conv_w, conv_b, dt_bias, A_log, D_d, ssd_ng,
          q_ng, kv_ng, w_uq, w_ukv, q_hg, k_hg, dq_g, dk_g, consts_d, masks_d, out_d):
    ctx = ExitStack()
    with ctx:
        def sb(name, shape, dt=F32):
            return ctx.enter_context(nc.sbuf_tensor(name, shape, dt))

        def sem(name):
            return ctx.enter_context(nc.semaphore(name))

        x = sb("x", [P, T, D])
        raw = sb("raw", [P, RAW, UK, WB])
        w_hi = sb("w_hi", [P, SPLIT, UK, WB], F32R)
        w_lo = sb("w_lo", [P, SPLIT, UK, WB], F32R)
        a_hi = sb("a_hi", [P, KT, S], F32R)
        a_lo = sb("a_lo", [P, KT, S], F32R)
        u = sb("u", [P, T, N_U])
        o = sb("o", [P, 4, T, WB])
        cst = sb("cst", [P, NC])
        lmask = sb("lmask", [P, 1 + len(LEVELS), P], U8)
        angle = sb("angle", [P, 2 * T * DIL_HD // 2])
        sc = sb("sincos", [P, 2, T, DIL_HD // 2])
        allp = sb("allp", [P, ROWS])
        lng = sb("lng", [P, KT])
        conv_par = sb("conv_par", [P, (SSD_TAPS + 1) * SSD_CT])
        row_hi = sb("row_hi", [SSD_H, S], F32R)
        row_lo = sb("row_lo", [SSD_H, S], F32R)
        pick = sb("pick", [SSD_H, SSD_H], F32R)
        posi = sb("posi", [P, T], I32)
        posf = sb("posf", [P, T])
        PARAM_WIDTHS = {"gla_ng": 128, "ssd_ng": 512, "q_ng": 384, "kv_ng": 128, "q_hg": 192, "k_hg": 192, "dq_g": 128, "dk_g": 128,
              "dtb": 8, "alog": 8, "D": 8}
        param, at = {}, 0
        param_rows = sb("param_rows", [P, sum(PARAM_WIDTHS.values())])
        for k, n in PARAM_WIDTHS.items():
            param[k] = param_rows[:, at:at + n]
            at += n
        wuq = sb("wuq", [P, MLA_QL // P, MLA_H * MLA_QK])
        wukv = sb("wukv", [P, MLA_H * (MLA_NOPE + MLA_V)])
        w2 = sb("w2", [GLA_R + 1, 256])
        powers = sb("powers", [P, 16])
        eps, minus_half = powers[:, 0:8], powers[:, 8:16]
        st = sb("st", [P, 153])
        sth = sb("sth", [P, 64])
        ar = sb("arena", [P, 7704])

        def tap_weight(j, f):
            return conv_par[:, SSD_CT * j + f:SSD_CT * j + f + 1]

        def conv_bias(f):
            return conv_par[:, SSD_CT * SSD_TAPS + f:SSD_CT * SSD_TAPS + f + 1]

        ident = cst[:, C_ID:C_ID + P]
        tri = cst[:, C_TRI:C_TRI + P]
        ones = cst[:, C_ONE:C_ONE + P]
        tri_ones = cst[:, C_TRI:C_TRI + 2 * P]
        cmask = cst[:, C_CZ:C_CZ + 2 * P]
        dadd = cst[:, C_DA:C_DA + 2 * P]
        dmul = cst[:, C_DM:C_DM + 2 * P]

        def A(start, size, pat=None, **k):
            v = ar[:, start:start + size]
            return v.rearrange(pat, **k) if pat else v

        def two(v, n):
            return v.rearrange("p (a b) -> p a b", a=n)

        h_full = [two(A(1024 * i, 1024), 4) for i in range(2)]
        prow = A(3584, P)
        alrT = A(7192, S)[0:GLA_R + 1]
        qT = o[:, 2, 0, :].rearrange("p (a s) -> p a s", a=2)
        kT = o[:, 2, 1, :].rearrange("p (a s) -> p a s", a=2)
        acc = o[:, 3].rearrange("p r (t a q) -> p r t a q", t=T, a=2)
        GT = two(A(0, 512), 2)
        Dl = [A(512, 512), A(1024, 512)]
        Wl = [A(1536, 512), A(2048, 512)]
        Ql = [A(6168 + 512 * i, 512, "p (r t a s) -> p r t a s", r=2, t=T, a=2) for i in range(2)]
        cross = A(2560, 512, "p (r a q) -> p r a q", r=2, a=2)
        la = two(A(3072, 512), 2)
        lt = two(A(3584, 512), 2)
        xc = two(A(4096, 8 * (S + 3)), 8)
        xdt = two(A(4096, 1024), 2)
        CBm = two(A(256, 768), 2)
        M = [two(A(a, 1536), 4) for a in (6168, 1536)]

        def conv(f):
            return u[:, f // 4, COL["xbc"] + (f % 4) * S:COL["xbc"] + (f % 4 + 1) * S]
        conv4 = [u[:, t, COL["xbc"]:COL["xbc"] + 4 * S] for t in range(2)]
        bsq = u[:, :, COL["cq"]:COL["cq"] + SSD_DI]
        mqk = u[:, :, 0:8 * MLA_QK].rearrange("p t (h d) -> p t h d", h=8)
        mv = u[:, :, 1536:2048]
        msq = A(6168, 1536, "p (t h d) -> p t h d", t=T, h=4)
        mtmp = [A(i * 512, 512, "p (t h d) -> p t h d", t=T, h=8) for i in range(4)]
        mqT, mkT = two(A(0, 1024), 4), two(A(1024, 1024), 4)
        mrT = A(2048, 1024, "p (a b s) -> p a b s", a=2, b=2)
        mrr = A(2048, 1024, "p (t h d) -> p t h d", t=T, h=8)
        Pb, PT = two(A(4096, 768), 2), two(A(4864, 768), 2)
        cT = two(A(3072, 1024), 4)
        gate = two(A(3072, 1024), 2)
        dqk = u[:, :, COL["dq"]:COL["dq"] + 1024].rearrange("p t (h d) -> p t h d", h=8)
        dv = u[:, :, COL["dv"]:COL["dv"] + 512]
        dsq = A(5632, 1024, "p (t h d) -> p t h d", t=T, h=4)
        dtmp = [A(5632 + i * 512, 512, "p (t h d) -> p t h d", t=T, h=4) for i in range(4)]
        dqT, dkT = two(A(5632, 1024), 4), two(A(6656, 1024), 4)

        def stat(a, n):
            return st[:, a:a + n]
        xss, xrs = stat(0, 2), stat(2, 2)
        gss, grs = stat(4, 8), stat(12, 8)
        dtv, dta, las, gcol, eA, dts = stat(20, 16), stat(36, 16), stat(52, 16), stat(68, 16), stat(84, 8), stat(92, 16)
        bss, brs = stat(108, 4), stat(112, 4)
        css, crs = stat(116, 4), stat(120, 4)
        mx, nm, sm, ri = stat(124, 4), stat(128, 4), (stat(132, 4), stat(140, 4)), stat(136, 4)
        nv = stat(144, 8)
        mss, mrs, dss, drs = (sth[:, 16 * i:16 * i + 16] for i in range(4))

        acc_ps = ctx.enter_context(nc.psum_tensor("gemm", [P, 2, T, WB], F32))
        pair = ctx.enter_context(nc.psum_tensor("pairs", [P, 2, 2, 512], F32))

        ident_in, rows_in, small_in, gate_in, params_in, out_written = (
            sem(k) for k in ("ident_in", "rows_in", "small_in", "gate_in", "params_in", "out_written"))
        x_in = [sem(f"x_in_{c}") for c in range(D // WB)]
        paced, setup_chain = sem("paced"), sem("setup_chain")
        x_updated = sem("x_updated")
        x_turned, x_gained, x_hi, x_lo = sem("x_turned"), sem("x_gained"), sem("x_hi"), sem("x_lo")
        weights_in = [sem(f"weights_in_{i}") for i in range(RAW)]
        hi_done, split_done, unit_used = sem("hi_done"), sem("split_done"), sem("unit_used")
        stage = {e: sem(f"{e}_stages") for e in ORDER}
        setup = {e: sem(f"{e}_setup") for e in ORDER}
        seen = {e: [] for e in ORDER}

        def signal(e, name):
            assert ORDER[e][len(seen[e])] == name, (e, name)
            seen[e].append(name)
            return stage[e], 1

        def reached(e, l):
            return lambda name: (stage[e], l * len(ORDER[e]) + ORDER[e].index(name) + 1)

        block = ctx.enter_context(nc.Block())

        def weights(l, b, k0):
            kind, c0, w = BLOCKS[b]
            m = w_out if kind == "out" else w_in
            return m[l].rearrange("(k p) n -> p k n", p=P)[:, k0:k0 + UK, c0:c0 + w]

        def x_load(engine, c):
            engine.dma_start(x[:, :, c * WB:(c + 1) * WB],
                             x_d.rearrange("o (t p) n -> p (o t) n", p=P)[:, :, c * WB:(c + 1) * WB]).then_inc(x_in[c], 16)

        N_PARAMS = len(PARAM_WIDTHS) + 2

        @block.sync
        def _(sp):
            sp.dma_start(cst[:, 0:P], consts_d[:, 0:P]).then_inc(ident_in, 16)
            for c in (0, 1):
                x_load(sp, c)
            with sp.Fori(0, DEPTH) as l:
                for n in range(UNITS):
                    b, k0 = n // UPB, n % UPB * UK
                    sp.wait_ge(split_done, l * UNITS + n + 1)
                    if k0 == 0 and BLOCKS[b][1] == 0:
                        sp.sem_inc(paced, 1)
                    sp.dma_start(raw[:, n % RAW, :, 0:BLOCKS[b][2]], weights(l, b, k0)).then_inc(weights_in[n % RAW], 16)
            parts = [(c * WB, (c + 1) * WB, 0, T) for c in range(D // WB - 1)] + [(D - WB, D, t, t + 1) for t in range(T)]
            for i, (c0, c1, t0, t1) in enumerate(parts):
                sp.wait_ge(x_updated, 4 * DEPTH + i + 1)
                sp.dma_start(out_d.rearrange("o (t p) n -> p (o t) n", p=P)[:, t0:t1, c0:c1], x[:, t0:t1, c0:c1]).then_inc(out_written, 16)
            sp.wait_ge(out_written, 16 * len(parts))

        @block.gpsimd
        def _(pool):
            pool.dma_start(posi[:, :], pos_d.rearrange("o (t p) -> p (o t)", p=P), allow_slow_non_contiguous=True).then_inc(small_in, 16)
            pool.wait_ge(x_in[3], 16)
            pool.dma_start(cst[:, P:], consts_d[:, P:]).then_inc(small_in, 16)
            pool.dma_start(A(2560, 1024).bitcast(I32), masks_d).then_inc(small_in, 16)
            pool.memset(eps, EPS)
            pool.memset(minus_half, -0.5)
            pool.wait_ge(small_in, 16 * 3)
            pool.tensor_copy(lmask[:, :, :].rearrange("p a b -> p (a b)"), A(2560, 1024).bitcast(I32))
            steps = [0]

            def link(ins):
                steps[0] += 1
                ins.then_inc(setup_chain, 1)
                pool.wait_ge(setup_chain, steps[0])
            two_pi = 2 * np.pi
            c1 = 6.28125
            c2 = float(np.float32(np.round((two_pi - c1) * 2 ** 20) / 2 ** 20))
            c3 = float(two_pi - c1 - c2)
            magic = 1.5 * 2.0 ** 23
            af, kf = angle[:, :], A(2048, 256)
            tf = A(2304, 256)
            link(pool.tensor_copy(posf[:, :], posi[:, :]))
            for a in range(2):
                for t in range(T):
                    link(pool.tensor_scalar(af[:, (2 * a + t) * 64:(2 * a + t + 1) * 64], cst[:, C_FR:C_FR + 64], posf[:, t:t + 1], None, ALU.mult))
            link(pool.tensor_scalar(kf[:, 0:128], af[:, 0:128], 1 / two_pi, 0.0, ALU.mult, ALU.add))
            link(pool.tensor_scalar(kf[:, 128:256], af[:, 128:256], 1 / two_pi, 0.25, ALU.mult, ALU.add))
            link(pool.tensor_scalar(kf, kf, magic, None, ALU.add))
            link(pool.tensor_scalar(kf, kf, magic, None, ALU.subtract))
            for c in (c1, c2, c3):
                link(pool.tensor_scalar(tf, kf, c, None, ALU.mult))
                link(pool.tensor_tensor(af, af, tf, ALU.subtract))
            link(pool.tensor_scalar(af[:, 128:256], af[:, 128:256], float(np.pi / 2), None, ALU.add))
            top = float(np.float32(3.1415925))
            pool.tensor_scalar(af, af, top, -top, ALU.min, ALU.max).then_inc(setup["pool"], 1)
            with pool.Fori(0, DEPTH) as l:
                me, act = reached("pool", l), reached("act", l)
                def rsqrt(name, dst, mean):
                    n = mean.shape[-1]
                    pool.wait_ge(*act(name + " sum"))
                    pool.tensor_tensor(nv[:, 0:n], mean, eps[:, 0:n], ALU.add).then_inc(*signal("pool", name + " mean"))
                    pool.wait_ge(*me(name + " mean"))
                    pool.tensor_tensor(dst, nv[:, 0:n], minus_half[:, 0:n], ALU.pow).then_inc(*signal("pool", name))
                    pool.wait_ge(*me(name))

                pool.dma_start(w2[0:GLA_R, :], gla_w2[l]).then_inc(gate_in, 16)
                pool.dma_start(w2[GLA_R:GLA_R + 1, :], gla_b[l].unsqueeze(0)).then_inc(gate_in, 16)
                rsqrt("x rs", xrs, xss)
                for k, src in (("gla_ng", gla_ng), ("ssd_ng", ssd_ng), ("q_ng", q_ng), ("kv_ng", kv_ng), ("q_hg", q_hg),
                               ("k_hg", k_hg), ("dq_g", dq_g), ("dk_g", dk_g), ("dtb", dt_bias), ("alog", A_log), ("D", D_d)):
                    pool.dma_start(param[k], src[l].partition_broadcast(P)).then_inc(params_in, 16)
                pool.dma_start(wuq[:, :, :], w_uq[l].rearrange("(k p) n -> p k n", p=P)).then_inc(params_in, 16)
                pool.dma_start(wukv[:, :], w_ukv[l]).then_inc(params_in, 16)
                rsqrt("gla rs", grs, gss)
                rsqrt("mla crs", crs, css)
                rsqrt("mla rs 0", mrs[:, 0:8], mss[:, 0:8])
                rsqrt("mla rs 1", mrs[:, 8:16], mss[:, 8:16])
                rsqrt("dil rs 0", drs[:, 0:8], dss[:, 0:8])
                rsqrt("dil rs 1", drs[:, 8:16], dss[:, 8:16])
                rsqrt("ssd rs", brs, bss)
                pool.wait_ge(*reached("dve", l)("yT 3"))

        @block.tensor
        def _(pe):
            pe.sem_inc(unit_used, SPLIT)
            pe.wait_ge(ident_in, 16)

            def xT(j, l):
                if l is None:
                    l = 0
                    pe.wait_ge(x_in[j], 16)
                else:
                    pe.wait_ge(x_updated, 4 * l + j + 1)
                if j >= 2:
                    pe.wait_ge(x_lo, 4 * l + j - 1)
                ps = pair[:, j % 2]
                for kk in range(4):
                    for t in range(T):
                        f = (4 * j + kk) * P
                        last = pe.transpose(ps[:, kk // 2, (kk % 2) * S + t * P:(kk % 2) * S + (t + 1) * P], x[:, t, f:f + P], ident)
                last.then_inc(x_turned, 1)

            for j in range(2):
                xT(j, None)
                if j == 0:
                    pe.wait_ge(rows_in, 16 * 3)
                    pe.transpose(acc_ps[:, 0, 0, 0:ROWS], prow[0:ROWS, :], ident[0:ROWS, 0:ROWS]).then_inc(setup["pe"], 1)
            with pe.Fori(0, DEPTH) as l:
                me, act, dve = reached("pe", l), reached("act", l), reached("dve", l)

                def unit(n):
                    b, k0 = n // UPB, n % UPB * UK
                    w = BLOCKS[b][2]
                    if k0 == 0 and b >= 2:
                        if b - 2 in OUT_BLOCK:
                            pe.wait_ge(x_updated, 4 * (l + 1) + OUT_BLOCK[b - 2] + 1)
                        else:
                            pe.wait_ge(*act(f"evac {b - 2}"))
                    if n == UPB:
                        pe.wait_ge(x_updated, 4 * (l + 1))
                    pe.wait_ge(split_done, l * UNITS + n + 1 + RAW)
                    if n < UPB and n % 2 == 0:
                        pe.wait_ge(x_lo, 4 * l + n // 2 + 1)
                    if U_OUT <= n < U_OUT + UPB and n % 2 == 0:
                        pe.wait_ge(*dve(f"yT {(n - U_OUT) // 2}"))
                    for j in range(UK):
                        k = k0 + j
                        for t in range(T):
                            acc_t = acc_ps[:, b % 2, t, 0:w]
                            tok = slice(t * P, (t + 1) * P)
                            hi, lo = w_hi[:, n % SPLIT, j, 0:w], w_lo[:, n % SPLIT, j, 0:w]
                            pe.matmul(acc_t, a_hi[:, k, tok], hi, start=k == 0, stop=False)
                            pe.matmul(acc_t, a_hi[:, k, tok], lo, start=False, stop=False)
                            last = pe.matmul(acc_t, a_lo[:, k, tok], hi, start=False, stop=k == KT - 1)
                    last.then_inc(unit_used, 1)

                jobs, now = [0], [0]

                def bank():
                    jobs[0] += 1
                    n = jobs[0]
                    assert PE_AT[JOBS[n - 1]] == now[0]
                    if n >= 3:
                        e, done = LAST_READER[JOBS[n - 3]]
                        pe.wait_ge(*{"act": act, "dve": dve}[e](done))
                    else:
                        pe.wait_ge(x_lo, 4 * l + 2 + n)
                    return pair[:, n % 2]

                def yT(j):
                    pe.wait_ge(*dve(f"y {j}"))
                    ps = bank()
                    for kk in range(4):
                        for t in range(T):
                            f = kk * P
                            last = pe.transpose(ps[:, kk // 2, (kk % 2) * S + t * P:(kk % 2) * S + (t + 1) * P], o[:, j, t, f:f + P], ident)
                    last.then_inc(*signal("pe", f"yT {j}"))

                def gla_qk():
                    pe.wait_ge(*act("evac 0"))
                    ps = bank()
                    for a in range(2):
                        for p in range(2):
                            for t in range(T):
                                c = a * 256 + p * P
                                last = pe.transpose(ps[:, a, p * S + t * P:p * S + (t + 1) * P], u[:, t, c:c + P], ident)
                    last.then_inc(*signal("pe", "gla qk"))

                def gla_lr():
                    pe.wait_ge(*act("evac 1"))
                    ps = bank()
                    for t in range(T):
                        last = pe.transpose(ps[0:GLA_R, 0, t * P:(t + 1) * P], u[:, t, COL["alr"]:COL["alr"] + GLA_R], ident)
                    last.then_inc(*signal("pe", "gla lr"))

                def gla_z():
                    pe.wait_ge(*act("gla lr"))
                    pe.wait_ge(gate_in, (l + 1) * 16 * 2)
                    ps = bank()
                    for t in range(T):
                        last = pe.matmul(ps[:, 0, t * 256:(t + 1) * 256], alrT[:, t * P:(t + 1) * P], w2[:, :], start=True, stop=True)
                    last.then_inc(*signal("pe", "gla z"))

                def gla_G():
                    pe.wait_ge(*dve("gla la"))
                    ps = bank()
                    for p in range(2):
                        pe.matmul(ps[:, 0, p * S:(p + 1) * S], la[:, 0, p * P:(p + 1) * P], tri_ones, start=True, stop=False)
                        last = pe.matmul(ps[:, 0, p * S + P:(p + 1) * S], la[:, 1, p * P:(p + 1) * P], tri, start=False, stop=True)
                    last.then_inc(*signal("pe", "gla G"))

                def gla_level(n):
                    pe.wait_ge(*dve(f"gla W {n}"))
                    ps = bank()
                    W = two(Wl[n % 2], 2)
                    for p in range(2):
                        if n == 0:
                            for r in range(2):
                                rows = slice(64 * r, 64 * r + 64)
                                last = pe.matmul(ps[:, r, p * P:(p + 1) * P], W[rows, p, 0:P], W[rows, p, P:S], start=True, stop=True)
                        else:
                            for t in range(T):
                                to = ps[:, 0, :].rearrange("p (r t a s) -> p r t a s", r=2, t=T, a=2)[:, :, t, p, :]
                                last = pe.matmul(to, W[:, p, t * P:(t + 1) * P], Ql[n % 2][:, :, t, p, :], start=True, stop=True)
                    last.then_inc(*signal("pe", f"gla level {n}"))

                def gla_diag():
                    ps = bank()
                    for r in range(2):
                        for p in range(2):
                            for t in range(T):
                                rows, tok = slice(64 * r, 64 * r + 64), slice(t * P, (t + 1) * P)
                                c = (t * 2 + p) * P
                                last = pe.matmul(ps[:, r, c:c + P], kT[rows, p, tok], qT[rows, p, tok], start=True, stop=True)
                    last.then_inc(*signal("pe", "gla diag"))

                def gla_out():
                    pe.wait_ge(*dve("gla diag"))
                    pe.wait_ge(*act("gla cross"))
                    ps = bank()
                    for h in range(GLA_H):
                        r, p = h % 2, h // 2
                        c = slice(h * GLA_DV, (h + 1) * GLA_DV)
                        v = slice(COL["av"] + h * GLA_DV, COL["av"] + (h + 1) * GLA_DV)
                        pe.matmul(ps[:, 0, c], acc[:, r, 0, p], u[:, 0, v], start=True, stop=True)
                        pe.matmul(ps[:, 1, c], cross[:, r, p], u[:, 0, v], start=True, stop=False)
                        last = pe.matmul(ps[:, 1, c], acc[:, r, 1, p], u[:, 1, v], start=False, stop=True)
                    last.then_inc(*signal("pe", "gla out"))

                def ssd_xT(i):
                    pe.wait_ge(*act("evac 4"))
                    ps = bank()
                    for kk in range(4):
                        for t in range(T):
                            c = COL["xbc"] + (4 * i + kk) * P
                            last = pe.transpose(ps[:, kk // 2, (kk % 2) * S + t * P:(kk % 2) * S + (t + 1) * P], u[:, t, c:c + P], ident)
                    last.then_inc(*signal("pe", f"ssd xT {i}"))

                def ssd_xs():
                    pe.wait_ge(*act("ssd silu 0"))
                    ps = bank()
                    for f in range(4):
                        for t in range(T):
                            last = pe.transpose(ps[:, t, f * P:(f + 1) * P], conv(f)[:, t * P:(t + 1) * P], ident)
                    last.then_inc(*signal("pe", "ssd xs"))

                def ssd_cum():
                    pe.wait_ge(*dve("ssd la"))
                    ps = bank()
                    l8 = [las[:, t * SSD_H:(t + 1) * SSD_H] for t in range(T)]
                    pe.matmul(ps[0:SSD_H, 0, 0:S], l8[0], tri_ones, start=True, stop=False)
                    pe.matmul(ps[0:SSD_H, 0, P:S], l8[1], tri, start=False, stop=True)
                    pe.matmul(ps[:, 1, 0:8], tri, l8[0], start=True, stop=True)
                    pe.matmul(ps[:, 1, 8:16], ones, l8[0], start=True, stop=False)
                    pe.matmul(ps[:, 1, 8:16], tri, l8[1], start=False, stop=True).then_inc(*signal("pe", "ssd cum"))

                def ssd_CB():
                    pe.wait_ge(*act("ssd silu 1"))
                    ps = bank()
                    for g in range(SSD_G):
                        pe.matmul(ps[:, g, 0:S], conv(4 + g)[:, 0:P], conv(6 + g), start=True, stop=True)
                        last = pe.matmul(ps[:, g, S:S + P], conv(4 + g)[:, P:S], conv(6 + g)[:, P:S], start=True, stop=True)
                    last.then_inc(*signal("pe", "ssd CB"))

                def ssd_bcast(g):
                    pe.wait_ge(*dve("ssd row lo"))
                    ps = bank()
                    for h in range(4):
                        to = ps[:, h // 2, (h % 2) * S:(h % 2 + 1) * S]
                        one = pick[:, 4 * g + h:4 * g + h + 1].to_broadcast([SSD_H, P])
                        pe.matmul(to, one, row_hi[:, :], start=True, stop=False)
                        last = pe.matmul(to, one, row_lo[:, :], start=False, stop=True)
                    last.then_inc(*signal("pe", f"ssd bcast {g}"))

                def ssd_Y(g):
                    pe.wait_ge(*dve(f"ssd M {g}"))
                    pe.wait_ge(*dve("ssd xdt"))
                    ps = bank()
                    for h in range(4):
                        hh = slice((4 * g + h) * SSD_HD, (4 * g + h + 1) * SSD_HD)
                        c = slice(h * SSD_HD, (h + 1) * SSD_HD)
                        pe.matmul(ps[:, 0, c], M[g][:, h, 0:P], xdt[:, 0, hh], start=True, stop=True)
                        pe.matmul(ps[:, 1, c], M[g][:, h, P:S], xdt[:, 0, hh], start=True, stop=False)
                        last = pe.matmul(ps[:, 1, c], M[g][:, h, S:S + P], xdt[:, 1, hh], start=False, stop=True)
                    last.then_inc(*signal("pe", f"ssd Y {g}"))

                def mla_cT():
                    pe.wait_ge(*dve("mla cn"))
                    ps = bank()
                    for kk in range(4):
                        for t in range(T):
                            c = COL["cq"] + kk * P
                            last = pe.transpose(ps[:, kk // 2, (kk % 2) * S + t * P:(kk % 2) * S + (t + 1) * P], u[:, t, c:c + P], ident)
                    last.then_inc(*signal("pe", "mla cT"))

                def mla_q(t):
                    pe.wait_ge(*act("mla cT"))
                    pe.wait_ge(params_in, (l + 1) * 16 * N_PARAMS)
                    ps = bank()
                    for half, (c, w) in enumerate(((0, 512), (512, 256))):
                        for k in range(3):
                            last = pe.matmul(ps[:, half, 0:w], cT[:, k, t * P:(t + 1) * P], wuq[:, k, c:c + w], start=k == 0, stop=k == 2)
                    last.then_inc(*signal("pe", f"mla q {t}"))

                def mla_kv(t):
                    ps = bank()
                    for half in range(2):
                        last = pe.matmul(ps[:, half, :], cT[:, 3, t * P:(t + 1) * P], wukv[:, half * 512:half * 512 + 512], start=True, stop=True)
                    last.then_inc(*signal("pe", f"mla kv {t}"))

                def heads_T(name, src):
                    ps = bank()
                    for h in range(4):
                        for t in range(T):
                            last = pe.transpose(ps[:, h // 2, (h % 2) * S + t * P:(h % 2) * S + (t + 1) * P], src(t, h), ident)
                    last.then_inc(*signal("pe", name))

                def scores(m, i, kq, rope):
                    pe.wait_ge(*act("mla rT" if rope else "dil kT"))
                    ps = bank()
                    for r in range(2):
                        h = 2 * i + r
                        for c0, c1, qs in ((0, P, slice(0, P)), (P, P + S, slice(P, S))):
                            ks = slice(0, c1 - c0)
                            q, k = kq
                            last = pe.matmul(ps[:, r, c0:c1], q[:, h, qs], k[:, h, ks], start=True, stop=not rope)
                            if rope:
                                rows = slice(64 * (h % 2), 64 * (h % 2) + 64)
                                last = pe.matmul(ps[:, r, c0:c1], mrT[rows, 0, h // 2, qs], mrT[rows, 1, h // 2, ks], start=False, stop=True)
                    last.then_inc(*signal("pe", f"{m} S {i}"))

                def probs_T(m, i):
                    pe.wait_ge(*(act if m == "mla" else dve)(f"{m} P {i}"))
                    ps = bank()
                    for r in range(2):
                        for c in range(3):
                            last = pe.transpose(ps[:, r, c * P:(c + 1) * P], Pb[:, r, c * P:(c + 1) * P], ident)
                    last.then_inc(*signal("pe", f"{m} PT {i}"))

                def values(m, i, v):
                    pe.wait_ge(*act(f"{m} PT {i}"))
                    ps = bank()
                    for r in range(2):
                        h, c = 2 * i + r, slice(r * P, (r + 1) * P)
                        hv = slice(h * P, (h + 1) * P)
                        pe.matmul(ps[:, 0, c], PT[:, r, 0:P], v[:, 0, hv], start=True, stop=True)
                        pe.matmul(ps[:, 1, c], PT[:, r, P:2 * P], v[:, 0, hv], start=True, stop=False)
                        last = pe.matmul(ps[:, 1, c], PT[:, r, 2 * P:3 * P], v[:, 1, hv], start=False, stop=True)
                    last.then_inc(*signal("pe", f"{m} O {i}"))

                def mla_qT():
                    pe.wait_ge(*dve("mla rope"))
                    heads_T("mla qT", lambda t, h: mqk[:, t, h, 0:P])

                def mla_kT():
                    heads_T("mla kT", lambda t, h: mqk[:, t, 4 + h, 0:P])

                def mla_rT():
                    rr = mrr.rearrange("p t (a b) d -> p t a (b d)", b=2)
                    heads_T("mla rT", lambda t, h: rr[:, t, h])

                run = {"gla qk": gla_qk, "gla lr": gla_lr, "gla z": gla_z, "gla G": gla_G, "gla diag": gla_diag,
                       "gla out": gla_out, "ssd xs": ssd_xs, "ssd cum": ssd_cum, "ssd CB": ssd_CB, "mla cT": mla_cT,
                       "mla qT": mla_qT, "mla kT": mla_kT, "mla rT": mla_rT}

                def stages(n):
                    for name in PE_AT:
                        if PE_AT[name] != n:
                            continue
                        i = int(name[-1]) if name[-1].isdigit() else None
                        if name.startswith("yT"):
                            yT(i)
                        elif name in run:
                            run[name]()
                        elif name.startswith("gla level"):
                            gla_level(i)
                        elif name.startswith("ssd xT"):
                            ssd_xT(i)
                        elif name.startswith("ssd bcast"):
                            ssd_bcast(i)
                        elif name.startswith("ssd Y"):
                            ssd_Y(i)
                        elif name.startswith("mla q "):
                            mla_q(i)
                        elif name.startswith("mla kv"):
                            mla_kv(i)
                        elif name == "dil qT":
                            pe.wait_ge(*dve("dil rope 1"))
                            heads_T(name, lambda t, h: dqk[:, t, h])
                        elif name == "dil kT":
                            heads_T(name, lambda t, h: dqk[:, t, 4 + h])
                        elif name.startswith("mla S"):
                            scores("mla", i, (mqT, mkT), True)
                        elif name.startswith("dil S"):
                            scores("dil", i, (dqT, dkT), False)
                        elif name.startswith("mla PT"):
                            probs_T("mla", i)
                        elif name.startswith("dil PT"):
                            probs_T("dil", i)
                        elif name.startswith("mla O"):
                            values("mla", i, mv)
                        elif name.startswith("dil O"):
                            values("dil", i, dv)

                for n in range(UNITS):
                    unit(n)
                    if n in (0, 2):
                        xT(2 + n // 2, l)
                    now[0] = n
                    stages(n)
                    if n in X_NEXT:
                        xT(X_NEXT[n], l + 1)

        SC = {"mla": MLA_QK ** -0.5, "dil": DIL_HD ** -0.5}

        def pair_of(name):
            return pair[:, (JOBS.index(name) + 1) % 2]

        def slot(name, lag=3):
            return PE_AT[name] + lag

        @block.scalar
        def _(act_):
            A_ = act_.activation
            for src, row, n in ((ln_g.rearrange("l (k p) -> (l k) p", p=P), 0, CONV_W),
                                (conv_w.rearrange("l j (c p) -> (l j c) p", p=P), CONV_W, CONV_B - CONV_W),
                                (conv_b.rearrange("l (c p) -> (l c) p", p=P), CONV_B, ROWS - CONV_B)):
                act_.dma_start(prow[row:row + n, :], src).then_inc(rows_in, 16)
            act_.wait_ge(x_in[0], 16)
            for c in (2, 3):
                x_load(act_, c)

            def xT_hi(j, l, units):
                act_.wait_ge(x_gained, 4 * l + j + 1)
                act_.wait_ge(unit_used, units + SPLIT)
                A_(a_hi[:, 4 * j:4 * j + 4, :], h_full[j % 2], ACT.Copy).then_inc(x_hi, 1)

            xT_hi(0, 0, 0)
            A_(pick[:, :], ident[0:SSD_H, 0:SSD_H], ACT.Copy).then_inc(setup["act"], 1)
            with act_.Fori(0, DEPTH) as l:
                pe, me, dve, pool = reached("pe", l), reached("act", l), reached("dve", l), reached("pool", l)

                def hi(n):
                    w = BLOCKS[n // UPB][2]
                    act_.wait_ge(weights_in[n % RAW], (l * (UNITS // RAW) + n // RAW + 1) * 16)
                    act_.wait_ge(unit_used, l * UNITS + n + 1)
                    A_(w_hi[:, n % SPLIT, :, 0:w], raw[:, n % RAW, :, 0:w], ACT.Copy).then_inc(hi_done, 1)

                def x_stats(t):
                    act_.wait_ge(x_updated, 4 * (l + 1))
                    square = A_(u[:, t, 0:D], x[:, t, :], ACT.Square, scale=D ** -0.5, accum_out=xss[:, t:t + 1])
                    if t == T - 1:
                        square.then_inc(*signal("act", "x rs sum"))

                def yT(j):
                    act_.wait_ge(*pe(f"yT {j}"))
                    act_.wait_ge(unit_used, l * UNITS + (N_INB - 1) * UPB + 2 * (j + 1) + SPLIT)
                    A_(a_hi[:, 4 * j:4 * j + 4, :], pair_of(f"yT {j}").rearrange("p b (k s) -> p (b k) s", k=2), ACT.Copy).then_inc(*signal("act", f"yT {j}"))

                def evac(b):
                    kind, c0, w = BLOCKS[b]
                    act_.wait_ge(unit_used, l * UNITS + (b + 1) * UPB + SPLIT)
                    if b == 0:
                        act_.wait_ge(*pool("x rs"))
                        act_.wait_ge(*me("x rs sum"))
                    if kind == "u":
                        for t in range(T):
                            last = A_(u[:, t, c0 - N_GATE:c0 - N_GATE + w], acc_ps[:, b % 2, t, 0:w], ACT.Copy, scale=xrs[:, t:t + 1])
                    else:
                        g = GATE_ORDER.index(GATE_BLOCK[b])
                        act_.wait_ge(*(pe("mla kv 1") if g == 0 else dve(f"gated {GB}" if g == 1 else f"y {GATE_ORDER[g - 1]}")))
                        for t in range(T):
                            last = A_(gate[:, t, :], acc_ps[:, b % 2, t, :], ACT.Silu, scale=xrs[:, t:t + 1])
                    last.then_inc(*signal("act", f"evac {b}"))
                    if kind != "u":
                        act_.preload_act_table_set("natural_log_exp_and_others")

                def gla_qk():
                    act_.wait_ge(*pe("gla qk"))
                    ps = pair_of("gla qk")
                    A_(qT, two(ps[:, 0, :], 2), ACT.Copy, scale=GLA_DK ** -0.5).then_inc(*signal("act", "gla q"))
                    A_(kT, two(ps[:, 1, :], 2), ACT.Copy).then_inc(*signal("act", "gla k"))

                def gla_lr():
                    act_.wait_ge(*pe("gla lr"))
                    act_.wait_ge(*dve("pad"))
                    A_(alrT[0:GLA_R, :], pair_of("gla lr")[0:GLA_R, 0, 0:S], ACT.Copy).then_inc(*signal("act", "gla lr"))

                def gla_z():
                    act_.wait_ge(*pe("gla z"))
                    A_(lt, two(pair_of("gla z")[:, 0, :], 2), ACT.Abs).then_inc(*signal("act", "gla abs"))
                    act_.wait_ge(*me("gla abs"))
                    A_(lt, lt, ACT.Exp, scale=-1.0).then_inc(*signal("act", "gla exp"))
                    act_.wait_ge(*me("gla exp"))
                    A_(lt, lt, ACT.Ln, bias=1.0).then_inc(*signal("act", "gla ln"))

                def gla_G():
                    act_.wait_ge(*pe("gla G"))
                    A_(GT, two(pair_of("gla G")[:, 0, :], 2), ACT.Copy, scale=1.0 / GLA_TAU).then_inc(*signal("act", "gla G"))

                def gla_E(n):
                    B = P >> n
                    v = Dl[n % 2].rearrange("p (a s) -> p a s", s=2 * B)
                    act_.wait_ge(*dve(f"gla D {n}"))
                    A_(v[:, :, 0:B], v[:, :, 0:B], ACT.Exp, scale=-1.0)
                    A_(v[:, :, B:2 * B], v[:, :, B:2 * B], ACT.Exp).then_inc(*signal("act", f"gla E {n}"))

                def gla_cross():
                    act_.wait_ge(*pe("gla level 0"))
                    A_(cross.rearrange("p r a q -> p r (a q)"), pair_of("gla level 0")[:, :, 0:256], ACT.Copy).then_inc(*signal("act", "gla cross"))

                def gla_norm():
                    act_.wait_ge(*pe("gla out"))
                    act_.wait_ge(*dve("gla W 7"))
                    ps = pair_of("gla out")
                    for t in range(T):
                        for h in range(GLA_H):
                            j = t * GLA_H + h
                            last = A_(A(512 + j * P, P), ps[:, t, h * P:(h + 1) * P], ACT.Square, scale=GLA_DV ** -0.5, accum_out=gss[:, j:j + 1])
                    last.then_inc(*signal("act", "gla rs sum"))

                def ssd_xT(i):
                    act_.wait_ge(*pe("ssd xT 1"))
                    act_.wait_ge(*dve("pad"))
                    A_(xc[:, 4 * i:4 * i + 4, 3:3 + S], pair_of(f"ssd xT {i}").rearrange("p b (k s) -> p (b k) s", k=2), ACT.Copy).then_inc(*signal("act", f"ssd xT {i}"))

                def conv_tap3(i):
                    act_.wait_ge(*me(f"ssd xT {i}"))
                    act_.wait_ge(*dve("conv par"))
                    for f in range(4 * i, 4 * i + 4):
                        last = A_(conv(f), xc[:, f, 3:3 + S], ACT.Identity, bias=conv_bias(f), scale=tap_weight(3, f))
                    last.then_inc(*signal("act", f"conv 3 {i}"))

                def sincos():
                    act_.wait_ge(setup["pool"], 1)
                    A_(sc[:, :, :, :].rearrange("p a t d -> p (a t d)"), angle[:, :], ACT.Sin).then_inc(*signal("act", "sincos"))

                def ssd_silu(i):
                    act_.wait_ge(*dve(f"conv {i} 5"))
                    A_(conv4[i], conv4[i], ACT.Silu).then_inc(*signal("act", f"ssd silu {i}"))

                def ssd_dt():
                    act_.wait_ge(*dve("ssd dt0"))
                    A_(dta, dtv, ACT.Abs).then_inc(*signal("act", "ssd abs"))
                    act_.wait_ge(*me("ssd abs"))
                    A_(dta, dta, ACT.Exp, scale=-1.0).then_inc(*signal("act", "ssd exp"))
                    A_(eA, param["alog"], ACT.Exp).then_inc(*signal("act", "ssd eA"))
                    act_.wait_ge(*me("ssd eA"))
                    A_(dta, dta, ACT.Ln, bias=1.0).then_inc(*signal("act", "ssd ln"))

                def ssd_cum():
                    act_.wait_ge(*pe("ssd cum"))
                    ps = pair_of("ssd cum")
                    A_(row_hi[:, :], ps[0:SSD_H, 0, 0:S], ACT.Copy).then_inc(*signal("act", "ssd row hi"))
                    A_(gcol, ps[:, 1, 0:16], ACT.Copy).then_inc(*signal("act", "ssd gcol"))

                def ssd_exp(g):
                    act_.wait_ge(*dve(f"ssd E {g}"))
                    A_(M[g][:, :, :], M[g][:, :, :], ACT.Exp).then_inc(*signal("act", f"ssd exp {g}"))

                def ssd_sq():
                    act_.wait_ge(*dve(f"gated {GB}"))
                    for t in range(T):
                        for g in range(SSD_G):
                            c = slice(g * 256, (g + 1) * 256)
                            last = A_(bsq[:, t, c], o[:, GB, t, c], ACT.Square, scale=256 ** -0.5, accum_out=bss[:, 2 * t + g:2 * t + g + 1])
                    last.then_inc(*signal("act", "ssd rs sum"))

                def mla_c():
                    act_.wait_ge(*me("evac 5"))
                    for t in range(T):
                        A_(A(3072 + t * 512, MLA_QL), u[:, t, COL["cq"]:COL["cq"] + MLA_QL], ACT.Square, scale=MLA_QL ** -0.5, accum_out=css[:, t:t + 1])
                        last = A_(A(3072 + t * 512 + MLA_QL, MLA_KVL), u[:, t, COL["ckv"]:COL["ckv"] + MLA_KVL], ACT.Square, scale=MLA_KVL ** -0.5, accum_out=css[:, 2 + t:3 + t])
                    last.then_inc(*signal("act", "mla crs sum"))

                def mla_cT():
                    act_.wait_ge(*pe("mla cT"))
                    act_.wait_ge(*me("mla crs sum"))
                    A_(cT, pair_of("mla cT").rearrange("p b (k s) -> p (b k) s", k=2), ACT.Copy).then_inc(*signal("act", "mla cT"))

                def mla_q(t):
                    act_.wait_ge(*pe(f"mla q {t}"))
                    A_(u[:, t, 0:768], pair_of(f"mla q {t}").rearrange("p b c -> p (b c)")[:, 0:768], ACT.Copy).then_inc(*signal("act", f"mla q {t}"))

                def mla_kv(t):
                    act_.wait_ge(*pe(f"mla kv {t}"))
                    ps = pair_of(f"mla kv {t}").rearrange("p b (h c) -> p (b h) c", h=2)
                    A_(mqk[:, t, 4:8, 0:P], ps[:, :, 0:P], ACT.Copy)
                    A_(mqk[:, t, 4:8, P:MLA_QK], u[:, t, COL["ckr"]:COL["ckr"] + 64].unsqueeze(1).to_broadcast([P, 4, 64]), ACT.Copy)
                    A_(mv[:, t, :].rearrange("p (h c) -> p h c", h=4), ps[:, :, P:2 * P], ACT.Copy).then_inc(*signal("act", f"mla kv {t}"))

                def head_sums(m, i):
                    if m == "mla":
                        act_.wait_ge(*me("mla kv 1" if i else "mla q 1"))
                        act_.wait_ge(*pe("ssd Y 0"))
                        buf, sq, total = mqk, msq, mss
                    else:
                        act_.wait_ge(*me("dil rs 0 sum" if i else "mla rs 1 sum"))
                        buf, sq, total = dqk, dsq, dss
                    for t in range(T):
                        for h in range(4):
                            j = 8 * i + 4 * t + h
                            last = A_(sq[:, t, h, :], buf[:, t, 4 * i + h, :], ACT.Square, scale=buf.shape[-1] ** -0.5, accum_out=total[:, j:j + 1])
                    last.then_inc(*signal("act", f"{m} rs {i} sum"))

                def heads_T(name, dst):
                    act_.wait_ge(*pe(name))
                    A_(dst, pair_of(name).rearrange("p b (k s) -> p (b k) s", k=2), ACT.Copy).then_inc(*signal("act", name))

                def probs(m, i):
                    act_.wait_ge(*dve(f"{m} nmax {i}"))
                    for r in range(2):
                        for t, (c0, c1) in enumerate(((0, P), (P, P + S))):
                            j = 2 * r + t
                            last = A_(Pb[:, r, c0:c1], Pb[:, r, c0:c1], ACT.Exp, bias=nm[:, j:j + 1], scale=SC[m],
                                      accum_out=sm[i][:, j:j + 1] if m == "mla" else None)
                    last.then_inc(*signal("act", f"{m} P {i}"))

                def probs_T(m, i):
                    act_.wait_ge(*pe(f"{m} PT {i}"))
                    A_(PT[:, :, :], pair_of(f"{m} PT {i}")[:, :, 0:384], ACT.Copy).then_inc(*signal("act", f"{m} PT {i}"))

                for n in range(UNITS):
                    hi(n)
                    if n in (0, 3, 5):
                        xT_hi((n + 2) // 2, l, l * UNITS - (3 if n == 0 else 0))
                    if n in (6, 7):
                        x_stats(n - 6)
                    if n == 13:
                        act_.preload_act_table_set("natural_log_exp_and_others")
                    for j in range(4):
                        if n == slot(f"yT {j}"):
                            yT(j)
                    if n in EVAC_AT:
                        evac(EVAC_AT[n])
                    if n == slot("gla qk"):
                        gla_qk()
                    if n == slot("gla lr"):
                        gla_lr()
                    if n == slot("gla z"):
                        gla_z()
                    if n == slot("gla G"):
                        gla_G()
                        gla_E(0)
                        gla_E(1)
                    for i in range(6):
                        if n == PE_AT[f"gla level {i}"] + 2:
                            gla_E(i + 2)
                    if n == slot("gla level 0"):
                        gla_cross()
                    if n == 46:
                        ssd_xT(0)
                        ssd_dt()
                    if n == 47:
                        ssd_xT(1)
                        conv_tap3(1)
                    if n == slot("gla out"):
                        gla_norm()
                    if n == 49:
                        conv_tap3(0)
                    if n == slot("ssd cum"):
                        ssd_cum()
                    if n == 54:
                        ssd_silu(1)
                    if n == 55:
                        sincos()
                    if n == 56:
                        mla_c()
                    if n == 60:
                        ssd_silu(0)
                        act_.preload_act_table_set("natural_log_exp_and_others")
                    if n == 65:
                        ssd_exp(0)
                    if n == 71:
                        ssd_exp(1)
                    if n == slot("mla cT"):
                        mla_cT()
                    for i in range(2):
                        if n == slot(f"mla q {i}"):
                            mla_q(i)
                        if n == slot(f"mla kv {i}"):
                            mla_kv(i)
                    if n == 73:
                        head_sums("mla", 0)
                    if n == 77:
                        head_sums("mla", 1)
                    if n == 80:
                        head_sums("dil", 0)
                    if n == 82:
                        head_sums("dil", 1)
                    if n == slot("mla qT"):
                        heads_T("mla qT", mqT)
                    if n == slot("mla kT"):
                        heads_T("mla kT", mkT)
                    if n == slot("mla rT"):
                        heads_T("mla rT", mrT.rearrange("p a b s -> p (a b) s"))
                    if n == slot("dil qT"):
                        heads_T("dil qT", dqT)
                    if n == slot("dil kT"):
                        heads_T("dil kT", dkT)
                    for m in ("mla", "dil"):
                        for i in range(2):
                            if n == slot(f"{m} S {i}"):
                                probs(m, i)
                            if n == slot(f"{m} PT {i}"):
                                probs_T(m, i)
                    if n == 94:
                        ssd_sq()
                    if n == UNITS - 3:
                        xT_hi(0, l + 1, l * UNITS + UNITS - UPB + 2)

        @block.vector
        def _(v):
            v.sem_inc(split_done, RAW)
            v.memset(acc_ps[:, 1], 0.0)
            v.wait_ge(setup["pe"], 1)
            v.tensor_copy(allp[:, :], acc_ps[:, 0, 0, 0:ROWS]).then_inc(setup["dve"], 1)
            v.wait_ge(setup["dve"], 1)
            v.tensor_copy(lng[:, :], allp[:, 0:KT]).then_inc(setup["dve"], 1)
            v.wait_ge(setup["dve"], 2)

            def x_gain(j, l):
                v.wait_ge(x_turned, 4 * l + j + 1)
                if j >= 2:
                    v.wait_ge(x_lo, 4 * l + j - 1)
                g = lng[:, 4 * j:4 * j + 4].unsqueeze(2).to_broadcast([P, 4, S])
                v.tensor_tensor(h_full[j % 2], pair[:, j % 2].rearrange("p b (k s) -> p (b k) s", k=2), g, ALU.mult).then_inc(x_gained, 1)

            def xT_lo(j, l):
                v.wait_ge(x_gained, 4 * l + j + 1)
                v.wait_ge(x_hi, 4 * l + j + 1)
                v.tensor_tensor(a_lo[:, 4 * j:4 * j + 4, :], h_full[j % 2], a_hi[:, 4 * j:4 * j + 4, :].bitcast(F32), ALU.subtract).then_inc(x_lo, 1)

            x_gain(0, 0)
            xT_lo(0, 0)
            for c in range(3):
                v.wait_ge(x_in[c], 16)
            v.sem_inc(x_updated, 3)

            def x_update(c, bank, units, tiles=slice(0, T)):
                v.wait_ge(unit_used, units + SPLIT)
                part = x[:, tiles, c * WB:(c + 1) * WB]
                v.tensor_tensor(part, part, acc_ps[:, bank, tiles], ALU.add).then_inc(x_updated, 1)

            with v.Fori(0, DEPTH) as l:
                pe, act, me, pool = reached("pe", l), reached("act", l), reached("dve", l), reached("pool", l)
                TT, TS, STT = v.tensor_tensor, v.tensor_scalar, v.scalar_tensor_tensor
                sig = lambda name: signal("dve", name)
                v.memset(alrT, 1.0)
                v.memset(xc[:, :, 0:3], 0.0).then_inc(*sig("pad"))
                n_w = SSD_TAPS * SSD_CT
                v.tensor_copy(conv_par[:, 0:n_w], allp[:, bass.ds(l * n_w + CONV_W, n_w)])
                v.tensor_copy(conv_par[:, n_w:], allp[:, bass.ds(l * SSD_CT + CONV_B, SSD_CT)]).then_inc(*sig("conv par"))

                def lo(n):
                    w = BLOCKS[n // UPB][2]
                    v.wait_ge(hi_done, l * UNITS + n + 1)
                    TT(w_lo[:, n % SPLIT, :, 0:w], raw[:, n % RAW, :, 0:w], w_hi[:, n % SPLIT, :, 0:w].bitcast(F32), ALU.subtract).then_inc(split_done, 1)

                def yT(j):
                    v.wait_ge(*act(f"yT {j}"))
                    TT(a_lo[:, 4 * j:4 * j + 4, :], pair_of(f"yT {j}").rearrange("p b (k s) -> p (b k) s", k=2), a_hi[:, 4 * j:4 * j + 4, :].bitcast(F32), ALU.subtract).then_inc(*sig(f"yT {j}"))

                def gated(g):
                    b = [k for k in GATE_BLOCK if GATE_BLOCK[k] == g][0]
                    v.wait_ge(*act(f"evac {b}"))
                    v.wait_ge(*me({GA: "gla o", GB: "ssd y 1", GC: "mla O 1", GD: "dil O 1"}[g]))
                    TT(o[:, g], o[:, g], gate, ALU.mult).then_inc(*sig(f"gated {g}" if g == GB else f"y {g}"))

                def gla_la():
                    v.wait_ge(setup["pool"], 1)
                    v.wait_ge(*act("gla ln"))
                    STT(la, two(pair_of("gla z")[:, 0, :], 2), 0.0, lt, ALU.min, ALU.subtract).then_inc(*sig("gla la"))

                def gla_D(n):
                    B = P >> n
                    g = GT.rearrange("p a s -> p (a s)").rearrange("p (n s) -> p n s", s=2 * B)
                    ref = g[:, :, B - 1:B].to_broadcast([P, S // B, 2 * B])
                    if n == 0:
                        v.wait_ge(*act("gla G"))
                    if n >= 2:
                        v.wait_ge(*me(f"gla W {n - 2}"))
                    TT(Dl[n % 2].rearrange("p (n s) -> p n s", s=2 * B), g, ref, ALU.subtract).then_inc(*sig(f"gla D {n}"))

                def gla_W(n):
                    B = P >> n
                    h = lambda t: t.rearrange("p (n s) -> p n s", s=2 * B)
                    W, E = h(Wl[n % 2]), h(Dl[n % 2])
                    k, q = h(kT.rearrange("p a s -> p (a s)")), h(qT.rearrange("p a s -> p (a s)"))
                    v.wait_ge(*act(f"gla E {n}"))
                    if n < 2:
                        v.wait_ge(*me("gla zero 1"))
                    if n >= 2:
                        v.wait_ge(*pe(f"gla level {n - 2}"))
                    last = TT(W[:, :, 0:B], k[:, :, 0:B], E[:, :, 0:B], ALU.mult)
                    if n == 0:
                        last = TT(W[:, :, B:], q[:, :, B:], E[:, :, B:], ALU.mult)
                    else:
                        for r in range(2):
                            rows = slice(64 * r, 64 * r + 64)
                            for p in range(2):
                                blocks = slice(p * (S // (2 * B)), (p + 1) * (S // (2 * B)))
                                to = Ql[n % 2][rows, r, :, p, :]
                                if B < 64:
                                    to = to.rearrange("p t (n s) -> p t n s", s=B)
                                    qq, ee = (m[rows, blocks, B:].rearrange("p (t n) s -> p t n s", t=T) for m in (q, E))
                                else:
                                    qq, ee = (m[rows, blocks, B:] for m in (q, E))
                                last = TT(to, qq, ee, ALU.mult)
                    last.then_inc(*sig(f"gla W {n}"))

                acc8 = acc.rearrange("p r t a q -> p (r t a) q")

                def gla_merge(n):
                    name = f"gla level {n}" if n < 8 else "gla diag"
                    i = n if n < 8 else 0
                    v.wait_ge(*pe(name))
                    v.wait_ge(*me(f"gla merge {n - 1}" if n > 1 else "gla zero 1"))
                    v.memset(st[:, 152:153], 0.0)
                    ps = pair_of(name).rearrange("p r (c q) -> p (r c) q", c=4)
                    mask = lmask[:, i].unsqueeze(1).to_broadcast([P, 8, P])
                    if n < 8:
                        B = P >> n
                        to, mask = (k.rearrange("p c (n s) -> p c n s", s=2 * B)[:, :, :, B:] for k in (acc8, mask))
                        ps = pair_of(name)[:, 0, :].rearrange("p (c n s) -> p c n s", c=8, s=B)
                    else:
                        to = acc8
                    v.copy_predicated(to, mask, ps).then_inc(*sig(f"gla merge {n}" if n < 8 else "gla diag"))

                def gla_norm():
                    v.wait_ge(*pool("gla rs"))
                    ps = pair_of("gla out")
                    for t in range(T):
                        for h in range(GLA_H):
                            c, j = slice(h * P, (h + 1) * P), t * GLA_H + h
                            last = STT(o[:, GA, t, c], ps[:, t, c], grs[:, j:j + 1], param["gla_ng"], ALU.mult, ALU.mult)
                    last.then_inc(*sig("gla o"))

                def ssd_dt0():
                    v.wait_ge(*act("evac 4"))
                    v.wait_ge(params_in, (l + 1) * 16 * N_PARAMS)
                    TT(two(dtv, 2), u[:, :, COL["dt"]:COL["dt"] + 8], param["dtb"].unsqueeze(1).to_broadcast([P, 2, 8]), ALU.add).then_inc(*sig("ssd dt0"))

                def ssd_la():
                    v.wait_ge(*act("ssd ln"))
                    STT(dts, dtv, 0.0, dta, ALU.max, ALU.add).then_inc(*sig("ssd dt"))
                    v.wait_ge(*me("ssd dt"))
                    STT(two(las, 2), two(dts, 2), -1.0, eA.unsqueeze(1).to_broadcast([P, 2, 8]), ALU.mult, ALU.mult).then_inc(*sig("ssd la"))

                def conv_step(i, s):
                    if s == 0:
                        v.wait_ge(*act(f"conv 3 {i}"))
                    if s >= 2:
                        v.wait_ge(*me(f"conv {i} {s - 2}"))
                    j = 2 - s // 2
                    for f in range(4 * i + s % 2 * 2, 4 * i + s % 2 * 2 + 2):
                        last = STT(conv(f), xc[:, f, j:j + S], tap_weight(j, f), conv(f), ALU.mult, ALU.add)
                    last.then_inc(*sig(f"conv {i} {s}"))

                def ssd_xD():
                    v.wait_ge(*pe("ssd xs"))
                    ps = pair_of("ssd xs").rearrange("p t (h c) -> p t h c", h=8)
                    ob = o[:, GB].rearrange("p t (h c) -> p t h c", h=8)
                    TT(ob, ps, param["D"].unsqueeze(1).unsqueeze(3).to_broadcast([P, T, 8, 64]), ALU.mult).then_inc(*sig("ssd xD"))

                def ssd_xdt():
                    v.wait_ge(*me("ssd xD"))
                    ps = pair_of("ssd xs").rearrange("p t (h c) -> p t h c", h=8)
                    TT(xdt.rearrange("p t (h c) -> p (t h) c", h=8), ps.rearrange("p t h c -> p (t h) c"), dts.unsqueeze(2).to_broadcast([P, 16, 64]), ALU.mult).then_inc(*sig("ssd xdt"))

                def ssd_row_lo():
                    v.wait_ge(*act("ssd gcol"))
                    TT(row_lo[:, :], pair_of("ssd cum")[0:SSD_H, 0, 0:S], row_hi[:, :].bitcast(F32), ALU.subtract).then_inc(*sig("ssd row lo"))

                def ssd_CB():
                    v.wait_ge(*pe("ssd CB"))
                    mk = cst[:, C_TRI:C_TRI + 384].unsqueeze(1).to_broadcast([P, 2, 384])
                    TT(CBm, pair_of("ssd CB")[:, :, 0:384], mk, ALU.mult).then_inc(*sig("ssd CB"))

                def ssd_E(g, h):
                    if h == 0:
                        v.wait_ge(*pe(f"ssd bcast {g}"))
                        v.wait_ge(*act("ssd gcol"))
                    ps = pair_of(f"ssd bcast {g}").rearrange("p b (h s) -> p (b h) s", h=2)
                    hh = 4 * g + h
                    TS(M[g][:, h, 0:S], ps[:, h, :], gcol[:, hh:hh + 1], 0.0, ALU.subtract, ALU.min)
                    last = TS(M[g][:, h, S:S + P], ps[:, h, P:S], gcol[:, 8 + hh:9 + hh], 0.0, ALU.subtract, ALU.min)
                    if h == 3:
                        last.then_inc(*sig(f"ssd E {g}"))

                def ssd_M(g):
                    v.wait_ge(*act(f"ssd exp {g}"))
                    v.wait_ge(*me("ssd CB"))
                    TT(M[g][:, :, :], M[g][:, :, :], CBm[:, g, :].unsqueeze(1).to_broadcast([P, 4, 384]), ALU.mult).then_inc(*sig(f"ssd M {g}"))

                def ssd_y(g):
                    v.wait_ge(*pe(f"ssd Y {g}"))
                    v.wait_ge(*me("ssd xD"))
                    ob = o[:, GB, :, g * 256:(g + 1) * 256]
                    TT(ob, ob, pair_of(f"ssd Y {g}")[:, :, 0:256], ALU.add).then_inc(*sig(f"ssd y {g}"))

                def ssd_norm():
                    v.wait_ge(*pool("ssd rs"))
                    for t in range(T):
                        for g in range(SSD_G):
                            c = slice(g * 256, (g + 1) * 256)
                            last = STT(o[:, GB, t, c], o[:, GB, t, c], brs[:, 2 * t + g:2 * t + g + 1], param["ssd_ng"][:, c], ALU.mult, ALU.mult)
                    last.then_inc(*sig(f"y {GB}"))

                def mla_cn(t):
                    v.wait_ge(*pool("mla crs"))
                    a, b = (u[:, t, COL[k]:COL[k] + n] for k, n in (("cq", MLA_QL), ("ckv", MLA_KVL)))
                    STT(a, a, crs[:, t:t + 1], param["q_ng"], ALU.mult, ALU.mult)
                    last = STT(b, b, crs[:, 2 + t:3 + t], param["kv_ng"], ALU.mult, ALU.mult)
                    if t:
                        last.then_inc(*sig("mla cn"))

                def head_norm(m, i, t):
                    v.wait_ge(*pool(f"{m} rs {i}"))
                    buf, rs = (mqk, mrs) if m == "mla" else (dqk, drs)
                    g = param[("q_hg", "k_hg")[i] if m == "mla" else ("dq_g", "dk_g")[i]]
                    for h in range(4):
                        j = 8 * i + 4 * t + h
                        last = STT(buf[:, t, 4 * i + h, :], buf[:, t, 4 * i + h, :], rs[:, j:j + 1], g, ALU.mult, ALU.mult)
                    last.then_inc(*sig(f"{m} n {i} {t}"))

                def rope_products(name, after, x1, x2, tmp, nh, hd, step):
                    v.wait_ge(*act("sincos"))
                    v.wait_ge(*me(after))
                    s, c = (sc[:, a, :, 0:64:step].unsqueeze(2).to_broadcast([P, T, nh, hd]) for a in range(2))
                    TT(tmp[0], x1, c, ALU.mult)
                    TT(tmp[1], x2, s, ALU.mult)
                    TT(tmp[2], x2, c, ALU.mult)
                    TT(tmp[3], x1, s, ALU.mult).then_inc(*sig(name + " products"))

                def rope_sums(name, y1, y2, tmp):
                    v.wait_ge(*me(name + " products"))
                    TT(y1, tmp[0], tmp[1], ALU.subtract)
                    TT(y2, tmp[2], tmp[3], ALU.add).then_inc(*sig(name))

                def smax(m, i):
                    v.wait_ge(*pe(f"{m} S {i}"))
                    if i:
                        v.wait_ge(*pe(f"{m} PT {i - 1}"))
                    ps = pair_of(f"{m} S {i}")
                    mk = cmask if m == "mla" else dadd
                    v.memset(st[:, 152:153], 0.0)
                    for r in range(2):
                        for t, (c0, c1) in enumerate(((0, P), (P, P + S))):
                            j = 2 * r + t
                            last = v.tensor_tensor_reduce(out=Pb[:, r, c0:c1], in0=ps[:, r, c0:c1], in1=mk[:, 2 * P - (c1 - c0):], scale=1.0,
                                                          scalar=-3e38, op0=ALU.add, op1=ALU.max, accum_out=mx[:, j:j + 1])
                    last.then_inc(*sig(f"{m} max {i}"))
                    v.wait_ge(*me(f"{m} max {i}"))
                    TS(nm, mx, -SC[m], None, ALU.mult).then_inc(*sig(f"{m} nmax {i}"))

                def taps(i):
                    v.wait_ge(*act(f"dil P {i}"))
                    for r in range(2):
                        for t, (c0, c1) in enumerate(((0, P), (P, P + S))):
                            j = 2 * r + t
                            last = v.tensor_tensor_reduce(out=Pb[:, r, c0:c1], in0=Pb[:, r, c0:c1], in1=dmul[:, 2 * P - (c1 - c0):], scale=1.0,
                                                          scalar=0.0, op0=ALU.mult, op1=ALU.add, accum_out=sm[i][:, j:j + 1])
                    last.then_inc(*sig(f"dil P {i}"))

                def out_heads(m, i):
                    if m == "dil":
                        v.wait_ge(*me(f"dil P {i}"))
                    else:
                        v.wait_ge(*act(f"mla P {i}"))
                    if (m, i) != ("mla", 0):
                        v.wait_ge(*me(f"{m} O 0" if i else "mla O 1"))
                    v.reciprocal(ri, sm[i]).then_inc(*sig(f"{m} ri {i}"))
                    v.wait_ge(*me(f"{m} ri {i}"))
                    v.wait_ge(*pe(f"{m} O {i}"))
                    ps = pair_of(f"{m} O {i}")
                    g = GC if m == "mla" else GD
                    for t in range(T):
                        for r in range(2):
                            h, j = 2 * i + r, 2 * r + t
                            last = TS(o[:, g, t, h * P:(h + 1) * P], ps[:, t, r * P:(r + 1) * P], ri[:, j:j + 1], None, ALU.mult)
                    last.then_inc(*sig(f"{m} O {i}"))

                for n in range(UNITS):
                    lo(n)
                    if n in (0, 3, 5):
                        x_gain((n + 2) // 2, l)
                        xT_lo((n + 2) // 2, l)
                    for j in range(4):
                        if n == slot(f"yT {j}"):
                            yT(j)
                    if n == 1:
                        v.wait_ge(x_in[3], 16)
                        v.wait_ge(setup["dve"], 2)
                        x_update(3, 1, l * UNITS)
                    if n % UPB == 2 and n // UPB - 1 in OUT_BLOCK:
                        b = n // UPB - 1
                        x_update(OUT_BLOCK[b], b % 2, l * UNITS + (b + 1) * UPB)
                    if n == slot("gla z"):
                        gla_la()
                        v.memset(acc8, 0.0)
                        for i in range(2):
                            v.memset(Wl[i], 0.0)
                            v.memset(Ql[i].rearrange("p r t a s -> p (r t a s)"), 0.0).then_inc(*sig(f"gla zero {i}"))
                    if n == slot("gla G"):
                        gla_D(0)
                        gla_D(1)
                        gla_W(0)
                    for i in range(1, 8):
                        if n == PE_AT[f"gla level {i - 1}"] + 1:
                            if i < 7:
                                gla_D(i + 1)
                            gla_W(i)
                        if n == PE_AT[f"gla level {i}"] + 3:
                            gla_merge(i)
                    if n == slot("gla diag"):
                        gla_merge(8)
                    if n == 45:
                        ssd_dt0()
                    if n == 47:
                        ssd_la()
                    for i in range(2):
                        for s in range(6):
                            if n == (54, 48)[i] + s:
                                conv_step(i, s)
                    if n == slot("gla out", 4):
                        gla_norm()
                    if n == slot("ssd cum"):
                        ssd_row_lo()
                    if n == slot("ssd CB"):
                        ssd_CB()
                    for t in range(T):
                        if n == 60 + t:
                            mla_cn(t)
                    for g in range(2):
                        for h in range(4):
                            if n == (62 + h, 69 + h // 2)[g]:
                                ssd_E(g, h)
                        if n == (68, 73)[g]:
                            ssd_M(g)
                    if n == 66:
                        ssd_xD()
                    if n == 67:
                        ssd_xdt()
                    if n == 73:
                        ssd_y(0)
                    if n == 79:
                        ssd_y(1)
                    for t in range(T):
                        if n == 77 + t:
                            head_norm("mla", 0, t)
                        if n == 81 + t:
                            head_norm("mla", 1, t)
                    if n == 83:
                        rope_products("mla rope", "mla n 1 1", mqk[:, :, :, P:P + 32], mqk[:, :, :, P + 32:P + 64], mtmp, 8, 32, 2)
                    if n == 84:
                        rope_sums("mla rope", mrr[:, :, :, 0:32], mrr[:, :, :, 32:64], mtmp)
                    for i in range(2):
                        b = dqk[:, :, 4 * i:4 * i + 4]
                        if n == 86 + i:
                            for t in range(T):
                                head_norm("dil", i, t)
                        if n == 88 + 2 * i:
                            rope_products(f"dil rope {i}", "dil rope 0" if i else "dil n 1 1", b[:, :, :, 0:64], b[:, :, :, 64:128], dtmp, 4, 64, 1)
                        if n == 89 + 2 * i:
                            rope_sums(f"dil rope {i}", b[:, :, :, 0:64], b[:, :, :, 64:128], dtmp)
                    for m in ("mla", "dil"):
                        for i in range(2):
                            if n == slot(f"{m} S {i}"):
                                smax(m, i)
                                if m == "dil":
                                    taps(i)
                            if n == slot(f"{m} O {i}"):
                                out_heads(m, i)
                    if n == 93:
                        gated(GB)
                    if n == 96:
                        ssd_norm()
                    if n == 99:
                        gated(GA)
                    if n == 107:
                        gated(GC)
                    if n == 115:
                        gated(GD)
                    if n == 128:
                        v.wait_ge(x_lo, 4 * (l + 1))
                        v.tensor_copy(lng[:, :], allp[:, bass.ds(l * KT + KT, KT)]).then_inc(*sig("ln gain"))
                        v.wait_ge(*me("ln gain"))
                    if n == UNITS - 3:
                        x_gain(0, l + 1)
                        xT_lo(0, l + 1)
            for t in range(T):
                x_update(3, 1, DEPTH * UNITS, slice(t, t + 1))


_INS = ["x", "positions", "ln_g", "w_in", "w_out", "gla_gate_w2", "gla_gate_b", "gla_norm_g", "ssd_conv_w", "ssd_conv_b",
        "ssd_dt_bias", "ssd_A_log", "ssd_D", "ssd_norm_g", "mla_q_norm_g", "mla_kv_norm_g", "mla_w_uq", "mla_w_ukv",
        "mla_q_head_g", "mla_k_head_g", "dil_q_g", "dil_k_g"]
_OUTS = [((1, S, D), "float32")]


def kernel(**inputs):
    import concourse.bacc as _bacc
    from concourse.bass_utils import run_bass_kernel_spmd as _run

    consts, masks = tables()
    given = {n: np.ascontiguousarray(inputs[n]) for n in _INS} | {"consts": consts, "masks": masks}
    nc = _bacc.Bacc("TRN2", target_bir_lowering=False, num_devices=1)
    arrays, args = {}, []
    for name, a in given.items():
        arrays[f"in_{name}_dram"] = a
        args.append(nc.dram_tensor(f"in_{name}_dram", a.shape, mybir.dt.from_np(a.dtype), kind="ExternalInput").ap())
    for i, (shape, dtype) in enumerate(_OUTS):
        args.append(nc.dram_tensor(f"out_{i}_dram", shape, mybir.dt.from_np(np.dtype(dtype)), kind="ExternalOutput").ap())
    build(nc, *args)
    r = _run(nc, [arrays], core_ids=[0])
    return r.results[0]["out_0_dram"]
```
